# Optimizing a Trainium2 kernel written in Bass

```python
import jax, jax.numpy as jnp
from jax import lax
import numpy as np

D_MODEL = 1024
BATCH = 1
SEQ = 1024
DEPTH = 1
DEC_BATCH = 8
DEC_SEQ = 4
PAST_LEN = 2048
PAGE_SIZE = 128

RW_HEADS = 8
RW_HEAD_DIM = 64
RW_WIDTH = RW_HEADS * RW_HEAD_DIM
DECAY_LORA = 64
A_LORA = 64
GATE_LORA = 128
RW_PROJ = 3 * RW_WIDTH + DECAY_LORA + A_LORA + GATE_LORA
RW_SPLITS = (RW_WIDTH, 2 * RW_WIDTH, 3 * RW_WIDTH, 3 * RW_WIDTH + DECAY_LORA, 3 * RW_WIDTH + DECAY_LORA + A_LORA)
LNX_EPS = 64e-5
MLA_HEADS = 8
QK_NOPE = 64
QK_ROPE = 32
V_DIM = 64
Q_LORA = 384
KV_LORA = 256
MLA_WIDTH = MLA_HEADS * V_DIM
MLA_PROJ = Q_LORA + KV_LORA + QK_ROPE
MLA_SCALE = (QK_NOPE + QK_ROPE) ** -0.5
ROPE_THETA = 10000.0
Q_BLOCK = 128
IN_PROJ = MLA_PROJ + RW_PROJ
MIX_WIDTH = RW_WIDTH + MLA_WIDTH
N_MEM = 256
MEM_HEADS = 4
MEM_HEAD_DIM = D_MODEL // MEM_HEADS
MEM_SCALE = MEM_HEAD_DIM ** -0.5
D_FF = 2816
CONV_W = 3
NORM_EPS = 1e-6

kernel_name = 'hymba_rwkv7_mla_memory_convffn_step'

def rmsnorm(x, g, eps=NORM_EPS):
    xf = x.astype(jnp.float32)
    y = xf * lax.rsqrt(jnp.mean(xf * xf, axis=-1, keepdims=True) + eps)
    return (y * g.astype(jnp.float32)).astype(x.dtype)

def rope(x, pos):
    half = QK_ROPE // 2
    inv = 1.0 / (ROPE_THETA ** (jnp.arange(half, dtype=jnp.float32) / half))
    ang = pos.astype(jnp.float32)[:, None] * inv[None, :]
    ang = ang.reshape(ang.shape[:1] + (1,) * (x.ndim - 3) + (half,))
    cos, sin = jnp.cos(ang), jnp.sin(ang)
    xf = x.astype(jnp.float32)
    x1, x2 = xf[..., :half], xf[..., half:]
    return jnp.concatenate([x1 * cos - x2 * sin, x1 * sin + x2 * cos], axis=-1).astype(x.dtype)

def rwkv7_group(p, shift_prev, state0, mu, w0, w2, a0, a2, g2, k_k, k_a, r_k, lnx_g, lnx_b):
    B, T, _ = p.shape
    p_prev = jnp.concatenate([shift_prev[:, None, :].astype(p.dtype), p[:, :-1]], axis=1)
    s = p + (p_prev - p) * mu
    r, k, v, wd, ad, gd = jnp.split(s, RW_SPLITS, axis=-1)
    w = -jax.nn.softplus(-(w0 + jnp.tanh(wd) @ w2).astype(jnp.float32)) - 0.5
    decay = jnp.exp(-jnp.exp(w))
    a = jax.nn.sigmoid(a0 + ad @ a2)
    g = jax.nn.sigmoid(gd) @ g2
    heads = lambda t: t.astype(jnp.float32).reshape(B, T, RW_HEADS, RW_HEAD_DIM)
    kk = heads(k * k_k)
    kk = kk / jnp.maximum(jnp.sqrt(jnp.sum(kk * kk, axis=-1, keepdims=True)), 1e-12)
    k = k * (1.0 + (a - 1.0) * k_a)
    r_h, k_h, v_h, a_h, d_h = heads(r), heads(k), heads(v), heads(a), heads(decay)

    def step(S, inp):
        r_t, d_t, k_t, v_t, kk_t, a_t = inp
        sa = -jnp.einsum('bhvk,bhk->bhv', S, kk_t)
        S = (S * d_t[:, :, None, :] + sa[..., None] * (kk_t * a_t)[:, :, None, :]
             + v_t[..., None] * k_t[:, :, None, :])
        return S, jnp.einsum('bhvk,bhk->bhv', S, r_t)

    xs = tuple(jnp.moveaxis(t, 1, 0) for t in (r_h, d_h, k_h, v_h, kk, a_h))
    state, out = lax.scan(step, state0.astype(jnp.float32), xs)
    out = jnp.moveaxis(out, 0, 1)
    mean = jnp.mean(out, axis=-1, keepdims=True)
    var = jnp.mean(jnp.square(out - mean), axis=-1, keepdims=True)
    y = ((out - mean) * lax.rsqrt(var + LNX_EPS)).reshape(B, T, RW_WIDTH)
    y = y * lnx_g.astype(jnp.float32) + lnx_b.astype(jnp.float32)
    bonus = jnp.sum(r_h * k_h * r_k.astype(jnp.float32), axis=-1, keepdims=True) * v_h
    y = (y + bonus.reshape(B, T, RW_WIDTH)) * g.astype(jnp.float32)
    return y.astype(p.dtype), state, p[:, -1]

def mla_full_causal(q_nope, q_rope, lat, k_rope, w_ukv):
    B, T = lat.shape[:2]
    kv = (lat @ w_ukv).reshape(B, T, MLA_HEADS, QK_NOPE + V_DIM)
    k_nope, v = kv[..., :QK_NOPE], kv[..., QK_NOPE:]
    kpos = jnp.arange(T)

    def block(i):
        s0 = i * Q_BLOCK
        qn = lax.dynamic_slice_in_dim(q_nope, s0, Q_BLOCK, axis=1)
        qr = lax.dynamic_slice_in_dim(q_rope, s0, Q_BLOCK, axis=1)
        sc = jnp.einsum('bqhd,bkhd->bhqk', qn, k_nope) + jnp.einsum('bqhr,bkr->bhqk', qr, k_rope)
        sc = sc.astype(jnp.float32) * MLA_SCALE
        qpos = s0 + jnp.arange(Q_BLOCK)
        sc = jnp.where(kpos[None, :] <= qpos[:, None], sc, -jnp.inf)
        pr = jax.nn.softmax(sc, axis=-1).astype(v.dtype)
        return jnp.einsum('bhqk,bkhd->bqhd', pr, v)

    out = lax.map(block, jnp.arange(T // Q_BLOCK))
    return jnp.moveaxis(out, 0, 1).reshape(B, T, MLA_WIDTH)

def mla_paged_step(q_nope, q_rope, lat_new, kr_new, lat_past, kr_past, w_ukv):
    B, T = lat_new.shape[:2]
    P = lat_past.shape[1]
    w = w_ukv.reshape(KV_LORA, MLA_HEADS, QK_NOPE + V_DIM)
    w_uk, w_uv = w[..., :QK_NOPE], w[..., QK_NOPE:]
    q_abs = jnp.einsum('bthd,chd->bthc', q_nope, w_uk)
    sc_past = jnp.einsum('bthc,bsc->bhts', q_abs, lat_past) + jnp.einsum('bthr,bsr->bhts', q_rope, kr_past)
    sc_new = jnp.einsum('bthc,bsc->bhts', q_abs, lat_new) + jnp.einsum('bthr,bsr->bhts', q_rope, kr_new)
    causal = jnp.arange(T)[None, :] <= jnp.arange(T)[:, None]
    sc_new = jnp.where(causal, sc_new.astype(jnp.float32) * MLA_SCALE, -jnp.inf)
    sc = jnp.concatenate([sc_past.astype(jnp.float32) * MLA_SCALE, sc_new], axis=-1)
    pr = jax.nn.softmax(sc, axis=-1).astype(lat_new.dtype)
    o_lat = (jnp.einsum('bhts,bsc->bthc', pr[..., :P], lat_past)
             + jnp.einsum('bhts,bsc->bthc', pr[..., P:], lat_new))
    o = jnp.einsum('bthc,chd->bthd', o_lat, w_uv)
    return o.reshape(B, T, MLA_WIDTH)

def memory_kv(mem, g, w_k, w_v):
    B = mem.shape[0]
    m = rmsnorm(mem, g)
    k = (m @ w_k).reshape(B, -1, MEM_HEADS, MEM_HEAD_DIM)
    v = (m @ w_v).reshape(B, -1, MEM_HEADS, MEM_HEAD_DIM)
    return k, v

def memory_attn(h, mem_k, mem_v, w_q, w_out):
    B, T, _ = h.shape
    q = (h @ w_q).reshape(B, T, MEM_HEADS, MEM_HEAD_DIM)
    sc = jnp.einsum('bthd,bmhd->bhtm', q, mem_k.astype(q.dtype)).astype(jnp.float32) * MEM_SCALE
    pr = jax.nn.softmax(sc, axis=-1).astype(q.dtype)
    o = jnp.einsum('bhtm,bmhd->bthd', pr, mem_v.astype(q.dtype)).reshape(B, T, D_MODEL)
    return o @ w_out

def conv_ffn(h, conv_prev, w_up, conv_w, conv_b, w_down):
    T = h.shape[1]
    u = h @ w_up
    up = jnp.concatenate([conv_prev.astype(u.dtype), u], axis=1)
    c = conv_b + sum(conv_w[j] * up[:, j:j + T] for j in range(CONV_W))
    gate, val = jnp.split(c, 2, axis=-1)
    return (jax.nn.silu(gate) * val) @ w_down, up[:, T:]

def _layer(x, pos, rw_shift, rw_state, conv_prev, mem_k, mem_v, lp, past):
    B, T, _ = x.shape
    h = rmsnorm(x, lp['g_mix'])
    proj = h @ lp['w_in']
    p_mla, p_rw = proj[..., :MLA_PROJ], proj[..., MLA_PROJ:]
    c_q = p_mla[..., :Q_LORA]
    c_kv = p_mla[..., Q_LORA:Q_LORA + KV_LORA]
    k_r = p_mla[..., Q_LORA + KV_LORA:]
    q = (rmsnorm(c_q, lp['q_norm_g']) @ lp['w_uq']).reshape(B, T, MLA_HEADS, QK_NOPE + QK_ROPE)
    q_nope, q_rope = q[..., :QK_NOPE], rope(q[..., QK_NOPE:], pos)
    lat = rmsnorm(c_kv, lp['kv_norm_g'])
    k_rope = rope(k_r, pos)
    if past is None:
        o_mla = mla_full_causal(q_nope, q_rope, lat, k_rope, lp['w_ukv'])
    else:
        o_mla = mla_paged_step(q_nope, q_rope, lat, k_rope, past[0], past[1], lp['w_ukv'])
    o_mla = rmsnorm(o_mla, lp['g_mla_out'])
    o_rw, rw_state_new, rw_shift_new = rwkv7_group(
        p_rw, rw_shift, rw_state, lp['rw_mu'], lp['rw_w0'], lp['rw_w2'], lp['rw_a0'], lp['rw_a2'],
        lp['rw_g2'], lp['rw_k_k'], lp['rw_k_a'], lp['rw_r_k'], lp['rw_lnx_g'], lp['rw_lnx_b'])
    x = x + jnp.concatenate([o_rw, o_mla], axis=-1) @ lp['w_o']
    x = x + memory_attn(rmsnorm(x, lp['g_mem_q']), mem_k, mem_v, lp['w_mq'], lp['w_mo'])
    f, conv_new = conv_ffn(rmsnorm(x, lp['g_ffn']), conv_prev, lp['w_up'], lp['conv_w'], lp['conv_b'], lp['w_down'])
    x = x + f
    return x, (lat, k_rope, rw_state_new, rw_shift_new, conv_new)

def setup_inputs(seed: int = 0) -> dict:
    key = jax.random.key(seed)
    keys = iter(jax.random.split(key, 64))
    nrm = lambda shape, scale: jax.random.normal(next(keys), shape, jnp.float32) * scale
    gain = lambda shape: 1.0 + nrm(shape, 0.05)
    L = DEPTH
    F2 = 2 * D_FF
    n_pages = PAST_LEN // PAGE_SIZE
    n_used = DEC_BATCH * n_pages
    n_phys = n_used + max(1, n_used // 4)
    perm = jax.random.permutation(next(keys), n_phys)
    page_table = perm[:n_used].reshape(DEC_BATCH, n_pages).astype(jnp.int32)
    return {
        'x_prompt': nrm((BATCH, SEQ, D_MODEL), 1.0),
        'x_sample': nrm((DEC_BATCH, DEC_SEQ, D_MODEL), 1.0),
        'cache_mla_latent': nrm((L, n_phys, PAGE_SIZE, KV_LORA), 1.0),
        'cache_mla_krope': nrm((L, n_phys, PAGE_SIZE, QK_ROPE), 1.0),
        'cache_mem_k': nrm((L, DEC_BATCH, N_MEM, MEM_HEADS, MEM_HEAD_DIM), 1.0),
        'cache_mem_v': nrm((L, DEC_BATCH, N_MEM, MEM_HEADS, MEM_HEAD_DIM), 1.0),
        'state_rwkv': nrm((L, DEC_BATCH, RW_HEADS, RW_HEAD_DIM, RW_HEAD_DIM), 0.5),
        'state_rwkv_shift': nrm((L, DEC_BATCH, RW_PROJ), 1.0),
        'state_ffn_conv': nrm((L, DEC_BATCH, CONV_W - 1, F2), 1.0),
        'page_table': page_table,
        'mem_prompt': nrm((BATCH, N_MEM, D_MODEL), 1.0),
        'g_mix': gain((L, D_MODEL)),
        'w_in': nrm((L, D_MODEL, IN_PROJ), D_MODEL ** -0.5),
        'q_norm_g': gain((L, Q_LORA)),
        'kv_norm_g': gain((L, KV_LORA)),
        'w_uq': nrm((L, Q_LORA, MLA_HEADS * (QK_NOPE + QK_ROPE)), Q_LORA ** -0.5),
        'w_ukv': nrm((L, KV_LORA, MLA_HEADS * (QK_NOPE + V_DIM)), KV_LORA ** -0.5),
        'g_mla_out': gain((L, MLA_WIDTH)),
        'rw_mu': jax.random.uniform(next(keys), (L, RW_PROJ), jnp.float32),
        'rw_w0': nrm((L, RW_WIDTH), 0.5),
        'rw_w2': nrm((L, DECAY_LORA, RW_WIDTH), DECAY_LORA ** -0.5),
        'rw_a0': nrm((L, RW_WIDTH), 0.1),
        'rw_a2': nrm((L, A_LORA, RW_WIDTH), A_LORA ** -0.5),
        'rw_g2': nrm((L, GATE_LORA, RW_WIDTH), GATE_LORA ** -0.5),
        'rw_k_k': 0.85 + nrm((L, RW_WIDTH), 0.05),
        'rw_k_a': 1.0 + nrm((L, RW_WIDTH), 0.05),
        'rw_r_k': nrm((L, RW_HEADS, RW_HEAD_DIM), 0.1),
        'rw_lnx_g': gain((L, RW_WIDTH)),
        'rw_lnx_b': nrm((L, RW_WIDTH), 0.01),
        'w_o': nrm((L, MIX_WIDTH, D_MODEL), MIX_WIDTH ** -0.5),
        'g_mem_q': gain((L, D_MODEL)),
        'g_mem_kv': gain((L, D_MODEL)),
        'w_mq': nrm((L, D_MODEL, D_MODEL), D_MODEL ** -0.5),
        'w_mk': nrm((L, D_MODEL, D_MODEL), D_MODEL ** -0.5),
        'w_mv': nrm((L, D_MODEL, D_MODEL), D_MODEL ** -0.5),
        'w_mo': nrm((L, D_MODEL, D_MODEL), D_MODEL ** -0.5),
        'g_ffn': gain((L, D_MODEL)),
        'w_up': nrm((L, D_MODEL, F2), D_MODEL ** -0.5),
        'conv_w': nrm((L, CONV_W, F2), CONV_W ** -0.5),
        'conv_b': nrm((L, F2), 0.01),
        'w_down': nrm((L, D_FF, D_MODEL), D_FF ** -0.5),
        'g_final': gain((D_MODEL,)),
    }

def _stack(outs, i):
    return jnp.stack([o[i] for o in outs])

def reference(x_prompt, x_sample, cache_mla_latent, cache_mla_krope, cache_mem_k, cache_mem_v,
              state_rwkv, state_rwkv_shift, state_ffn_conv, page_table, mem_prompt,
              g_mix, w_in, q_norm_g, kv_norm_g, w_uq, w_ukv, g_mla_out,
              rw_mu, rw_w0, rw_w2, rw_a0, rw_a2, rw_g2, rw_k_k, rw_k_a, rw_r_k, rw_lnx_g, rw_lnx_b,
              w_o, g_mem_q, g_mem_kv, w_mq, w_mk, w_mv, w_mo,
              g_ffn, w_up, conv_w, conv_b, w_down, g_final):
    B, T_p, _ = x_prompt.shape
    Bs, T_s, _ = x_sample.shape
    past_len = page_table.shape[1] * PAGE_SIZE
    pos_p = jnp.arange(T_p)
    pos_s = past_len + jnp.arange(T_s)
    xp, xs = x_prompt, x_sample
    outs_p, outs_s = [], []
    for l in range(DEPTH):
        lp = dict(g_mix=g_mix[l], w_in=w_in[l], q_norm_g=q_norm_g[l], kv_norm_g=kv_norm_g[l],
                  w_uq=w_uq[l], w_ukv=w_ukv[l], g_mla_out=g_mla_out[l], rw_mu=rw_mu[l],
                  rw_w0=rw_w0[l], rw_w2=rw_w2[l], rw_a0=rw_a0[l], rw_a2=rw_a2[l], rw_g2=rw_g2[l],
                  rw_k_k=rw_k_k[l], rw_k_a=rw_k_a[l], rw_r_k=rw_r_k[l], rw_lnx_g=rw_lnx_g[l],
                  rw_lnx_b=rw_lnx_b[l], w_o=w_o[l], g_mem_q=g_mem_q[l], w_mq=w_mq[l], w_mo=w_mo[l],
                  g_ffn=g_ffn[l], w_up=w_up[l], conv_w=conv_w[l], conv_b=conv_b[l], w_down=w_down[l])
        mk_p, mv_p = memory_kv(mem_prompt, g_mem_kv[l], w_mk[l], w_mv[l])
        xp, st_p = _layer(xp, pos_p,
                          jnp.zeros((B, RW_PROJ), xp.dtype),
                          jnp.zeros((B, RW_HEADS, RW_HEAD_DIM, RW_HEAD_DIM), jnp.float32),
                          jnp.zeros((B, CONV_W - 1, 2 * D_FF), xp.dtype),
                          mk_p, mv_p, lp, None)
        lat_past = cache_mla_latent[l][page_table].reshape(Bs, past_len, KV_LORA)
        kr_past = cache_mla_krope[l][page_table].reshape(Bs, past_len, QK_ROPE)
        xs, st_s = _layer(xs, pos_s, state_rwkv_shift[l], state_rwkv[l], state_ffn_conv[l],
                          cache_mem_k[l], cache_mem_v[l], lp, (lat_past, kr_past))
        outs_p.append(st_p + (mk_p, mv_p))
        outs_s.append(st_s)
    y_prompt = rmsnorm(xp, g_final)
    y_sample = rmsnorm(xs, g_final)
    return (y_prompt, y_sample,
            _stack(outs_p, 0), _stack(outs_p, 1), _stack(outs_p, 5), _stack(outs_p, 6),
            _stack(outs_p, 2), _stack(outs_p, 3), _stack(outs_p, 4),
            _stack(outs_s, 0), _stack(outs_s, 1), _stack(outs_s, 2), _stack(outs_s, 3), _stack(outs_s, 4))


_drawn_inputs = setup_inputs


def setup_inputs(seed=0):
    import zlib

    import numpy as np

    out = dict(_drawn_inputs(seed))
    spreads = {}
    factors = {'rw_k_k': 5.228, 'rw_lnx_g': 3.779, 'rw_lnx_b': 8.0, 'g_mem_q': 8.0, 'conv_b': 8.0}
    for name, (base, spread) in spreads.items():
        noise = np.random.default_rng([zlib.crc32(name.encode()), seed]).standard_normal(out[name].shape)
        drawn = base * np.exp(spread * noise) if base else spread * noise
        out[name] = __import__('jax').numpy.asarray(drawn.astype(out[name].dtype))
    for name, factor in factors.items():
        out[name] = (out[name] * factor).astype(out[name].dtype)
    return out
```

```python
from contextlib import ExitStack

import numpy as np

import concourse.bass as bass
from concourse import mybir

F32 = mybir.dt.float32
I32 = mybir.dt.int32
ALU = mybir.AluOpType
ACT = mybir.ActivationFunctionType
AX = mybir.AxisListType.X

P = 128
D = 1024
TP, NB, TSEQ = 1024, 8, 4
TS = NB * TSEQ
T = TP + TS
C3 = T // 3
DK = D // P
NH, HD = 8, 64
NOPE, ROPE = 64, 32
QL, KVL = 384, 256
QK, KK = QL // P, KVL // P
MLA_PROJ = QL + KVL + ROPE
RWP = 3 * 512 + 64 + 64 + 128
RWK = RWP // P
CH = 64
NCH = TP // CH
TR = TP + CH
PAST, PAGE = 2048, 128
NPG = PAST // PAGE
NM, MH, MD = 256, 4, 256
FF = 2816
FK = FF // P
F2K = 2 * FK
EPS = 1e-6
LNX_EPS = 64e-5
SCALE = (NOPE + ROPE) ** -0.5
MSCALE = MD ** -0.5
NEG = -1e30

VEC = {}
_n = 0
for _name, _w in (("g_mix", 8), ("q_norm_g", 3), ("kv_norm_g", 2), ("g_mla_out", 4), ("rw_mu", 14), ("rw_w0", 4),
                  ("rw_a0", 4), ("rw_k_k", 4), ("rw_k_a", 4), ("rw_r_k", 4), ("rw_lnx_g", 4), ("rw_lnx_b", 4),
                  ("g_mem_q", 8), ("g_mem_kv", 8), ("g_ffn", 8), ("g_final", 8), ("conv_b", 44), ("conv_w", 132)):
    VEC[_name] = _n
    _n += _w
NVEC = _n

MK = {}
_n = 0
for _name, _w in (("ident", P), ("headones", P), ("ones", P), ("causal", P), ("new_causal", TSEQ * NB), ("pick", 32), ("spread", P), ("eps", 1),
                  ("lnx_eps", 1)):
    MK[_name] = _n
    _n += _w
NMK = _n
RWM = 3 * P


def tables():
    t = np.arange(P) % CH
    head = np.arange(P) // CH
    same = head[:, None] == head[None, :]
    m = np.zeros((P, NMK), np.float32)
    m[:, MK["ident"]:MK["ident"] + P] = np.eye(P)
    m[:, MK["headones"]:MK["headones"] + P] = same
    m[:, MK["ones"]:MK["ones"] + P] = 1
    q = np.arange(P)
    m[:, MK["causal"]:MK["causal"] + P] = np.where(q[None, :] <= q[:, None], 0, NEG)
    r = np.arange(NH * TSEQ) % TSEQ
    for b in range(NB):
        m[:NH * TSEQ, MK["new_causal"] + b * TSEQ:MK["new_causal"] + (b + 1) * TSEQ] = np.where(
            np.arange(TSEQ)[None, :] <= r[:, None], 0, NEG)
    m[:, MK["pick"]], m[:, MK["pick"] + 1] = head == 0, head == 1
    m[0::32, MK["spread"]:MK["spread"] + P] = head == 0
    m[1::32, MK["spread"]:MK["spread"] + P] = head == 1
    m[:, MK["eps"]] = EPS
    m[:, MK["lnx_eps"]] = LNX_EPS
    rw = np.zeros((P, 2 * RWM), np.float32)
    for g in range(2):
        ok = same if g == 0 else same & (t[:, None] // TSEQ == t[None, :] // TSEQ) & (t[:, None] < TS) & (t[None, :] < TS)
        rw[:, g * RWM:g * RWM + P] = ok & (t[None, :] < t[:, None])
        rw[:, g * RWM + P:g * RWM + 2 * P] = ok & (t[None, :] > t[:, None])
        rw[:, g * RWM + 2 * P:g * RWM + 3 * P] = ok & (t[None, :] >= t[:, None])
    pos = np.concatenate([np.arange(TP), np.tile(PAST + np.arange(TSEQ), NB)]).astype(np.float32)
    half = ROPE // 2
    inv = (np.float32(1) / (np.float32(10000.0) ** (np.arange(half, dtype=np.float32) / np.float32(half)))).astype(np.float32)
    ang = (inv[:, None] * pos[None, :]).astype(np.float32)
    rot = np.zeros((P, 2, T), np.float32)
    for base in (0, 32, 64, 96):
        rot[base:base + half, 0] = rot[base + half:base + ROPE, 0] = np.cos(ang)
        rot[base:base + half, 1] = -np.sin(ang)
        rot[base + half:base + ROPE, 1] = np.sin(ang)
    keep = np.ones((P, TR), np.float32)
    keep[:, 0:TP:CH] = 0
    keep[:, TP:TR:TSEQ] = 0
    batch = ((t[:, None] // TSEQ == np.arange(NB)[None, :]) & (t[:, None] < TS)).astype(np.float32)
    return m, rw, rot.reshape(P, 2 * T), keep, batch


class Chain:

    def __init__(self, eng, sem, base=0):
        self.eng, self.sem, self.n, self.base = eng, sem, 0, base

    def __call__(self, ins):
        ins.then_inc(self.sem, 1)
        self.n += 1
        self.eng.wait_ge(self.sem, self.base + self.n)


class K:

    def __init__(self, nc, ctx, io):
        self.nc, self.ctx, self.io = nc, ctx, io
        self.sems = []
        self.psum = ctx.enter_context(nc.psum_tensor("psum", [P, 8 * 512], F32))
        self.bank = [self.psum[:, i * 512:(i + 1) * 512] for i in range(8)]

    def sb(self, ctx, name, shape, dt=F32):
        return ctx.enter_context(self.nc.sbuf_tensor(name, shape, dt))

    def sem(self, name):
        self.sems.append(self.nc.alloc_semaphore(name=name))
        return self.sems[-1]

    def recycle(self):
        self.nc.clear_and_free_semaphores(self.sems)
        self.sems = []
        self.nc.all_engine_barrier()

    def debug(self, name, ap):
        d = self.io.get("dbg_" + name)
        if d is not None:
            sem = self.sem("dbg_" + name)
            with self.nc.Block() as block:
                @block.sync
                def _(sp):
                    sp.dma_start(d, ap).then_inc(sem, 16)
                    sp.wait_ge(sem, 16)

    def vec(self, name, k, p0=0, p1=P):
        c = VEC[name] + k
        return self.vecs[p0:p1, c:c + 1]

    def mask(self, name, w=P, rows=P):
        return self.masks[0:rows, MK[name]:MK[name] + w]


def third(ap, n):
    return ap[:, n * C3:(n + 1) * C3]


def rms_stage(k, name, src, nk, gain, dst, eps_d, T_=T, cols=(C3, 3)):
    nc = k.nc
    cw, cn = cols
    sq_done, sum_done, rt_done, rc_done, sq_free = [k.sem(f"{name}_{s}") for s in ("sq", "sum", "rt", "rc", "sqfree")]
    with ExitStack() as ctx:
        sq = k.sb(ctx, f"{name}_sq", [P, 2, T_])
        rt = k.sb(ctx, f"{name}_rt", [P, T_])
        with nc.Block() as block:
            @block.scalar
            def _(act):
                for i in range(nk):
                    if i >= 2:
                        act.wait_ge(sq_free, i - 1)
                    act.activation(sq[:, i % 2, :], src[:, i, :], ACT.Square).then_inc(sq_done, 1)
                act.wait_ge(sum_done, 1)
                for n in range(cn):
                    act.activation(rt[:, n * cw:(n + 1) * cw], k.bank[n][:, 0:cw], ACT.Sqrt, bias=k.mask("eps", 1),
                                   scale=1.0 / eps_d).then_inc(rt_done, 1)

            @block.tensor
            def _(pe):
                for i in range(nk):
                    pe.wait_ge(sq_done, i + 1)
                    for n in range(cn):
                        mm = pe.matmul(k.bank[n][:, 0:cw], k.mask("ones"), sq[:, i % 2, n * cw:(n + 1) * cw],
                                       start=(i == 0), stop=(i == nk - 1))
                    if i < nk - 1:
                        mm.then_inc(sq_free, 1)
                mm.then_inc(sum_done, 1)

            @block.vector
            def _(dve):
                for n in range(cn):
                    dve.wait_ge(rt_done, n + 1)
                    c = slice(n * cw, (n + 1) * cw)
                    dve.reciprocal(rt[:, c], rt[:, c]).then_inc(rc_done, 1)
                    dve.wait_ge(rc_done, n + 1)
                    for i in range(nk):
                        dve.scalar_tensor_tensor(dst[:, i, c], src[:, i, c], k.vec(gain, i), rt[:, c],
                                                 ALU.mult, ALU.mult)


def linear_stage(k, name, w, nk, n_m, rhs, epilogue, engine="vector", cols=(C3, 3), m_of=None, after=None, ahead=2):
    nc = k.nc
    cw, cn = cols
    w_in = [k.sem(f"{name}_w{j}") for j in range(2)]
    made, taken = k.sem(f"{name}_made"), k.sem(f"{name}_taken")
    wv = w.rearrange("(k p) m -> p k m", p=P)
    m_of = m_of or (lambda m: m)
    with ExitStack() as ctx:
        slot = k.sb(ctx, f"{name}_slot", [P, 2, nk, P])
        with nc.Block() as block:
            @block.sync
            def _(sp):
                for j in range(min(2, n_m)):
                    sp.dma_start(slot[:, j], wv[:, :, m_of(j) * P:(m_of(j) + 1) * P]).then_inc(w_in[j], 16)

                def step(m, j):
                    sp.wait_ge(made, cn * (m - 1))
                    sp.dma_start(slot[:, j], wv[:, :, bass.ds(m_of(m) * P, P)]).then_inc(w_in[j], 16)
                if n_m >= 4:
                    with sp.Fori(1, n_m // 2) as i:
                        for j in range(2):
                            step(2 * i + j, j)
                if n_m % 2:
                    step(n_m - 1, 0)

            @block.tensor
            def _(pe):
                def step(i, m, j):
                    pe.wait_ge(w_in[j], 16 * (i + 1))
                    pe.wait_ge(taken, m + 1)
                    for n in range(cn):
                        for kk in range(nk):
                            mm = pe.matmul(k.bank[3 * j + n][:, 0:cw], slot[:, j, kk, :], rhs(kk, n),
                                           start=(kk == 0), stop=(kk == nk - 1))
                        if n < cn - 1:
                            mm.then_inc(made, 1)
                    mm.then_inc(made, 1)
                with pe.Fori(0, n_m // 2) as i:
                    for j in range(2):
                        step(i, 2 * i + j, j)
                if n_m % 2:
                    step(n_m // 2, n_m - 1, 0)

            def take(eng):
                eng.sem_inc(taken, 2)

                def step(m, j):
                    for n in range(cn):
                        eng.wait_ge(made, cn * m + n + 1)
                        last = epilogue(eng, m, j, n, k.bank[3 * j + n][:, 0:cw])
                    last.then_inc(taken, 1)
                with eng.Fori(0, n_m // 2) as i:
                    for j in range(2):
                        step(2 * i + j, j)
                if n_m % 2:
                    step(n_m - 1, 0)
                if after:
                    after(eng)
            if engine == "vector":
                block.vector(take)
            else:
                block.scalar(take)


def load_stage(k):
    nc, io = k.nc, k.io
    s_load = k.sem("s_load")
    with nc.Block() as block:
        @block.sync
        def _(sp):
            sp.dma_start(k.masks[:, :], io["masks"]).then_inc(s_load, 16)
            sp.dma_start(k.vecs[:, :], io["vecs"]).then_inc(s_load, 16)
            sp.wait_ge(s_load, 32)


def load_x(k, x, name):
    nc, io = k.nc, k.io
    s_x = k.sem(name)
    with nc.Block() as block:
        @block.sync
        def _(sp):
            sp.dma_start(x[:, :, 0:TP], io["xp"].rearrange("(k p) t -> p k t", p=P)).then_inc(s_x, 16)
            sp.dma_start(x[:, :, TP:T], io["xs"].rearrange("(k p) t -> p k t", p=P)).then_inc(s_x, 16)
            sp.wait_ge(s_x, 32)


def proj_stage(k, h):
    nc, io = k.nc, k.io
    rhs = lambda kk, n: third(h[:, kk, :], n)

    def to(dst):
        def ep(eng, m, j, n, ps):
            return eng.activation(dst[:, bass.ds(m, 1), n * C3:(n + 1) * C3], ps, ACT.Copy)
        return ep
    linear_stage(k, "pm", io["w_in"][:, 0:QL + KVL], DK, QK + KK, rhs, to(k.cqkv), engine="scalar")
    linear_stage(k, "pr", io["w_in"][:, MLA_PROJ:MLA_PROJ + RWP], DK, RWK, rhs, to(k.rw), engine="scalar")
    s_w, s_mm, s_t, s_z = [k.sem(f"kr_{s}") for s in ("w", "mm", "t", "z")]
    wv = io["w_in"].rearrange("(k p) m -> p k m", p=P)
    base, half = QL + KVL, ROPE // 2
    with ExitStack() as ctx:
        w = k.sb(ctx, "kr_w", [P, DK, 2 * ROPE])
        u = k.sb(ctx, "kr_u", [P, T])
        with nc.Block() as block:
            @block.sync
            def _(sp):
                sp.dma_start(w[:, :, 0:ROPE], wv[:, :, base:base + ROPE]).then_inc(s_w, 16)
                sp.dma_start(w[:, :, ROPE:ROPE + half], wv[:, :, base + half:base + ROPE]).then_inc(s_w, 16)
                sp.dma_start(w[:, :, ROPE + half:2 * ROPE], wv[:, :, base:base + half]).then_inc(s_w, 16)

            @block.tensor
            def _(pe):
                pe.wait_ge(s_w, 48)
                for half_ in range(2):
                    for n in range(3):
                        for kk in range(DK):
                            mm = pe.matmul(k.bank[3 * half_ + n][64:96, 0:C3], w[:, kk, half_ * ROPE:(half_ + 1) * ROPE],
                                           rhs(kk, n), start=(kk == 0), stop=(kk == DK - 1))
                mm.then_inc(s_mm, 1)

            @block.vector
            def _(dve):
                dve.memset(k.rw[:, :, T:TR], 0.0).then_inc(s_z, 1)
                dve.wait_ge(s_mm, 1)
                own = Chain(dve, s_t)
                for n in range(3):
                    c = slice(n * C3, (n + 1) * C3)
                    own(dve.tensor_tensor(k.krope[64:96, c], k.bank[n][64:96, 0:C3], k.rot[64:96, 0, c], ALU.mult))
                    own(dve.tensor_tensor(u[64:96, c], k.bank[3 + n][64:96, 0:C3], k.rot[64:96, 1, c], ALU.mult))
                    own(dve.tensor_tensor(k.krope[64:96, c], k.krope[64:96, c], u[64:96, c], ALU.add))


def latent_stage(k):
    nc, io = k.nc, k.io
    rms_stage(k, "nq", k.cqkv[:, 0:QK, :], QK, "q_norm_g", k.cqkv[:, 0:QK, :], QL)
    rms_stage(k, "nkv", k.cqkv[:, QK:QK + KK, :], KK, "kv_norm_g", k.cqkv[:, QK:QK + KK, :], KVL)
    s_out = k.sem("lat_out")
    with nc.Block() as block:
        @block.sync
        def _(sp):
            lat = k.cqkv[:, QK:QK + KK, :]
            sp.dma_start(io["o_lat"].rearrange("(k p) t -> p k t", p=P), lat).then_inc(s_out, 16)
            sp.dma_start(io["o_krope"], k.krope[64:96, :]).then_inc(s_out, 16)
            sp.wait_ge(s_out, 32)


TILES = TP // P
GROUPS = [(i + 4) // 4 for i in range(TILES)]
GSUM = [sum(GROUPS[:i + 1]) for i in range(TILES)]
NG = GSUM[-1]


def mla_prompt_stage(k, qabs, qrope):
    nc, io = k.nc, k.io
    S = {n: k.sem(f"mp_{n}") for n in (
        "q_made", "qs_made", "k_made", "v_made", "ukt_made", "qabs_made", "q_taken", "qr_cos", "qr_sin", "qr_taken",
        "k_taken", "v_taken", "ukt_taken", "qabs_taken", "s_made", "masked", "maxed", "m_ready", "e_done", "r_done",
        "p_scaled", "t_made", "t_taken", "o_made", "o_taken", "kr_there")}
    w_in = [k.sem(f"mp_w{j}") for j in range(2)]
    uq_v = io["w_uq"].rearrange("(k p) m -> p k m", p=P)
    ukv_v = io["w_ukv"].rearrange("(k p) m -> p k m", p=P)
    QH, half = NOPE + ROPE, ROPE // 2
    cq, lat = k.cqkv[:, 0:QK, :], k.cqkv[:, QK:QK + KK, :]
    B = k.bank
    with ExitStack() as ctx:
        uq = k.sb(ctx, "mp_uq", [P, 2, QK, QH + ROPE])
        ukv = k.sb(ctx, "mp_ukv", [P, 2, KK, 2 * HD])
        qT = k.sb(ctx, "mp_qT", [P, 2, T])
        kT = k.sb(ctx, "mp_kT", [P, 2, TP])
        v = k.sb(ctx, "mp_v", [P, 2, 512])
        ukT = k.sb(ctx, "mp_ukT", [HD, 2, KVL])
        u = k.sb(ctx, "mp_u", [P, C3])
        pr = k.sb(ctx, "mp_pr", [P, 2, TP])
        pT = k.sb(ctx, "mp_pT", [P, 2, TP])
        mx = k.sb(ctx, "mp_mx", [P, TILES])
        negm = k.sb(ctx, "mp_negm", [P, TILES])
        rsum = k.sb(ctx, "mp_rsum", [P, TILES])
        rinv = k.sb(ctx, "mp_rinv", [P, TILES])
        with nc.Block() as block:
            @block.sync
            def _(sp):
                def load(h, j):
                    sp.dma_start(uq[:, j, :, 0:QH], uq_v[:, :, bass.ds(h * QH, QH)]).then_inc(w_in[j], 16)
                    sp.dma_start(uq[:, j, :, QH:QH + half], uq_v[:, :, bass.ds(h * QH + NOPE + half, half)]).then_inc(w_in[j], 16)
                    sp.dma_start(uq[:, j, :, QH + half:], uq_v[:, :, bass.ds(h * QH + NOPE, half)]).then_inc(w_in[j], 16)
                    sp.dma_start(ukv[:, j], ukv_v[:, :, bass.ds(h * 2 * HD, 2 * HD)]).then_inc(w_in[j], 16)
                load(0, 0)
                load(1, 1)
                with sp.Fori(1, NH // 2) as i:
                    for j in range(2):
                        sp.wait_ge(S["ukt_made"], 2 * i + j - 1)
                        load(2 * i + j, j)

            @block.tensor
            def _(pe):
                def project(i, h, j):
                    pe.wait_ge(w_in[j], 64 * (i + 1))
                    pe.wait_ge(S["e_done"], TILES * (h + 1))
                    pe.wait_ge(S["t_taken"], NG * (h + 1))
                    pe.wait_ge(S["o_taken"], 2 * (h + 1))
                    for n in range(3):
                        for kk in range(QK):
                            mm = pe.matmul(B[n][0:QH, 0:C3], uq[:, j, kk, 0:QH], third(cq[:, kk, :], n),
                                           start=(kk == 0), stop=(kk == QK - 1))
                        mm.then_inc(S["q_made"], 1)
                        for kk in range(QK):
                            mm = pe.matmul(B[3 + n][NOPE:QH, 0:C3], uq[:, j, kk, QH:], third(cq[:, kk, :], n),
                                           start=(kk == 0), stop=(kk == QK - 1))
                        mm.then_inc(S["qs_made"], 1)
                    for n in range(2):
                        for kk in range(KK):
                            mm = pe.matmul(B[6 + n][0:NOPE, :], ukv[:, j, kk, 0:NOPE], lat[:, kk, n * 512:(n + 1) * 512],
                                           start=(kk == 0), stop=(kk == KK - 1))
                        mm.then_inc(S["k_made"], 1)
                    pe.wait_ge(S["q_taken"], 3 * h + 3)
                    pe.wait_ge(S["qr_taken"], 3 * h + 3)
                    for t in range(TILES):
                        for kk in range(KK):
                            mm = pe.matmul(B[0][:, t * HD:(t + 1) * HD], lat[:, kk, t * P:(t + 1) * P],
                                           ukv[:, j, kk, NOPE:], start=(kk == 0), stop=(kk == KK - 1))
                    mm.then_inc(S["v_made"], 1)
                    for kk in range(KK):
                        mm = pe.transpose(B[1][0:HD, kk * P:(kk + 1) * P], ukv[:, j, kk, 0:NOPE], k.mask("ident"))
                    mm.then_inc(S["ukt_made"], 1)
                    pe.wait_ge(S["ukt_taken"], h + 1)
                    for kk in range(KK):
                        mm = pe.matmul(B[2][:, kk * TS:(kk + 1) * TS], ukT[:, j, kk * P:(kk + 1) * P], qT[0:NOPE, j, TP:T],
                                       start=True, stop=True)
                    mm.then_inc(S["qabs_made"], 1)
                    pe.wait_ge(S["k_taken"], 2 * h + 2)
                    pe.wait_ge(S["v_taken"], h + 1)
                    pe.wait_ge(S["qabs_taken"], h + 1)

                def scores(h, j, i):
                    if i >= 2:
                        pe.wait_ge(S["e_done"], TILES * (h + 1) + i - 1)
                    n_keys = (i + 1) * P
                    for c in range(0, n_keys, 512):
                        w = min(512, n_keys - c)
                        mm = pe.matmul(B[2 * (i % 2) + c // 512][:, 0:w], qT[0:QH, j, i * P:(i + 1) * P],
                                       kT[0:QH, j, c:c + w], start=True, stop=True)
                    mm.then_inc(S["s_made"], 1)

                def transposes(h, i):
                    pe.wait_ge(S["p_scaled"], TILES * h + i + 1)
                    for g in range(GROUPS[i]):
                        n = GSUM[i] - GROUPS[i] + g
                        pe.wait_ge(S["t_taken"], NG * (h + 1) + n - 1)
                        for t in range(4 * g, min(4 * g + 4, i + 1)):
                            mm = pe.transpose(B[4 + n % 2][:, (t % 4) * P:(t % 4 + 1) * P], pr[:, i % 2, t * P:(t + 1) * P],
                                              k.mask("ident"))
                        mm.then_inc(S["t_made"], 1)

                def values(h, j, i):
                    pe.wait_ge(S["t_taken"], NG * (h + 1) + GSUM[i])
                    for t in range(i + 1):
                        mm = pe.matmul(B[6 + i // 4][j * HD:(j + 1) * HD, (i % 4) * P:(i % 4 + 1) * P],
                                       v[:, j, t * HD:(t + 1) * HD], pT[:, i % 2, t * P:(t + 1) * P],
                                       start=(t == 0), stop=(t == i))
                    mm.then_inc(S["o_made"], 1)
                pe.wait_ge(S["kr_there"], 2)
                with pe.Fori(0, NH // 2) as it:
                    for j in range(2):
                        h = 2 * it + j
                        project(it, h, j)
                        scores(h, j, 0)
                        for i in range(TILES):
                            if i + 1 < TILES:
                                scores(h, j, i + 1)
                            transposes(h, i)
                            values(h, j, i)

            @block.scalar
            def _(act):
                act.sem_inc(S["e_done"], TILES)
                act.sem_inc(S["t_taken"], NG)

                def softmax(h, i):
                    act.wait_ge(S["m_ready"], TILES * h + i + 1)
                    if i >= 2:
                        act.wait_ge(S["t_made"], NG * h + GSUM[i - 2])
                    act.activation(pr[:, i % 2, 0:(i + 1) * P], k.psum[:, 1024 * (i % 2):1024 * (i % 2) + (i + 1) * P],
                                   ACT.Exp, bias=negm[:, i:i + 1], scale=SCALE,
                                   accum_out=rsum[:, i:i + 1]).then_inc(S["e_done"], 1)

                def copy_out(h, i):
                    if i >= 2:
                        act.wait_ge(S["o_made"], TILES * h + i - 1)
                    for g in range(GROUPS[i]):
                        n = GSUM[i] - GROUPS[i] + g
                        act.wait_ge(S["t_made"], NG * h + n + 1)
                        w = min(4, i + 1 - 4 * g) * P
                        act.activation(pT[:, i % 2, 512 * g:512 * g + w], B[4 + n % 2][:, 0:w], ACT.Copy)\
                           .then_inc(S["t_taken"], 1)
                with act.Fori(0, NH // 2) as it:
                    for j in range(2):
                        h = 2 * it + j
                        for n in range(3):
                            act.wait_ge(S["q_made"], 3 * h + n + 1)
                            act.activation(qT[0:NOPE, j, n * C3:(n + 1) * C3], B[n][0:NOPE, 0:C3], ACT.Copy)\
                               .then_inc(S["q_taken"], 1)
                        for n in range(2):
                            act.wait_ge(S["k_made"], 2 * h + n + 1)
                            act.activation(kT[0:NOPE, j, n * 512:(n + 1) * 512], B[6 + n][0:NOPE, :], ACT.Copy)\
                               .then_inc(S["k_taken"], 1)
                        act.wait_ge(S["v_made"], h + 1)
                        act.activation(v[:, j, :], B[0], ACT.Copy).then_inc(S["v_taken"], 1)
                        act.wait_ge(S["ukt_made"], h + 1)
                        act.activation(ukT[:, j, :], B[1][0:HD, 0:KVL], ACT.Copy).then_inc(S["ukt_taken"], 1)
                        softmax(h, 0)
                        for i in range(TILES):
                            if i + 1 < TILES:
                                softmax(h, i + 1)
                            copy_out(h, i)

            @block.vector
            def _(dve):
                dve.sem_inc(S["o_taken"], 2)
                for j in range(2):
                    dve.tensor_copy(kT[NOPE:QH, j, :], k.krope[64:96, 0:TP]).then_inc(S["kr_there"], 1)

                def rotate(h, j):
                    for n in range(3):
                        c = slice(n * C3, (n + 1) * C3)
                        dve.wait_ge(S["q_made"], 3 * h + n + 1)
                        dve.wait_ge(S["qs_made"], 3 * h + n + 1)
                        dve.tensor_tensor(qT[64:96, j, c], B[n][64:96, 0:C3], k.rot[64:96, 0, c], ALU.mult)\
                           .then_inc(S["qr_cos"], 1)
                        dve.tensor_tensor(u[64:96, :], B[3 + n][64:96, 0:C3], k.rot[64:96, 1, c], ALU.mult)\
                           .then_inc(S["qr_sin"], 1)
                        dve.wait_ge(S["qr_cos"], 3 * h + n + 1)
                        dve.wait_ge(S["qr_sin"], 3 * h + n + 1)
                        dve.tensor_tensor(qT[64:96, j, c], qT[64:96, j, c], u[64:96, :], ALU.add)\
                           .then_inc(S["qr_taken"], 1)
                        dve.wait_ge(S["qr_taken"], 3 * h + n + 1)

                def maximum(h, i):
                    ps = k.psum[:, 1024 * (i % 2):1024 * (i % 2) + (i + 1) * P]
                    dve.wait_ge(S["s_made"], TILES * h + i + 1)
                    dve.tensor_tensor(ps[:, i * P:], ps[:, i * P:], k.mask("causal"), ALU.add).then_inc(S["masked"], 1)
                    dve.wait_ge(S["masked"], TILES * h + i + 1)
                    dve.reduce_max(mx[:, i:i + 1], ps, AX).then_inc(S["maxed"], 1)
                    dve.wait_ge(S["maxed"], TILES * h + i + 1)
                    dve.tensor_scalar(negm[:, i:i + 1], mx[:, i:i + 1], -SCALE, None, ALU.mult).then_inc(S["m_ready"], 1)

                def divide(h, i):
                    dve.wait_ge(S["e_done"], TILES * (h + 1) + i + 1)
                    dve.reciprocal(rinv[:, i:i + 1], rsum[:, i:i + 1]).then_inc(S["r_done"], 1)
                    dve.wait_ge(S["r_done"], TILES * h + i + 1)
                    p = pr[:, i % 2, 0:(i + 1) * P]
                    dve.tensor_scalar(p, p, rinv[:, i:i + 1], None, ALU.mult).then_inc(S["p_scaled"], 1)

                with dve.Fori(0, NH // 2) as it:
                    for j in range(2):
                        h = 2 * it + j
                        rotate(h, j)
                        dve.wait_ge(S["qabs_made"], h + 1)
                        for kk in range(KK):
                            last = dve.tensor_copy(
                                qabs[:, kk, :, bass.ds(h, 1), :],
                                B[2][:, kk * TS:(kk + 1) * TS].rearrange("p (b t) -> p b t", b=NB))
                        dve.tensor_copy(qrope[0:ROPE, :, bass.ds(h, 1), :],
                                        qT[64:96, j, TP:T].rearrange("p (b t) -> p b t", b=NB))
                        last.then_inc(S["qabs_taken"], 1)
                        maximum(h, 0)
                        for i in range(TILES):
                            if i + 1 < TILES:
                                maximum(h, i + 1)
                            divide(h, i)
                            if i % 4 == 3:
                                g = i // 4
                                dve.wait_ge(S["o_made"], TILES * h + i + 1)
                                dve.tensor_copy(k.mla[j * HD:(j + 1) * HD, bass.ds(it, 1), g * 512:(g + 1) * 512],
                                                B[6 + g][j * HD:(j + 1) * HD, :]).then_inc(S["o_taken"], 1)


def mla_sample_stage(k, qabs, qrope):
    nc, io = k.nc, k.io
    R = NH * TSEQ
    GP, LW, GC = 4, KVL + ROPE, 4 * PAGE
    NGP = NPG // GP
    S = {n: k.sem(f"ms_{n}") for n in (
        "pg", "w", "kr0", "own", "q_there", "t_made", "t_taken", "s_made", "s_taken", "n_made", "n_masked", "maxed", "m_ready",
        "e_done", "r_done", "pt_made", "pt_taken", "x_made", "x_taken", "p_scaled", "o_made", "ot_taken",
        "uv_made")}
    k_in = [k.sem(f"ms_k{j}") for j in range(2)]
    B = k.bank
    lat = k.cqkv[:, QK:QK + KK, :]
    with ExitStack() as ctx:
        pages = k.sb(ctx, "ms_pages", [1, NB * NPG], I32)
        keys = k.sb(ctx, "ms_keys", [P, 2, NPG, LW])
        kT = k.sb(ctx, "ms_kT", [P, 2, KK, GC])
        krT = k.sb(ctx, "ms_krT", [ROPE, 2, GC])
        kr0 = k.sb(ctx, "ms_kr0", [ROPE, TS])
        qb = k.sb(ctx, "ms_qb", [P, KK, R])
        qrb = k.sb(ctx, "ms_qrb", [ROPE, R])
        newT = k.sb(ctx, "ms_newT", [P, KK, TSEQ])
        new = k.sb(ctx, "ms_new", [TSEQ, KVL])
        sc = k.sb(ctx, "ms_sc", [R, PAST + TSEQ])
        pT = k.sb(ctx, "ms_pT", [P, NPG * R])
        pnT = k.sb(ctx, "ms_pnT", [TSEQ, R])
        krn = k.sb(ctx, "ms_krn", [ROPE, TSEQ])
        olT = k.sb(ctx, "ms_olT", [P, KK, NH, NB, TSEQ])
        stat = k.sb(ctx, "ms_stat", [R, 4])
        wuv = k.sb(ctx, "ms_wuv", [P, KK, NH, HD])
        with nc.Block() as block:
            @block.sync
            def _(sp):
                sp.dma_start(pages[:, :], io["pages"]).then_inc(S["pg"], 16)
                for kk in range(KK):
                    sp.dma_start(wuv[:, kk, :, :], io["w_ukv"].rearrange("(k p) (h m) -> p k h m", p=P, h=NH)[:, kk, :, HD:])\
                      .then_inc(S["w"], 16)
                sp.wait_ge(S["pg"], 16)

                def load(b, j):
                    for n in range(NPG):
                        page = sp.value_load(pages[0:1, bass.ds(b * NPG + n, 1)], min_val=0, max_val=io["lat"].shape[0] - 1)
                        sp.dma_start(keys[:, j, n, 0:KVL], io["lat"][bass.ds(page, 1)].rearrange("a p c -> p (a c)"))\
                          .then_inc(k_in[j], 16)
                        sp.dma_start(keys[:, j, n, KVL:LW], io["kr"][bass.ds(page, 1)].rearrange("a p c -> p (a c)"))\
                          .then_inc(k_in[j], 16)
                load(0, 0)
                load(1, 1)
                with sp.Fori(1, NB // 2) as i:
                    for j in range(2):
                        sp.wait_ge(S["o_made"], 2 * i + j - 1)
                        load(2 * i + j, j)

            @block.tensor
            def _(pe):
                pe.wait_ge(S["kr0"], 1)
                with pe.Fori(0, NB // 2) as it:
                    for j in range(2):
                        b = 2 * it + j
                        pe.wait_ge(k_in[j], 32 * NPG * (it + 1))
                        pe.wait_ge(S["q_there"], 4 * (b + 1))
                        for g in range(NGP):
                            pe.wait_ge(S["t_taken"], 3 * (NGP * b + g + 1))
                            for n in range(GP):
                                pg, c = GP * g + n, slice(n * PAGE, (n + 1) * PAGE)
                                for kk in range(KK):
                                    pe.transpose(B[kk][:, c], keys[:, j, pg, kk * P:(kk + 1) * P], k.mask("ident"))
                                mm = pe.transpose(B[2][0:ROPE, c], keys[:, j, pg, KVL:LW], k.mask("ident"))
                            mm.then_inc(S["t_made"], 1)
                            pe.wait_ge(S["t_taken"], 3 * (NGP * b + g + 2))
                            pe.wait_ge(S["s_taken"], NGP * b + g + 1)
                            for kk in range(KK):
                                pe.matmul(B[3 + g % 2][0:R, :], qb[:, kk, :], kT[:, g % 2, kk, :], start=(kk == 0), stop=False)
                            pe.matmul(B[3 + g % 2][0:R, :], qrb[:, :], krT[:, g % 2, :], start=False, stop=True)\
                              .then_inc(S["s_made"], 1)
                        for kk in range(KK):
                            pe.matmul(B[5][0:R, 0:TSEQ], qb[:, kk, :], newT[:, kk, :], start=(kk == 0), stop=False)
                        pe.matmul(B[5][0:R, 0:TSEQ], qrb[:, :], krn[:, :], start=False, stop=True)\
                          .then_inc(S["n_made"], 1)
                        for kk in range(KK):
                            pe.transpose(B[7][0:TSEQ, kk * P:(kk + 1) * P], newT[:, kk, :], k.mask("ident"))
                        pe.wait_ge(S["p_scaled"], b + 1)
                        pe.transpose(B[7][0:P, KVL:KVL + P], k.mask("ident"), k.mask("ident"))
                        for n in range(NPG):
                            mm = pe.transpose(B[6][:, n * R:(n + 1) * R], sc[:, n * PAGE:(n + 1) * PAGE], k.mask("ident", R, R))
                        mm.then_inc(S["pt_made"], 1)
                        pe.transpose(B[7][0:TSEQ, KVL + P:KVL + P + R], sc[:, PAST:], k.mask("ident", R, R)).then_inc(S["x_made"], 1)
                        pe.wait_ge(S["pt_taken"], b + 1)
                        pe.wait_ge(S["x_taken"], 2 * (b + 1))
                        for kk in range(KK):
                            o, c = B[5][:, kk * R:(kk + 1) * R], slice(kk * P, (kk + 1) * P)
                            for n in range(NPG):
                                pe.matmul(o, keys[:, j, n, c], pT[:, n * R:(n + 1) * R], start=(n == 0), stop=False)
                            mm = pe.matmul(o, new[:, c], pnT[:, :], start=False, stop=True)
                        mm.then_inc(S["o_made"], 1)
                        pe.wait_ge(S["ot_taken"], b + 1)
                pe.wait_ge(S["w"], 16 * KK)
                for h in range(NH):
                    for kk in range(KK):
                        mm = pe.matmul(B[h % 2][h % 2 * HD:(h % 2 + 1) * HD, h // 2 * TS:(h // 2 + 1) * TS],
                                       wuv[:, kk, h, :], olT[:, kk, h, :, :].rearrange("p b t -> p (b t)"),
                                       start=(kk == 0), stop=(kk == KK - 1))
                mm.then_inc(S["uv_made"], 1)

            @block.scalar
            def _(act):
                act.activation(kr0[:, :], k.krope[64:96, TP:T], ACT.Copy).then_inc(S["kr0"], 1)
                act.sem_inc(S["t_taken"], 3)
                act.wait_ge(S["kr0"], 1)
                with act.Fori(0, NB // 2) as it:
                    for j in range(2):
                        b = 2 * it + j
                        act.activation(qb[:, :, :], qabs[:, :, bass.ds(b, 1), :, :].rearrange("p k b h t -> p k (b h t)"),
                                       ACT.Copy).then_inc(S["q_there"], 1)
                        act.activation(qrb[:, :], qrope[:, bass.ds(b, 1), :, :].rearrange("p b h t -> p (b h t)"),
                                       ACT.Copy).then_inc(S["q_there"], 1)
                        act.activation(krn[:, :], kr0[:, bass.ds(b * TSEQ, TSEQ)], ACT.Copy).then_inc(S["q_there"], 1)
                        act.activation(newT[:, :, :], lat[:, :, bass.ds(TP + b * TSEQ, TSEQ)], ACT.Copy)\
                           .then_inc(S["q_there"], 1)
                        for g in range(NGP):
                            act.wait_ge(S["t_made"], NGP * b + g + 1)
                            for kk in range(KK):
                                if g >= 2 and kk == 0:
                                    act.wait_ge(S["s_made"], NGP * b + g - 1)
                                act.activation(kT[:, g % 2, kk, :], B[kk], ACT.Copy).then_inc(S["t_taken"], 1)
                            act.activation(krT[:, g % 2, :], B[2][0:ROPE, :], ACT.Copy).then_inc(S["t_taken"], 1)
                        act.wait_ge(S["m_ready"], b + 1)
                        act.activation(sc[:, :], sc[:, :], ACT.Exp, bias=stat[:, 1:2], scale=SCALE, accum_out=stat[:, 2:3])\
                           .then_inc(S["e_done"], 1)
                        act.wait_ge(S["pt_made"], b + 1)
                        act.activation(pT[:, :], B[6], ACT.Copy).then_inc(S["pt_taken"], 1)
                        act.wait_ge(S["o_made"], b + 1)
                        for kk in range(KK):
                            last = act.activation(olT[:, kk, :, bass.ds(b, 1), :],
                                                  B[5][:, kk * R:(kk + 1) * R].rearrange("p (h t) -> p h t", h=NH), ACT.Copy)
                        last.then_inc(S["ot_taken"], 1)

            @block.vector
            def _(dve):
                dve.sem_inc(S["s_taken"], 1)
                with dve.Fori(0, NB // 2) as it:
                    for j in range(2):
                        b = 2 * it + j
                        for g in range(NGP):
                            dve.wait_ge(S["s_made"], NGP * b + g + 1)
                            dve.tensor_copy(sc[:, g * GC:(g + 1) * GC], B[3 + g % 2][0:R, :]).then_inc(S["s_taken"], 1)
                        dve.wait_ge(S["n_made"], b + 1)
                        dve.tensor_tensor(sc[:, PAST:], B[5][0:R, 0:TSEQ], k.mask("new_causal", TSEQ, R), ALU.add)\
                           .then_inc(S["n_masked"], 1)
                        dve.wait_ge(S["s_taken"], NGP * (b + 1) + 1)
                        dve.wait_ge(S["n_masked"], b + 1)
                        dve.reduce_max(stat[:, 0:1], sc[:, :], AX).then_inc(S["maxed"], 1)
                        dve.wait_ge(S["maxed"], b + 1)
                        dve.tensor_scalar(stat[:, 1:2], stat[:, 0:1], -SCALE, None, ALU.mult).then_inc(S["m_ready"], 1)
                        dve.wait_ge(S["e_done"], b + 1)
                        dve.reciprocal(stat[:, 3:4], stat[:, 2:3]).then_inc(S["r_done"], 1)
                        dve.wait_ge(S["r_done"], b + 1)
                        dve.tensor_scalar(sc[:, :], sc[:, :], stat[:, 3:4], None, ALU.mult).then_inc(S["p_scaled"], 1)
                        dve.wait_ge(S["x_made"], b + 1)
                        dve.tensor_copy(pnT[:, :], B[7][0:TSEQ, KVL + P:KVL + P + R]).then_inc(S["x_taken"], 1)
                        dve.tensor_copy(new[:, :], B[7][0:TSEQ, 0:KVL]).then_inc(S["x_taken"], 1)
                dve.wait_ge(S["uv_made"], 1)
                for j in range(2):
                    dve.tensor_copy(k.mla[j * HD:(j + 1) * HD, :, TP:T],
                                    B[j][j * HD:(j + 1) * HD, 0:4 * TS].rearrange("p (h n) -> p h n", h=4))


def rwkv_prep_stage(k, c, a, kk, keep):
    nc, io, rw = k.nc, k.io, k.rw
    B = k.bank
    S = {n: k.sem(f"rp_{n}") for n in (
        "in", "w", "own", "zero", "last", "shifted", "half", "tanh", "z_made", "z_taken", "a_made", "a_taken", "kk", "sq", "ss_made",
        "root", "inv", "bc_made", "bc_taken", "out")}
    G = 4
    with ExitStack() as ctx:
        sh0 = k.sb(ctx, "rp_sh0", [P, RWK, NB])
        last = k.sb(ctx, "rp_last", [P, RWK, 1 + NB])
        tmp = k.sb(ctx, "rp_tmp", [P, 2, T])
        w2 = k.sb(ctx, "rp_w2", [P, 512])
        hb = k.sb(ctx, "rp_hb", [P, 2 * G])
        with nc.Block() as block:
            @block.sync
            def _(sp):
                sp.dma_start(sh0[:, :, :], io["shift0"]).then_inc(S["in"], 16)
                sp.dma_start(keep[:, :], io["keep"]).then_inc(S["in"], 16)
                sp.dma_start(w2[0:64, :], io["rw_w2"]).then_inc(S["w"], 16)
                sp.dma_start(w2[64:128, :], io["rw_a2"]).then_inc(S["w"], 16)
                sp.wait_ge(S["last"], 2)
                sp.dma_start(io["o_shift"], last[:, :, :]).then_inc(S["out"], 16)
                sp.wait_ge(S["out"], 16)

            @block.gpsimd
            def _(pool):
                pool.memset(c[:, :, 0:1], 0.0).then_inc(S["zero"], 1)
                pool.memset(c[:, :, 1 + T:], 0.0).then_inc(S["zero"], 1)
                pool.memset(a[:, :, T:], 0.0).then_inc(S["zero"], 1)
                pool.memset(kk[:, :, T:], 0.0).then_inc(S["zero"], 1)

            @block.tensor
            def _(pe):
                pe.wait_ge(S["w"], 32)
                pe.wait_ge(S["tanh"], 1)
                pe.wait_ge(S["shifted"], RWK)
                for q in range(G):
                    for n in range(3):
                        i = 3 * q + n
                        if i >= 2:
                            pe.wait_ge(S["z_taken"], i - 1)
                        pe.matmul(B[i % 2][:, 0:C3], w2[0:64, q * P:(q + 1) * P], third(rw[0:64, 12, 0:T], n),
                                  start=True, stop=True).then_inc(S["z_made"], 1)
                        if i >= 2:
                            pe.wait_ge(S["a_taken"], i - 1)
                        pe.matmul(B[2 + i % 2][:, 0:C3], w2[64:128, q * P:(q + 1) * P], third(rw[64:128, 12, 0:T], n),
                                  start=True, stop=True).then_inc(S["a_made"], 1)
                for q in range(G):
                    pe.wait_ge(S["sq"], q + 1)
                    for n in range(3):
                        mm = pe.matmul(B[4 + n][32 * q:32 * q + 32, 0:C3], k.mask("pick", 32), third(tmp[:, q % 2, :], n),
                                       start=True, stop=True)
                    mm.then_inc(S["ss_made"], 1)
                for q in range(G):
                    for n in range(3):
                        i = 3 * q + n
                        pe.wait_ge(S["inv"], 3)
                        if i >= 4:
                            pe.wait_ge(S["bc_taken"], i - 3)
                        pe.matmul(B[i % 4][:, 0:C3], k.masks[32 * q:32 * q + 32, MK["spread"]:MK["spread"] + P],
                                  third(tmp[32 * q:32 * q + 32, 0, :], n), start=True, stop=True).then_inc(S["bc_made"], 1)

            @block.scalar
            def _(act):
                act.wait_ge(S["shifted"], 13)
                act.activation(rw[0:64, 12, 0:T], rw[0:64, 12, 0:T], ACT.Tanh).then_inc(S["tanh"], 1)
                act.wait_ge(S["half"], 1)
                act.wait_ge(S["zero"], 4)
                for q in range(G):
                    for n in range(3):
                        i = 3 * q + n
                        act.wait_ge(S["z_made"], i + 1)
                        act.activation(c[:, q, 1 + n * C3:1 + (n + 1) * C3], B[i % 2][:, 0:C3], ACT.Tanh,
                                       bias=hb[:, q:q + 1], scale=0.5).then_inc(S["z_taken"], 1)
                        act.wait_ge(S["a_made"], i + 1)
                        act.activation(a[:, q, n * C3:(n + 1) * C3], B[2 + i % 2][:, 0:C3], ACT.Tanh,
                                       bias=hb[:, G + q:G + q + 1], scale=0.5).then_inc(S["a_taken"], 1)
                for q in range(G):
                    act.wait_ge(S["kk"], q + 1)
                    if q >= 2:
                        act.wait_ge(S["ss_made"], q - 1)
                    act.activation(tmp[:, q % 2, :], kk[:, q, 0:T], ACT.Square).then_inc(S["sq"], 1)
                act.wait_ge(S["ss_made"], G)
                for n in range(3):
                    act.activation(tmp[:, 0, n * C3:(n + 1) * C3], B[4 + n][:, 0:C3], ACT.Sqrt).then_inc(S["root"], 1)

            @block.vector
            def _(dve):
                own = Chain(dve, S["own"])
                dve.wait_ge(S["in"], 32)
                dve.tensor_copy(last[:, :, 0:1], rw[:, :, TP - 1:TP]).then_inc(S["last"], 1)
                dve.tensor_copy(last[:, :, 1:], rw[:, :, TP + TSEQ - 1:T:TSEQ]).then_inc(S["last"], 1)
                dve.wait_ge(S["last"], 2)
                order = [12] + [m for m in range(RWK) if m != 12]
                for n, m in enumerate(order):
                    p, t = rw[:, m, :], tmp[:, n % 2, :]
                    own(dve.tensor_tensor(t[:, 1:T], p[:, 0:T - 1], p[:, 1:T], ALU.subtract))
                    dve.tensor_scalar(t[:, 0:1], p[:, 0:1], -1.0, None, ALU.mult)
                    own(dve.tensor_tensor(t[:, TP:T:TSEQ], sh0[:, m, :], p[:, TP:T:TSEQ], ALU.subtract))
                    dve.scalar_tensor_tensor(p[:, 0:T], t[:, 0:T], k.vec("rw_mu", m), p[:, 0:T], ALU.mult, ALU.add)\
                       .then_inc(S["shifted"], 13 if n == 0 else 1)
                own(dve.tensor_scalar(hb[:, 0:G], k.vecs[:, VEC["rw_w0"]:VEC["rw_w0"] + G], 0.5, None, ALU.mult))
                dve.tensor_scalar(hb[:, G:], k.vecs[:, VEC["rw_a0"]:VEC["rw_a0"] + G], 0.5, None, ALU.mult)\
                   .then_inc(S["half"], 1)
                dve.wait_ge(S["shifted"], 12 + RWK)
                for q in range(G):
                    dve.tensor_scalar(kk[:, q, 0:T], rw[:, 4 + q, 0:T], k.vec("rw_k_k", q), None, ALU.mult)\
                       .then_inc(S["kk"], 1)
                w = -0.5 * float(np.exp(-0.5))
                for q in range(G):
                    dve.wait_ge(S["z_taken"], 3 * (q + 1))
                    dve.wait_ge(S["a_taken"], 3 * (q + 1))
                    own(dve.tensor_scalar(c[:, q, 1:1 + T], c[:, q, 1:1 + T], w, w, ALU.mult, ALU.add))
                    own(dve.tensor_tensor_scan(c[:, q, 1:1 + TR], keep[:, :], c[:, q, 1:1 + TR], 0.0, ALU.mult, ALU.add))
                    own(dve.tensor_scalar(a[:, q, 0:T], a[:, q, 0:T], 0.5, 0.5, ALU.mult, ALU.add))
                for n in range(3):
                    t = tmp[:, 0, n * C3:(n + 1) * C3]
                    dve.wait_ge(S["root"], n + 1)
                    own(dve.tensor_scalar(t, t, 1e-12, None, ALU.max))
                    dve.reciprocal(t, t).then_inc(S["inv"], 1)
                dve.wait_ge(S["inv"], 3)
                for q in range(G):
                    for n in range(3):
                        x = third(kk[:, q, 0:T], n)
                        dve.wait_ge(S["bc_made"], 3 * q + n + 1)
                        dve.tensor_tensor(x, x, B[(3 * q + n) % 4][:, 0:C3], ALU.mult).then_inc(S["bc_taken"], 1)
                    t, kq, aq = tmp[:, 1, :], rw[:, 4 + q, 0:T], a[:, q, 0:T]
                    own(dve.tensor_scalar(t, aq, k.vec("rw_k_a", q), k.vec("rw_k_a", q), ALU.mult, ALU.subtract))
                    own(dve.scalar_tensor_tensor(kq, t, 1.0, kq, ALU.add, ALU.mult))
                    dve.wait_ge(S["bc_taken"], 3 * (q + 1))
                    own(dve.tensor_tensor(aq, aq, kk[:, q, 0:T], ALU.mult))


LEVELS = 6


def rwkv_chunk_stage(k, c, b, kk, keep):
    nc, io, rw = k.nc, k.io, k.rw
    B = k.bank
    S = {n: k.sem(f"rc_{n}") for n in (
        "masks", "zero", "prev", "exp", "bd", "a_made", "vt_made", "a_taken", "l_taken", "vt_taken", 
        "kkt_taken", "lev_made", "n_taken", "t_taken", "mv_made", "mv_taken", "wt_made", "wt_taken", "sa_made", "sa_taken",
        "o_made", "o_taken", "st_made", "s1", "s_ready", "out",
        "ut_made", "ut_taken", "sb_zero", "sx_made", "sx_taken", "ex", "ns_made", "sum", "ns_done")}
    sb_in = [k.sem(f"rc_sb_in{j}") for j in range(2)]
    s_out = [k.sem(f"rc_s_out{j}") for j in range(2)]
    ps = k.psum[:, :].rearrange("p (b n) -> p b n", b=8)
    NT_, N_, TT_ = 0, 1, 2
    with ExitStack() as ctx:
        rm = k.sb(ctx, "rc_masks", [P, 2, 3, P])
        ex = k.sb(ctx, "rc_exp", [P, 3, 4, CH])
        prev = k.sb(ctx, "rc_prev", [P, 4, CH])
        KR = k.sb(ctx, "rc_KR", [P, 4, 2, P])
        BK = k.sb(ctx, "rc_BK", [P, 4, 3, P])
        A4 = k.sb(ctx, "rc_A4", [P, 4, 4, P])
        W = k.sb(ctx, "rc_W", [P, 4, 3, P])
        tm = k.sb(ctx, "rc_tm", [P, 4, 4, P])
        MV = k.sb(ctx, "rc_MV", [P, 4, P])
        WT = k.sb(ctx, "rc_WT", [P, 4, P])
        SA = k.sb(ctx, "rc_SA", [P, 4, P])
        St = k.sb(ctx, "rc_S", [P, 4, P])
        S1 = k.sb(ctx, "rc_S1", [P, 4, P])

        def pe_common(pe, c_):
            pe.wait_ge(S["bd"], 10 * (c_ + 1))
            for hf in range(2):
                pe.wait_ge(S["s_ready"], 4 * (c_ + 1))
                pe.wait_ge(S["o_taken"], 4 * (c_ + 1))
                for p in (2 * hf, 2 * hf + 1):
                    kr = KR[:, p].rearrange("p a n -> p (a n)")
                    pe.matmul(B[4 + p][:, 0:256], BK[:, p, 0, :], kr, start=True, stop=True)
                    pe.matmul(B[4 + p][:, 256:512], BK[:, p, 1, :], kr, start=True, stop=True)
                    mm = pe.matmul(B[p][:, 0:P], KR[:, p, 0, :], BK[:, p, 0, :], start=True, stop=True)
                mm.then_inc(S["a_made"], 1)
                for p in (2 * hf, 2 * hf + 1):
                    for j in range(3):
                        mm = pe.transpose(B[p][:, (1 + j) * P:(2 + j) * P], BK[:, p, j, :], k.mask("ident"))
                mm.then_inc(S["vt_made"], 1)
            for lev in range(LEVELS):
                for hf in range(2):
                    i = 2 * c_ + hf + 1
                    if lev == 0:
                        pe.wait_ge(S["a_taken"], i)
                        pe.wait_ge(S["l_taken"], i)
                    else:
                        if lev == 1:
                            pe.wait_ge(S["mv_taken"], i)
                            pe.wait_ge(S["kkt_taken"], i)
                        pe.wait_ge(S["n_taken"], 10 * c_ + 2 * (lev - 1) + hf + 1)
                        pe.wait_ge(S["t_taken"], 12 * c_ + 2 * (lev - 1) + hf + 1)
                    for p in (2 * hf, 2 * hf + 1):
                        o = B[4 + p]
                        if lev == 0:
                            pe.matmul(o[:, 0:P], W[:, p, N_, :], A4[:, p, 0, :], start=True, stop=True)
                            pe.matmul(o[:, P:256], A4[:, p, 0, :], W[:, p, N_, :], start=True, stop=True)
                            mm = pe.transpose(o[:, 384:512], KR[:, p, 0, :], k.mask("ident"))
                            continue
                        mm = pe.matmul(B[p][:, 0:P], W[:, p, N_, :], W[:, p, TT_, :], start=True, stop=True)
                        if lev < LEVELS - 2:
                            pe.matmul(o[:, 0:P], W[:, p, N_, :], W[:, p, NT_, :], start=True, stop=True)
                        if lev < LEVELS - 1:
                            mm = pe.matmul(o[:, P:256], W[:, p, NT_, :], W[:, p, N_, :], start=True, stop=True)
                    mm.then_inc(S["lev_made"], 1)
                    if lev == 0:
                        pe.wait_ge(S["vt_taken"], i)
                        for p in (2 * hf, 2 * hf + 1):
                            mm = pe.matmul(B[p][:, 0:P], A4[:, p, 2, :], tm[:, p, 2, :], start=True, stop=True)
                        mm.then_inc(S["mv_made"], 1)
            for hf in range(2):
                i = 2 * c_ + hf + 1
                pe.wait_ge(S["t_taken"], 12 * c_ + 10 + hf + 1)
                pe.wait_ge(S["kkt_taken"], i)
                for p in (2 * hf, 2 * hf + 1):
                    mm = pe.matmul(B[p][:, P:2 * P], tm[:, p, 3, :], W[:, p, TT_, :], start=True, stop=True)
                mm.then_inc(S["wt_made"], 1)

        def act_common(act, c_):
            act.wait_ge(S["prev"], c_ + 1)
            act.wait_ge(S["s_ready"], 4 * (c_ + 1))
            tok = bass.ds(1 + c_ * CH, CH)
            act.activation(ex[:, 0], c[:, :, tok], ACT.Exp).then_inc(S["exp"], 1)
            act.activation(ex[:, 1], c[:, :, tok], ACT.Exp, scale=-1.0).then_inc(S["exp"], 1)
            act.activation(ex[:, 2], prev[:, :, :], ACT.Exp).then_inc(S["exp"], 1)
            for hf in range(2):
                i, pp = 2 * c_ + hf + 1, slice(2 * hf, 2 * hf + 2)
                act.wait_ge(S["l_taken"], i)
                act.activation(tm[:, pp, 0:3, :].rearrange("p a b n -> p a (b n)"), ps[:, pp, P:512], ACT.Copy)\
                   .then_inc(S["vt_taken"], 1)
            for lev in range(LEVELS - 1):
                for hf in range(2):
                    i, pp = 2 * c_ + hf + 1, slice(2 * hf, 2 * hf + 2)
                    bk = slice(4 + 2 * hf, 6 + 2 * hf)
                    act.wait_ge(S["lev_made"], 12 * c_ + 2 * lev + hf + 1)
                    if lev < LEVELS - 2:
                        act.activation(W[:, pp, 0:2, :].rearrange("p b a n -> p b (a n)"), ps[:, bk, 0:256], ACT.Copy)\
                           .then_inc(S["n_taken"], 1)
                    else:
                        act.activation(W[:, pp, N_, :], ps[:, bk, P:256], ACT.Copy).then_inc(S["n_taken"], 1)
                    if lev == 0:
                        act.activation(tm[:, pp, 3, :], ps[:, bk, 384:512], ACT.Copy).then_inc(S["kkt_taken"], 1)
                        act.wait_ge(S["mv_made"], i)
                        act.activation(MV[:, pp, :], ps[:, pp, 0:P], ACT.Copy).then_inc(S["mv_taken"], 1)
            for hf in range(2):
                pp = slice(2 * hf, 2 * hf + 2)
                act.wait_ge(S["wt_made"], 2 * c_ + hf + 1)
                act.activation(WT[:, pp, :], ps[:, pp, P:2 * P], ACT.Copy).then_inc(S["wt_taken"], 1)

        def dve_common(dve, c_, g):
            tok, before = bass.ds(c_ * CH, CH), bass.ds(c_ * CH, CH)
            dve.wait_ge(S["s_ready"], 4 * (c_ + 1))
            dve.wait_ge(S["o_taken"], 4 * (c_ + 1))
            dve.tensor_tensor(prev[:, :, :], c[:, :, before], keep[:, tok].unsqueeze(1).broadcast_to([P, 4, CH]), ALU.mult)\
               .then_inc(S["prev"], 1)
            dve.wait_ge(S["exp"], 3 * (c_ + 1))
            for hh in range(2):
                h, o = slice(hh * CH, (hh + 1) * CH), slice(hh * CH, (hh + 1) * CH)
                dve.tensor_tensor(KR[h, :, 0, o], kk[h, :, tok], ex[h, 2], ALU.mult).then_inc(S["bd"], 1)
                dve.tensor_tensor(KR[h, :, 1, o], rw[h, 0:4, tok], ex[h, 0], ALU.mult).then_inc(S["bd"], 1)
                dve.tensor_tensor(BK[h, :, 0, o], b[h, :, tok], ex[h, 1], ALU.mult).then_inc(S["bd"], 1)
                dve.tensor_tensor(BK[h, :, 1, o], rw[h, 4:8, tok], ex[h, 1], ALU.mult).then_inc(S["bd"], 1)
                dve.tensor_copy(BK[h, :, 2, o], rw[h, 8:12, tok]).then_inc(S["bd"], 1)
            for hf in range(2):
                i, pp, bk = 2 * c_ + hf + 1, slice(2 * hf, 2 * hf + 2), slice(4 + 2 * hf, 6 + 2 * hf)
                dve.wait_ge(S["a_made"], i)
                for j in range(2):
                    q = slice(2 * j, 2 * j + 2)
                    last = dve.tensor_tensor(
                        A4[:, pp, q, :].rearrange("p b a n -> p b (a n)"), ps[:, bk, 256 * j:256 * (j + 1)],
                        rm[:, g, 1:3, :].rearrange("p a n -> p (a n)").unsqueeze(1).broadcast_to([P, 2, 256]), ALU.mult)
                last.then_inc(S["a_taken"], 1)
                dve.wait_ge(S["vt_made"], i)
                dve.tensor_tensor(W[:, pp, N_, :], ps[:, pp, 0:P], rm[:, g, 0, :].unsqueeze(1).broadcast_to([P, 2, P]),
                                  ALU.mult).then_inc(S["l_taken"], 1)
                dve.wait_ge(S["a_taken"], i)
                dve.scalar_tensor_tensor(W[:, pp, TT_, :], A4[:, pp, 0, :], -1.0,
                                         k.mask("ident").unsqueeze(1).broadcast_to([P, 2, P]), ALU.mult, ALU.add)\
                   .then_inc(S["t_taken"], 1)
            for lev in range(1, LEVELS):
                for hf in range(2):
                    pp, bk = slice(2 * hf, 2 * hf + 2), slice(4 + 2 * hf, 6 + 2 * hf)
                    dve.wait_ge(S["lev_made"], 12 * c_ + 2 * lev + hf + 1)
                    dve.wait_ge(S["t_taken"], 12 * c_ + 2 * (lev - 1) + hf + 1)
                    dve.tensor_tensor(W[:, pp, TT_, :], W[:, pp, TT_, :], ps[:, pp, 0:P], ALU.add)\
                       .then_inc(S["t_taken"], 1)

        with nc.Block() as block:
            @block.sync
            def _(sp):
                sp.dma_start(rm[:, :, :, :].rearrange("p a b n -> p (a b n)"), io["rwmasks"]).then_inc(S["masks"], 16)
                sp.wait_ge(S["s_ready"], 4 * (NCH + 1))
                for j in range(2):
                    h = slice(j * HD, (j + 1) * HD)
                    sp.dma_start(io["o_rwkv_p"].rearrange("(q j) k v -> j k q v", j=2)[j], St[h, :, h]).then_inc(S["out"], 16)
                sp.wait_ge(S["out"], 32)

            @block.gpsimd
            def _(pool):
                pool.memset(KR[:, :, :, :], 0.0).then_inc(S["zero"], 1)
                pool.memset(BK[:, :, :, :], 0.0).then_inc(S["zero"], 1)
                pool.memset(St[:, :, :], 0.0).then_inc(S["zero"], 1)

            @block.tensor
            def _(pe):
                pe.wait_ge(S["zero"], 3)
                with pe.Fori(0, NCH) as c_:
                    pe_common(pe, c_)
                    for hf in range(2):
                        i = 2 * c_ + hf + 1
                        pe.wait_ge(S["mv_taken"], i)
                        pe.wait_ge(S["wt_taken"], i)
                        for p in (2 * hf, 2 * hf + 1):
                            pe.matmul(B[p][:, 256:384], W[:, p, TT_, :], MV[:, p, :], start=True, stop=False)
                            mm = pe.matmul(B[p][:, 256:384], WT[:, p, :], St[:, p, :], start=False, stop=True)
                        mm.then_inc(S["sa_made"], 1)
                    for hf in range(2):
                        i = 2 * c_ + hf + 1
                        pe.wait_ge(S["sa_taken"], i)
                        for p in (2 * hf, 2 * hf + 1):
                            pe.matmul(B[p][:, 0:P], tm[:, p, 0, :], SA[:, p, :], start=True, stop=False)
                            mm = pe.matmul(B[p][:, 0:P], tm[:, p, 1, :], tm[:, p, 2, :], start=False, stop=True)
                            pe.matmul(B[p][:, 384:512], St[:, p, :], KR[:, p, 1, :], start=True, stop=False)
                            pe.matmul(B[p][:, 384:512], SA[:, p, :], A4[:, p, 1, :], start=False, stop=False)
                            mm = pe.matmul(B[p][:, 384:512], tm[:, p, 2, :], A4[:, p, 3, :], start=False, stop=True)
                        mm.then_inc(S["o_made"], 1)

            @block.scalar
            def _(act):
                with act.Fori(0, NCH) as c_:
                    act_common(act, c_)
                    act.wait_ge(S["exp"], 3 * (c_ + 1))
                    for p in range(4):
                        act.activation(S1[:, p, :], St[:, p, :], ACT.Copy, scale=ex[:, 0, p, CH - 1:CH]).then_inc(S["s1"], 1)

            @block.vector
            def _(dve):
                dve.wait_ge(S["masks"], 16)
                dve.wait_ge(S["zero"], 3)
                dve.sem_inc(S["s_ready"], 4)
                dve.sem_inc(S["o_taken"], 4)
                with dve.Fori(0, NCH) as c_:
                    dve_common(dve, c_, 0)
                    for hf in range(2):
                        pp = slice(2 * hf, 2 * hf + 2)
                        dve.wait_ge(S["sa_made"], 2 * c_ + hf + 1)
                        dve.tensor_scalar(SA[:, pp, :], ps[:, pp, 256:384], -1.0, None, ALU.mult).then_inc(S["sa_taken"], 1)
                    dve.wait_ge(S["s1"], 4 * (c_ + 1))
                    for hf in range(2):
                        dve.wait_ge(S["o_made"], 2 * c_ + hf + 1)
                        for p in (2 * hf, 2 * hf + 1):
                            dve.scalar_tensor_tensor(St[:, p, :], B[p][:, 0:P], ex[:, 0, p, CH - 1:CH], S1[:, p, :],
                                                     ALU.mult, ALU.add).then_inc(S["s_ready"], 1)
                        for hh in range(2):
                            h, pp = slice(hh * HD, (hh + 1) * HD), slice(2 * hf, 2 * hf + 2)
                            dve.tensor_copy(c[h, pp, bass.ds(1 + c_ * CH, CH)], ps[h, pp, 384 + hh * CH:384 + (hh + 1) * CH])\
                               .then_inc(S["o_taken"], 1)

        SB = k.sb(ctx, "rc_SB", [P, 2, NB, P])
        EX = k.sb(ctx, "rc_EX", [P, 2, NB, P])
        bm = k.sb(ctx, "rc_bm", [P, NB])
        G = NCH
        with nc.Block() as block:
            @block.sync
            def _(sp):
                sp.dma_start(bm[:, :], io["batchmask"]).then_inc(S["masks"], 16)
                sp.wait_ge(S["sb_zero"], 1)
                for p in range(4):
                    if p >= 2:
                        sp.wait_ge(s_out[p % 2], 32)
                    for j in range(2):
                        h = slice(j * HD, (j + 1) * HD)
                        sp.dma_start(SB[h, p % 2, :, h], io["s0"][:, 2 * p + j].rearrange("b k v -> k b v"))\
                          .then_inc(sb_in[p % 2], 16)

            @block.gpsimd
            def _(pool):
                pool.memset(SB[:, :, :, :], 0.0).then_inc(S["sb_zero"], 1)
                for p in range(4):
                    pool.wait_ge(S["ns_done"], p + 1)
                    for j in range(2):
                        h = slice(j * HD, (j + 1) * HD)
                        pool.dma_start(io["o_rwkv_s"][:, 2 * p + j].rearrange("b k v -> k b v"), SB[h, p % 2, :, h])\
                            .then_inc(s_out[p % 2], 16)
                for j in range(2):
                    pool.wait_ge(s_out[j], 64)

            @block.tensor
            def _(pe):
                pe_common(pe, G)
                for p in range(4):
                    own = (2 * G + p // 2 + 1)
                    pe.wait_ge(S["mv_taken"], own)
                    pe.wait_ge(S["wt_taken"], own)
                    pe.wait_ge(sb_in[p % 2], 32 * (p // 2 + 1))
                    sa = B[p][:, 256:384]
                    sav = sa.rearrange("p (h t) -> p h t", h=2)
                    wt = WT[:, p, :].rearrange("p (h t) -> p h t", h=2)
                    r = KR[:, p, 1, :].rearrange("p (h t) -> p h t", h=2)
                    pe.matmul(sa, MV[:, p, :], W[:, p, TT_, :], start=True, stop=True)
                    for n in range(NB):
                        t = slice(n * TSEQ, (n + 1) * TSEQ)
                        mm = pe.matmul(sav[:, :, t], SB[:, p % 2, n, :], wt[:, :, t], start=False, stop=True,
                                       skip_group_check=True)
                    mm.then_inc(S["ut_made"], 1)
                    pe.wait_ge(S["ut_taken"], p + 1)
                    pe.transpose(B[p][:, P:2 * P], S1[:, p, :], k.mask("ident")).then_inc(S["sx_made"], 1)
                    pe.wait_ge(S["sx_taken"], p + 1)
                    o = B[p][:, 384:512]
                    ov = o.rearrange("p (h t) -> p h t", h=2)
                    pe.matmul(o, SA[:, p, :], A4[:, p, 1, :], start=True, stop=False)
                    pe.matmul(o, tm[:, p, 2, :], A4[:, p, 3, :], start=False, stop=True)
                    for n in range(NB):
                        t = slice(n * TSEQ, (n + 1) * TSEQ)
                        mm = pe.matmul(ov[:, :, t], SB[:, p % 2, n, :], r[:, :, t], start=False, stop=True,
                                       skip_group_check=True)
                    mm.then_inc(S["o_made"], 1)
                    pe.wait_ge(S["ex"], 2 * (p + 1))
                    if p >= 2:
                        pe.wait_ge(S["sum"], p - 1)
                    for n in range(2):
                        o = B[4 + 2 * (p % 2) + n]
                        bt = slice(4 * n, 4 * n + 4)
                        pe.matmul(o, tm[:, p, 0, :], EX[:, 0, bt, :].rearrange("p b v -> p (b v)"), start=True, stop=False)
                        mm = pe.matmul(o, tm[:, p, 1, :], EX[:, 1, bt, :].rearrange("p b v -> p (b v)"), start=False, stop=True)
                    mm.then_inc(S["ns_made"], 1)

            @block.scalar
            def _(act):
                act_common(act, G)
                for p in range(4):
                    act.wait_ge(S["sx_made"], p + 1)
                    act.activation(SA[:, p, :], B[p][:, P:2 * P], ACT.Copy).then_inc(S["sx_taken"], 1)

            @block.vector
            def _(dve):
                dve.wait_ge(S["masks"], 32)
                dve_common(dve, G, 1)
                for p in range(4):
                    dve.wait_ge(S["ut_made"], p + 1)
                    dve.tensor_scalar(S1[:, p, :], B[p][:, 256:384], -1.0, None, ALU.mult).then_inc(S["ut_taken"], 1)
                    dve.wait_ge(S["sx_taken"], p + 1)
                    if p >= 1:
                        dve.wait_ge(S["ns_made"], p)
                    for j, x in enumerate((SA[:, p, :], tm[:, p, 2, :])):
                        dve.tensor_tensor(EX[:, j], x.unsqueeze(1).broadcast_to([P, NB, P]),
                                          bm[:, :].unsqueeze(2).broadcast_to([P, NB, P]), ALU.mult).then_inc(S["ex"], 1)
                    dve.wait_ge(S["o_made"], 2 * NCH + p + 1)
                    for hh in range(2):
                        h = slice(hh * HD, (hh + 1) * HD)
                        dve.tensor_copy(c[h, p, 1 + TP:1 + T], B[p][h, 384 + hh * CH:384 + hh * CH + TS])
                    dve.wait_ge(S["ns_made"], p + 1)
                    sb = SB[:, p % 2]
                    new = ps[:, 4 + 2 * (p % 2):6 + 2 * (p % 2), :].rearrange("p a n -> p (a n)").rearrange("p (b v) -> p b v", b=NB)
                    dve.tensor_tensor(sb, sb, new, ALU.add).then_inc(S["sum"], 1)
                    dve.wait_ge(S["sum"], p + 1)
                    end = ex[:, 0, p, TSEQ - 1:TS:TSEQ]
                    dve.tensor_tensor(sb, sb, end.unsqueeze(2).broadcast_to([P, NB, P]), ALU.mult).then_inc(S["ns_done"], 1)


def rwkv_out_stage(k, y):
    nc, io, rw = k.nc, k.io, k.rw
    B = k.bank
    S = {n: k.sem(f"ro_{n}") for n in ("w", "sig", "gated", "mean", "c_done", "sq", "var", "root", "inv", "rk", "made",
                                       "own", "aff")}
    Y = lambda q, n=None: y[:, q, 1:1 + T] if n is None else y[:, q, 1 + n * C3:1 + (n + 1) * C3]
    G = 4
    with ExitStack() as ctx:
        g2 = k.sb(ctx, "ro_g2", [P, 512])
        sq = k.sb(ctx, "ro_sq", [P, 2, T])
        inv = k.sb(ctx, "ro_inv", [P, T])
        rk = k.sb(ctx, "ro_rk", [P, 2, T])
        t = k.sb(ctx, "ro_t", [P, 2, C3])
        with nc.Block() as block:
            @block.sync
            def _(sp):
                sp.dma_start(g2[:, :], io["rw_g2"]).then_inc(S["w"], 16)

            @block.tensor
            def _(pe):
                for q in range(G):
                    for n in range(3):
                        i = 3 * q + n
                        if i >= 4:
                            pe.wait_ge(S["c_done"], i - 3)
                        pe.matmul(B[i % 4][:, 0:C3], k.mask("headones"), Y(q, n), start=True, stop=True).then_inc(S["mean"], 1)
                for q in range(G):
                    pe.wait_ge(S["sq"], q + 1)
                    for n in range(3):
                        mm = pe.matmul(B[4 + n][32 * q:32 * q + 32, 0:C3], k.mask("pick", 32), third(sq[:, q % 2, :], n),
                                       start=True, stop=True)
                    mm.then_inc(S["var"], 1)
                pe.wait_ge(S["inv"], 3)
                pe.wait_ge(S["w"], 16)
                pe.wait_ge(S["gated"], 1)
                pe.wait_ge(S["c_done"], 3 * G)
                for q in range(G):
                    pe.wait_ge(S["rk"], q + 1)
                    for n in range(3):
                        i = 3 * q + n
                        j = 3 * (i % 2)
                        if i >= 2:
                            pe.wait_ge(S["own"], i - 1)
                        pe.matmul(B[j][:, 0:C3], k.masks[32 * q:32 * q + 32, MK["spread"]:MK["spread"] + P],
                                  third(inv[32 * q:32 * q + 32, :], n), start=True, stop=True)
                        pe.matmul(B[j + 1][:, 0:C3], k.mask("headones"), third(rk[:, q % 2, :], n), start=True, stop=True)
                        pe.matmul(B[j + 2][:, 0:C3], g2[:, q * P:(q + 1) * P], third(rw[:, 13, 0:T], n),
                                  start=True, stop=True).then_inc(S["made"], 1)

            @block.scalar
            def _(act):
                act.activation(rw[:, 13, 0:T], rw[:, 13, 0:T], ACT.Tanh, scale=0.5).then_inc(S["sig"], 1)
                for q in range(G):
                    act.wait_ge(S["c_done"], 3 * (q + 1))
                    if q >= 2:
                        act.wait_ge(S["var"], q - 1)
                    act.activation(sq[:, q % 2, :], Y(q), ACT.Square).then_inc(S["sq"], 1)
                act.wait_ge(S["var"], G)
                for n in range(3):
                    act.activation(third(inv, n), B[4 + n][:, 0:C3], ACT.Sqrt, bias=k.mask("lnx_eps", 1), scale=1.0 / HD)\
                       .then_inc(S["root"], 1)

            @block.vector
            def _(dve):
                dve.wait_ge(S["sig"], 1)
                dve.tensor_scalar(rw[:, 13, 0:T], rw[:, 13, 0:T], 0.5, 0.5, ALU.mult, ALU.add).then_inc(S["gated"], 1)

                def bonus(q):
                    if q >= 2:
                        dve.wait_ge(S["made"], 3 * (q - 1))
                    dve.scalar_tensor_tensor(rk[:, q % 2, :], rw[:, q, 0:T], k.vec("rw_r_k", q), rw[:, 4 + q, 0:T],
                                             ALU.mult, ALU.mult).then_inc(S["rk"], 1)
                for q in range(G):
                    for n in range(3):
                        i = 3 * q + n
                        dve.wait_ge(S["mean"], i + 1)
                        dve.scalar_tensor_tensor(Y(q, n), B[i % 4][:, 0:C3], -1.0 / HD, Y(q, n), ALU.mult, ALU.add)\
                           .then_inc(S["c_done"], 1)
                bonus(0)
                bonus(1)
                for n in range(3):
                    dve.wait_ge(S["root"], n + 1)
                    dve.reciprocal(third(inv, n), third(inv, n)).then_inc(S["inv"], 1)
                step = Chain(dve, S["aff"])
                for q in range(G):
                    if q >= 2:
                        bonus(q)
                    for n in range(3):
                        i = 3 * q + n
                        j = 3 * (i % 2)
                        dve.wait_ge(S["made"], i + 1)
                        u, v = t[:, 0, :], third(rw[:, 8 + q, 0:T], n)
                        step(dve.tensor_tensor(Y(q, n), Y(q, n), B[j][:, 0:C3], ALU.mult))
                        dve.tensor_tensor(u, v, B[j + 1][:, 0:C3], ALU.mult)
                        step(dve.tensor_scalar(Y(q, n), Y(q, n), k.vec("rw_lnx_g", q), k.vec("rw_lnx_b", q), ALU.mult, ALU.add))
                        step(dve.tensor_tensor(Y(q, n), Y(q, n), u, ALU.add))
                        dve.tensor_tensor(Y(q, n), Y(q, n), B[j + 2][:, 0:C3], ALU.mult).then_inc(S["own"], 1)


def residual(k):
    def ep(eng, m, j, n, ps):
        xs = k.x[:, bass.ds(m, 1), n * C3:(n + 1) * C3].rearrange("p a t -> p (a t)")
        return eng.tensor_tensor(xs, xs, ps, ALU.add)
    return ep


def memory_kv_stage(k, kmT, vm):
    nc, io = k.nc, k.io
    S = {n: k.sem(f"mk_{n}") for n in ("in", "w", "v_made", "v_taken", "out")}
    with ExitStack() as ctx:
        mem = k.sb(ctx, "mk_mem", [P, DK, NM])
        wv = k.sb(ctx, "mk_wv", [P, DK, D])
        with nc.Block() as block:
            @block.sync
            def _(sp):
                sp.dma_start(mem[:, :, :], io["memT"].rearrange("(k p) m -> p k m", p=P)).then_inc(S["in"], 16)
                sp.dma_start(wv[:, :, :], io["w_mv"].rearrange("(k p) m -> p k m", p=P)).then_inc(S["w"], 16)
                sp.wait_ge(S["in"], 16)
        rms_stage(k, "nmem", mem, DK, "g_mem_kv", mem, D, T_=NM, cols=(NM, 1))

        def ep(eng, m, j, n, ps):
            return eng.activation(kmT[:, bass.ds(m, 1), :], ps, ACT.Copy)
        linear_stage(k, "mk", io["w_mk"], DK, DK, lambda kk, n: mem[:, kk, :], ep, engine="scalar", cols=(NM, 1))
        with nc.Block() as block:
            @block.tensor
            def _(pe):
                pe.wait_ge(S["w"], 16)
                for mt in range(2):
                    for n in range(2):
                        for kk in range(DK):
                            mm = pe.matmul(k.bank[2 * mt + n], mem[:, kk, mt * P:(mt + 1) * P], wv[:, kk, n * 512:(n + 1) * 512],
                                           start=(kk == 0), stop=(kk == DK - 1))
                        mm.then_inc(S["v_made"], 1)

            @block.scalar
            def _(act):
                for mt in range(2):
                    for n in range(2):
                        act.wait_ge(S["v_made"], 2 * mt + n + 1)
                        act.activation(vm[:, mt, n * 512:(n + 1) * 512], k.bank[2 * mt + n], ACT.Copy).then_inc(S["v_taken"], 1)

            @block.sync
            def _(sp):
                sp.dma_start(io["o_memk"].rearrange("(k p) m -> p k m", p=P), kmT[:, :, :]).then_inc(S["out"], 16)
                sp.wait_ge(S["v_taken"], 4)
                sp.dma_start(io["o_memv"].rearrange("(a p) d -> p a d", p=P), vm[:, :, :]).then_inc(S["out"], 16)
                sp.wait_ge(S["out"], 32)


def memory_attention_stage(k, q, kmT, vm, o):
    nc, io = k.nc, k.io
    B = k.bank
    names = ("q_there", "s_made", "maxed", "m_ready", "e_done", "r_done", "p_scaled", "t_made", "t_taken", "o_made", "o_taken")
    S = {n: k.sem(f"ma_{n}") for n in names}
    with ExitStack() as ctx:
        qt = k.sb(ctx, "ma_q", [P, DK, P])
        pr = k.sb(ctx, "ma_p", [P, MH, NM])
        pT = k.sb(ctx, "ma_pT", [P, MH, 2, P])
        st = k.sb(ctx, "ma_st", [P, 4, MH])
        with nc.Block() as block:
            @block.tensor
            def _(pe):
                with pe.Fori(0, TILES) as i:
                    pe.wait_ge(S["q_there"], i + 1)
                    for h in range(MH):
                        for dk in range(2):
                            mm = pe.matmul(B[h // 2][:, h % 2 * NM:(h % 2 + 1) * NM], qt[:, 2 * h + dk, :], kmT[:, 2 * h + dk, :],
                                           start=(dk == 0), stop=(dk == 1))
                    mm.then_inc(S["s_made"], 1)
                    pe.wait_ge(S["p_scaled"], i + 1)
                    for h in range(MH):
                        for mt in range(2):
                            mm = pe.transpose(B[2 + h // 2][:, (h % 2 * 2 + mt) * P:(h % 2 * 2 + mt + 1) * P],
                                              pr[:, h, mt * P:(mt + 1) * P], k.mask("ident"))
                    mm.then_inc(S["t_made"], 1)
                    pe.wait_ge(S["t_taken"], i + 1)
                    pe.wait_ge(S["o_taken"], i + 1)
                    for h in range(MH):
                        for dk in range(2):
                            c = 2 * h + dk
                            for mt in range(2):
                                mm = pe.matmul(B[4 + c // 4][:, c % 4 * P:(c % 4 + 1) * P], vm[:, mt, c * P:(c + 1) * P],
                                               pT[:, h, mt, :], start=(mt == 0), stop=(mt == 1))
                    mm.then_inc(S["o_made"], 1)

            @block.scalar
            def _(act):
                with act.Fori(0, TILES) as i:
                    act.activation(qt[:, :, :], q[:, :, bass.ds(i * P, P)], ACT.Copy).then_inc(S["q_there"], 1)
                    act.wait_ge(S["m_ready"], i + 1)
                    for h in range(MH):
                        act.activation(pr[:, h, :], B[h // 2][:, h % 2 * NM:(h % 2 + 1) * NM], ACT.Exp, bias=st[:, 1, h:h + 1],
                                       scale=MSCALE, accum_out=st[:, 2, h:h + 1]).then_inc(S["e_done"], 1)
                    act.wait_ge(S["t_made"], i + 1)
                    act.activation(pT[:, :, :, :].rearrange("p h a n -> p (h a n)"), k.psum[:, 1024:2048], ACT.Copy)\
                       .then_inc(S["t_taken"], 1)

            @block.vector
            def _(dve):
                dve.sem_inc(S["o_taken"], 1)
                with dve.Fori(0, TILES) as i:
                    dve.wait_ge(S["s_made"], i + 1)
                    dve.reduce_max(st[:, 0, :], k.psum[:, 0:1024].rearrange("p (h n) -> p h n", h=MH), AX).then_inc(S["maxed"], 1)
                    dve.wait_ge(S["maxed"], i + 1)
                    dve.tensor_scalar(st[:, 1, :], st[:, 0, :], -MSCALE, None, ALU.mult).then_inc(S["m_ready"], 1)
                    dve.wait_ge(S["e_done"], MH * (i + 1))
                    dve.reciprocal(st[:, 3, :], st[:, 2, :]).then_inc(S["r_done"], 1)
                    dve.wait_ge(S["r_done"], i + 1)
                    dve.tensor_tensor(pr[:, :, :], pr[:, :, :], st[:, 3, :].unsqueeze(2).broadcast_to([P, MH, NM]), ALU.mult)\
                       .then_inc(S["p_scaled"], 1)
                    dve.wait_ge(S["o_made"], i + 1)
                    dve.tensor_copy(o[:, :, bass.ds(i * P, P)], k.psum[:, 2048:3072].rearrange("p (c n) -> p c n", c=DK))\
                       .then_inc(S["o_taken"], 1)
    Z = {n: k.sem(f"mz_{n}") for n in names}
    kv_in = [k.sem(f"mz_kv{j}") for j in range(2)]
    with ExitStack() as ctx:
        ks = k.sb(ctx, "mz_k", [P, 2, DK, NM])
        vs = k.sb(ctx, "mz_v", [P, 2, 2, D])
        pr = k.sb(ctx, "mz_p", [P, NM])
        pT = k.sb(ctx, "mz_pT", [P, 2, P])
        st = k.sb(ctx, "mz_st", [P, 4])
        with nc.Block() as block:
            @block.sync
            def _(sp):
                def load(b, j):
                    bb = bass.ds(b, 1)
                    sp.dma_start(ks[:, j], io["memk"][bb].rearrange("a (k p) m -> p (a k) m", p=P)).then_inc(kv_in[j], 16)
                    sp.dma_start(vs[:, j], io["memv"][bb].rearrange("a (k p) d -> p (a k) d", p=P)).then_inc(kv_in[j], 16)
                load(0, 0)
                load(1, 1)
                with sp.Fori(1, NB // 2) as it:
                    for j in range(2):
                        sp.wait_ge(Z["o_made"], 2 * it + j - 1)
                        load(2 * it + j, j)

            @block.tensor
            def _(pe):
                with pe.Fori(0, NB // 2) as it:
                    for j in range(2):
                        b = 2 * it + j
                        pe.wait_ge(kv_in[j], 32 * (it + 1))
                        for h in range(MH):
                            for dk in range(2):
                                mm = pe.matmul(B[0][32 * h:32 * h + 32, 0:NM], q[:, 2 * h + dk, TP:T], ks[:, j, 2 * h + dk, :],
                                               start=(dk == 0), stop=(dk == 1))
                        mm.then_inc(Z["s_made"], 1)
                        pe.wait_ge(Z["p_scaled"], b + 1)
                        for mt in range(2):
                            mm = pe.transpose(B[1][:, mt * P:(mt + 1) * P], pr[:, mt * P:(mt + 1) * P], k.mask("ident"))
                        mm.then_inc(Z["t_made"], 1)
                        pe.wait_ge(Z["t_taken"], b + 1)
                        for c in range(DK):
                            for mt in range(2):
                                mm = pe.matmul(B[2][:, c * TSEQ:(c + 1) * TSEQ], vs[:, j, mt, c * P:(c + 1) * P],
                                               pT[:, mt, bass.ds(c // 2 * TS + b * TSEQ, TSEQ)], start=(mt == 0), stop=(mt == 1))
                        mm.then_inc(Z["o_made"], 1)
                        pe.wait_ge(Z["o_taken"], b + 1)

            @block.scalar
            def _(act):
                with act.Fori(0, NB) as b:
                    act.wait_ge(Z["m_ready"], b + 1)
                    act.activation(pr[:, :], B[0][:, 0:NM], ACT.Exp, bias=st[:, 1:2], scale=MSCALE, accum_out=st[:, 2:3])\
                       .then_inc(Z["e_done"], 1)
                    act.wait_ge(Z["t_made"], b + 1)
                    act.activation(pT[:, :, :].rearrange("p a n -> p (a n)"), B[1][:, 0:2 * P], ACT.Copy).then_inc(Z["t_taken"], 1)

            @block.vector
            def _(dve):
                with dve.Fori(0, NB) as b:
                    dve.wait_ge(Z["s_made"], b + 1)
                    dve.reduce_max(st[:, 0:1], B[0][:, 0:NM], AX).then_inc(Z["maxed"], 1)
                    dve.wait_ge(Z["maxed"], b + 1)
                    dve.tensor_scalar(st[:, 1:2], st[:, 0:1], -MSCALE, None, ALU.mult).then_inc(Z["m_ready"], 1)
                    dve.wait_ge(Z["e_done"], b + 1)
                    dve.reciprocal(st[:, 3:4], st[:, 2:3]).then_inc(Z["r_done"], 1)
                    dve.wait_ge(Z["r_done"], b + 1)
                    dve.tensor_scalar(pr[:, :], pr[:, :], st[:, 3:4], None, ALU.mult).then_inc(Z["p_scaled"], 1)
                    dve.wait_ge(Z["o_made"], b + 1)
                    dve.tensor_copy(o[:, :, bass.ds(TP + b * TSEQ, TSEQ)],
                                    B[2][:, 0:DK * TSEQ].rearrange("p (c n) -> p c n", c=DK)).then_inc(Z["o_taken"], 1)


def ffn_up_stage(k, h, hid):
    nc, io = k.nc, k.io
    B = k.bank
    UP, US = 2 + TP, 2 + TSEQ
    U = UP + NB * US
    CV = U - 2
    S = {n: k.sem(f"fu_{n}") for n in ("in", "zero", "made", "taken", "u_there", "past", "u_free", "c_first", "c_mid", "c_done",
                                       "cap", "tanh", "g_done", "hid", "out")}
    w_in = [k.sem(f"fu_w{j}") for j in range(2)]
    wv = io["w_up"].rearrange("(k p) m -> p k m", p=P)
    with ExitStack() as ctx:
        slot = k.sb(ctx, "fu_slot", [P, 2, DK, P])
        u = k.sb(ctx, "fu_u", [P, 2, U])
        cv_ = k.sb(ctx, "fu_c", [P, 2, U])
        th_ = k.sb(ctx, "fu_t", [P, U])
        cv, th = cv_[:, :, 0:CV], th_[:, 0:CV]
        past = k.sb(ctx, "fu_past", [P, F2K, NB, 2])
        cap = k.sb(ctx, "fu_cap", [P, F2K, 1 + NB, 2])
        seg = lambda ap, lo: ap[:, UP:U].rearrange("p (b n) -> p b n", b=NB)[:, :, lo:lo + TSEQ]
        with nc.Block() as block:
            @block.sync
            def _(sp):
                def load(i, j):
                    sp.dma_start(slot[:, j], wv[:, :, bass.ds((i + FK * j) * P, P)]).then_inc(w_in[j], 16)
                load(0, 0)
                load(0, 1)
                sp.dma_start(past[:, :, :, :], io["conv0"]).then_inc(S["in"], 16)
                with sp.Fori(1, FK) as i:
                    for j in range(2):
                        sp.wait_ge(S["made"], 3 * (2 * i + j - 1))
                        load(i, j)
                sp.wait_ge(S["cap"], F2K + 1)
                sp.dma_start(io["o_conv"], cap[:, :, :, :].rearrange("p m s j -> p m (s j)")).then_inc(S["out"], 16)
                sp.wait_ge(S["out"], 16)

            @block.tensor
            def _(pe):
                with pe.Fori(0, FK) as i:
                    for j in range(2):
                        pe.wait_ge(w_in[j], 16 * (i + 1))
                        pe.wait_ge(S["taken"], 2 * i + j + 1)
                        for n in range(3):
                            for kk in range(DK):
                                mm = pe.matmul(B[3 * j + n][:, 0:C3], slot[:, j, kk, :], third(h[:, kk, :], n),
                                               start=(kk == 0), stop=(kk == DK - 1))
                            mm.then_inc(S["made"], 1)

            @block.scalar
            def _(act):
                act.sem_inc(S["taken"], 2)
                act.wait_ge(S["in"], 16)
                act.wait_ge(S["zero"], 1)
                with act.Fori(0, FK) as i:
                    for j in range(2):
                        m = 2 * i + j
                        act.wait_ge(S["u_free"], m + 1)
                        act.wait_ge(S["cap"], m + 1)
                        act.activation(u[:, j, UP:U].rearrange("p (b n) -> p b n", b=NB)[:, :, 0:2],
                                       past[:, bass.ds(i + FK * j, 1), :, :].rearrange("p a b n -> p (a b) n"), ACT.Copy)\
                           .then_inc(S["past"], 1)
                        for n in range(3):
                            act.wait_ge(S["made"], 3 * m + n + 1)
                            if n < 2:
                                act.activation(u[:, j, 2 + n * C3:2 + (n + 1) * C3], B[3 * j + n][:, 0:C3], ACT.Copy)
                                continue
                            w = TP - 2 * C3
                            act.activation(u[:, j, 2 + 2 * C3:UP], B[3 * j + 2][:, 0:w], ACT.Copy)
                            act.activation(seg(u[:, j, :], 2), B[3 * j + 2][:, w:C3].rearrange("p (b n) -> p b n", b=NB), ACT.Copy)\
                               .then_inc(S["taken"], 1)
                        act.wait_ge(S["past"], m + 1)
                        act.wait_ge(S["taken"], m + 3)
                        act.wait_ge(S["hid"], 2 * (i + 1))
                        b0 = VEC["conv_b"] + i + FK * j
                        w2 = VEC["conv_w"] + 2 * F2K + i + FK * j
                        act.activation(cv[:, j, :], u[:, j, 2:U], ACT.Identity, bias=k.vecs[:, bass.ds(b0, 1)],
                                       scale=k.vecs[:, bass.ds(w2, 1)]).then_inc(S["c_first"], 1)
                    act.wait_ge(S["c_done"], 2 * i + 1)
                    act.activation(th[:, :], cv[:, 0, :], ACT.Tanh, scale=0.5).then_inc(S["tanh"], 1)

            @block.vector
            def _(dve):
                dve.sem_inc(S["u_free"], 2)
                dve.sem_inc(S["cap"], 1)
                dve.sem_inc(S["hid"], 2)
                dve.memset(u[:, :, 0:2], 0.0).then_inc(S["zero"], 1)
                with dve.Fori(0, FK) as i:
                    for j in range(2):
                        m = 2 * i + j
                        dve.wait_ge(S["c_first"], m + 1)
                        dst = cap[:, bass.ds(i + FK * j, 1), :, :].rearrange("p a s j -> p (a s) j")
                        dve.tensor_copy(dst[:, 0:1, :], u[:, j, UP - 2:UP].unsqueeze(1))
                        dve.tensor_copy(dst[:, 1:, :], u[:, j, UP:U].rearrange("p (b n) -> p b n", b=NB)[:, :, US - 2:US])\
                           .then_inc(S["cap"], 1)
                        tap = lambda n: k.vecs[:, bass.ds(VEC["conv_w"] + n * F2K + i + FK * j, 1)]
                        dve.scalar_tensor_tensor(cv[:, j, :], u[:, j, 1:U - 1], tap(1), cv[:, j, :], ALU.mult, ALU.add)\
                           .then_inc(S["c_mid"], 1)
                        dve.wait_ge(S["c_mid"], m + 1)
                        dve.scalar_tensor_tensor(cv[:, j, :], u[:, j, 0:U - 2], tap(0), cv[:, j, :], ALU.mult, ALU.add)\
                           .then_inc(S["c_done"], 1)
                        dve.wait_ge(S["c_done"], m + 1)
                        dve.sem_inc(S["u_free"], 1)
                    dve.wait_ge(S["tanh"], i + 1)
                    dve.scalar_tensor_tensor(th[:, :], th[:, :], 1.0, cv[:, 0, :], ALU.add, ALU.mult).then_inc(S["g_done"], 1)
                    dve.wait_ge(S["g_done"], i + 1)
                    hm = hid[:, bass.ds(i, 1), :].rearrange("p a t -> p (a t)")
                    dve.scalar_tensor_tensor(hm[:, 0:TP], th[:, 0:TP], 0.5, cv[:, 1, 0:TP], ALU.mult, ALU.mult)\
                       .then_inc(S["hid"], 1)
                    dve.scalar_tensor_tensor(hm[:, TP:T].rearrange("p (b n) -> p b n", b=NB), seg(th_[:, :], 0), 0.5,
                                             seg(cv_[:, 1, :], 0), ALU.mult, ALU.mult).then_inc(S["hid"], 1)


def store_stage(k, y):
    s = k.sem("y_out")
    with k.nc.Block() as block:
        @block.sync
        def _(sp):
            sp.dma_start(k.io["o_y"].rearrange("(k p) t -> p k t", p=P), y).then_inc(s, 16)
            sp.wait_ge(s, 16)


def program(nc, io):
    with ExitStack() as ctx:
        k = K(nc, ctx, io)
        k.masks = k.sb(ctx, "masks", [P, NMK])
        k.vecs = k.sb(ctx, "vecs", [P, NVEC])
        mix = k.sb(ctx, "mix", [P, 4 * (1 + TR) + 4 * T])
        k.y = mix[:, 0:4 * (1 + TR)].rearrange("p (k t) -> p k t", k=4)
        k.mla = mix[:, 4 * (1 + TR):].rearrange("p (k t) -> p k t", k=4)
        load_stage(k)
        with ExitStack() as rctx:
            k.rw = k.sb(rctx, "rw", [P, RWK, TR])
            with ExitStack() as mctx:
                k.cqkv = k.sb(mctx, "cqkv", [P, QK + KK, T])
                k.krope = k.sb(mctx, "krope", [P, T])
                qabs = k.sb(mctx, "qabs", [P, KK, NB, NH, TSEQ])
                qrope = k.sb(mctx, "qrope", [ROPE, NB, NH, TSEQ])
                with ExitStack() as tctx:
                    k.rot = k.sb(tctx, "rot", [P, 2, T])
                    s_rot = k.sem("s_rot")
                    with nc.Block() as block:
                        @block.sync
                        def _(sp):
                            sp.dma_start(k.rot[:, :, :].rearrange("p a t -> p (a t)"), io["rot"]).then_inc(s_rot, 16)
                            sp.wait_ge(s_rot, 16)
                    with ExitStack() as hctx:
                        h = k.sb(hctx, "h", [P, DK, T])
                        load_x(k, h, "s_x0")
                        rms_stage(k, "nmix", h, DK, "g_mix", h, D)
                        proj_stage(k, h)
                    latent_stage(k)
                    mla_prompt_stage(k, qabs, qrope)
                mla_sample_stage(k, qabs, qrope)
                k.debug("mla", k.mla[:, :, :])
            k.recycle()
            a = k.sb(rctx, "rw_a", [P, 4, TR])
            kk = k.sb(rctx, "rw_kk", [P, 4, TR])
            keep = k.sb(rctx, "rw_keep", [P, TR])
            rwkv_prep_stage(k, k.y, a, kk, keep)
            rwkv_chunk_stage(k, k.y, a, kk, keep)
            k.recycle()
            rwkv_out_stage(k, k.y)
            k.debug("rw", k.y[:, :, 1:1 + T])
        k.x = k.sb(ctx, "x", [P, DK, T])
        load_x(k, k.x, "s_x1")
        rms_stage(k, "nmla", k.mla, 4, "g_mla_out", k.mla, 512)
        both = lambda kk, n: k.y[:, kk, 1 + n * C3:1 + (n + 1) * C3] if kk < 4 else third(k.mla[:, kk - 4, :], n)
        linear_stage(k, "wo", io["w_o"], DK, DK, both, residual(k))
        k.debug("x1", k.x[:, :, :])
        k.recycle()
        h = mix[:, 0:DK * T].rearrange("p (k t) -> p k t", k=DK)
        of_h = lambda kk, n: third(h[:, kk, :], n)
        with ExitStack() as actx:
            kmT = k.sb(actx, "kmT", [P, DK, NM])
            vm = k.sb(actx, "vm", [P, 2, D])
            memory_kv_stage(k, kmT, vm)
            rms_stage(k, "nmq", k.x, DK, "g_mem_q", h, D)
            q = k.sb(actx, "q", [P, DK, T])

            def to_q(eng, m, j, n, ps):
                return eng.activation(q[:, bass.ds(m, 1), n * C3:(n + 1) * C3], ps, ACT.Copy)
            linear_stage(k, "mq", io["w_mq"], DK, DK, of_h, to_q, engine="scalar")
            memory_attention_stage(k, q, kmT, vm, h)
        linear_stage(k, "mo", io["w_mo"], DK, DK, of_h, residual(k))
        k.debug("x2", k.x[:, :, :])
        k.recycle()
        rms_stage(k, "nffn", k.x, DK, "g_ffn", h, D)
        with ExitStack() as fctx:
            hid = k.sb(fctx, "hid", [P, FK, T])
            ffn_up_stage(k, h, hid)
            linear_stage(k, "wd", io["w_down"], FK, DK, lambda kk, n: third(hid[:, kk, :], n), residual(k))
        rms_stage(k, "nfin", k.x, DK, "g_final", h, D)
        store_stage(k, h)


OUTS = {
    "o_y": (D, T), "o_lat": (KVL, T), "o_krope": (ROPE, T),
    "o_memk": (D, NM), "o_memv": (NM, D),
    "o_rwkv_p": (NH, HD, HD), "o_rwkv_s": (NB, NH, HD, HD),
    "o_shift": (P, RWK, 1 + NB), "o_conv": (P, F2K, 2 * (1 + NB)),
}


DEBUG = {}


def build(nc, arrays):
    io = {}
    for name, a in arrays.items():
        io[name] = nc.dram_tensor(f"in_{name}", a.shape, mybir.dt.from_np(a.dtype), kind="ExternalInput").ap()
    for name, shape in OUTS.items():
        io[name] = nc.dram_tensor(name, shape, F32, kind="ExternalOutput").ap()
    for name, shape in DEBUG.items():
        io["dbg_" + name] = nc.dram_tensor("dbg_" + name, shape, F32, kind="ExternalOutput").ap()
    program(nc, io)


def kernel(**inputs):
    import numpy as _np
    import concourse.bacc as _bacc
    from concourse.bass_utils import run_bass_kernel_spmd as _run

    x = {n: _np.asarray(a) for n, a in inputs.items()}
    tile = lambda a: _np.ascontiguousarray(a)
    m, rw, rot, keep, batch = tables()
    arrays = {"masks": m, "rwmasks": rw, "rot": rot, "keep": keep, "batchmask": batch}
    arrays["vecs"] = tile(_np.concatenate([x[n].reshape(-1, P) for n in VEC]).T)
    arrays["xp"] = tile(x["x_prompt"][0].T)
    arrays["xs"] = tile(x["x_sample"].reshape(TS, D).T)
    arrays["memT"] = tile(x["mem_prompt"][0].T)
    arrays["lat"] = x["cache_mla_latent"][0]
    arrays["kr"] = x["cache_mla_krope"][0]
    arrays["pages"] = x["page_table"].reshape(1, -1)
    arrays["memk"] = tile(x["cache_mem_k"][0].reshape(NB, NM, D).transpose(0, 2, 1))
    arrays["memv"] = x["cache_mem_v"][0].reshape(NB, NM, D)
    arrays["s0"] = tile(x["state_rwkv"][0].transpose(0, 1, 3, 2))
    arrays["shift0"] = tile(x["state_rwkv_shift"][0].reshape(NB, RWK, P).transpose(2, 1, 0))
    arrays["conv0"] = tile(x["state_ffn_conv"][0].reshape(NB, 2, F2K, P).transpose(3, 2, 0, 1))
    for n in ("w_in", "w_uq", "w_ukv", "rw_w2", "rw_a2", "rw_g2", "w_o", "w_mq", "w_mk", "w_mv", "w_mo", "w_up", "w_down"):
        arrays[n] = x[n][0]
    nc = _bacc.Bacc("TRN2", target_bir_lowering=False, num_devices=1)
    build(nc, arrays)
    r = _run(nc, [{f"in_{n}": a for n, a in arrays.items()}], core_ids=[0]).results[0]
    T_ = lambda a: tile(a.T)
    y, lat, kr = T_(r["o_y"]), T_(r["o_lat"]), T_(r["o_krope"])
    sh = r["o_shift"].transpose(2, 1, 0).reshape(1 + NB, RWP)
    cv = r["o_conv"].transpose(2, 1, 0).reshape(1 + NB, 2, 2 * FF)
    st = lambda a, n: tile(a.reshape(n, NH, HD, HD).transpose(0, 1, 3, 2))[None]
    return (y[None, :TP], y[TP:].reshape(NB, TSEQ, D),
            lat[None, None, :TP], kr[None, None, :TP],
            T_(r["o_memk"]).reshape(1, 1, NM, MH, MD), r["o_memv"].reshape(1, 1, NM, MH, MD),
            st(r["o_rwkv_p"], 1), sh[None, :1], cv[None, :1],
            lat[TP:].reshape(1, NB, TSEQ, KVL), kr[TP:].reshape(1, NB, TSEQ, ROPE),
            st(r["o_rwkv_s"], NB), sh[None, 1:], cv[None, 1:])
```

```python
from contextlib import ExitStack

import numpy as np

import concourse.bass as bass
from concourse import mybir

F32 = mybir.dt.float32
FR = mybir.dt.float32r
I32 = mybir.dt.int32
ALU = mybir.AluOpType
ACT = mybir.ActivationFunctionType
AX = mybir.AxisListType.X

P = 128
D = 1024
TP, NB, TSEQ = 1024, 8, 4
TS = NB * TSEQ
T = TP + TS
C3 = T // 3
DK = D // P
NH, HD = 8, 64
NOPE, ROPE = 64, 32
QL, KVL = 384, 256
QK, KK = QL // P, KVL // P
MLA_PROJ = QL + KVL + ROPE
RWP = 3 * 512 + 64 + 64 + 128
RWK = RWP // P
CH = 64
NCH = TP // CH
TR = TP + CH
PAST, PAGE = 2048, 128
NPG = PAST // PAGE
NM, MH, MD = 256, 4, 256
FF = 2816
FK = FF // P
F2K = 2 * FK
EPS = 1e-6
LNX_EPS = 64e-5
SCALE = (NOPE + ROPE) ** -0.5
MSCALE = MD ** -0.5
NEG = -1e30

VEC = {}
_n = 0
for _name, _w in (("g_mix", 8), ("q_norm_g", 3), ("kv_norm_g", 2), ("g_mla_out", 4), ("rw_mu", 14), ("rw_w0", 4),
                  ("rw_a0", 4), ("rw_k_k", 4), ("rw_k_a", 4), ("rw_r_k", 4), ("rw_lnx_g", 4), ("rw_lnx_b", 4),
                  ("g_mem_q", 8), ("g_mem_kv", 8), ("g_ffn", 8), ("g_final", 8), ("conv_b", 44), ("conv_w", 132)):
    VEC[_name] = _n
    _n += _w
NVEC = _n

MK = {}
_n = 0
for _name, _w in (("ident", P), ("headones", P), ("ones", P), ("causal", P), ("new_causal", TSEQ * NB), ("pick", 32), ("spread", P), ("eps", 1),
                  ("lnx_eps", 1)):
    MK[_name] = _n
    _n += _w
NMK = _n
RWM = 3 * P
Y_WORDS = (4 * (1 + TR) + 7) // 8 * 8


def tables():
    t = np.arange(P) % CH
    head = np.arange(P) // CH
    same = head[:, None] == head[None, :]
    m = np.zeros((P, NMK), np.float32)
    m[:, MK["ident"]:MK["ident"] + P] = np.eye(P)
    m[:, MK["headones"]:MK["headones"] + P] = same
    m[:, MK["ones"]:MK["ones"] + P] = 1
    q = np.arange(P)
    m[:, MK["causal"]:MK["causal"] + P] = np.where(q[None, :] <= q[:, None], 0, NEG)
    r = np.arange(NH * TSEQ) % TSEQ
    for b in range(NB):
        m[:NH * TSEQ, MK["new_causal"] + b * TSEQ:MK["new_causal"] + (b + 1) * TSEQ] = np.where(
            np.arange(TSEQ)[None, :] <= r[:, None], 0, NEG)
    m[:, MK["pick"]], m[:, MK["pick"] + 1] = head == 0, head == 1
    m[0::32, MK["spread"]:MK["spread"] + P] = head == 0
    m[1::32, MK["spread"]:MK["spread"] + P] = head == 1
    m[:, MK["eps"]] = EPS
    m[:, MK["lnx_eps"]] = LNX_EPS
    rw = np.zeros((P, 2 * RWM), np.float32)
    for g in range(2):
        ok = same if g == 0 else same & (t[:, None] // TSEQ == t[None, :] // TSEQ) & (t[:, None] < TS) & (t[None, :] < TS)
        rw[:, g * RWM:g * RWM + P] = ok & (t[None, :] < t[:, None])
        rw[:, g * RWM + P:g * RWM + 2 * P] = ok & (t[None, :] > t[:, None])
        rw[:, g * RWM + 2 * P:g * RWM + 3 * P] = ok & (t[None, :] >= t[:, None])
    pos = np.concatenate([np.arange(TP), np.tile(PAST + np.arange(TSEQ), NB)]).astype(np.float32)
    half = ROPE // 2
    inv = (np.float32(1) / (np.float32(10000.0) ** (np.arange(half, dtype=np.float32) / np.float32(half)))).astype(np.float32)
    ang = (inv[:, None] * pos[None, :]).astype(np.float32)
    rot = np.zeros((P, 2, T), np.float32)
    for base in (0, 32, 64, 96):
        rot[base:base + half, 0] = rot[base + half:base + ROPE, 0] = np.cos(ang)
        rot[base:base + half, 1] = -np.sin(ang)
        rot[base + half:base + ROPE, 1] = np.sin(ang)
    keep = np.ones((P, TR), np.float32)
    keep[:, 0:TP:CH] = 0
    keep[:, TP:TR:TSEQ] = 0
    batch = ((t[:, None] // TSEQ == np.arange(NB)[None, :]) & (t[:, None] < TS)).astype(np.float32)
    return m, rw, rot.reshape(P, 2 * T), keep, batch


class Chain:

    def __init__(self, eng, sem, base=0):
        self.eng, self.sem, self.n, self.base = eng, sem, 0, base

    def __call__(self, ins):
        ins.then_inc(self.sem, 1)
        self.n += 1
        self.eng.wait_ge(self.sem, self.base + self.n)


class K:

    def __init__(self, nc, ctx, io):
        self.nc, self.ctx, self.io = nc, ctx, io
        self.sems = []
        self.psum = ctx.enter_context(nc.psum_tensor("psum", [P, 8 * 512], F32))
        self.bank = [self.psum[:, i * 512:(i + 1) * 512] for i in range(8)]

    def sb(self, ctx, name, shape, dt=F32):
        return ctx.enter_context(self.nc.sbuf_tensor(name, shape, dt))

    def at(self, base, name, shape, dt=F32, words=0):
        return self.nc.alloc_sbuf_tensor_at(name, shape, dt, offset=base + 4 * words)

    def sem(self, name):
        self.sems.append(self.nc.alloc_semaphore(name=name))
        return self.sems[-1]

    def recycle(self):
        self.nc.clear_and_free_semaphores(self.sems)
        self.sems = []
        self.nc.all_engine_barrier()

    def debug(self, name, ap):
        d = self.io.get("dbg_" + name)
        if d is not None:
            sem = self.sem("dbg_" + name)
            with self.nc.Block() as block:
                @block.sync
                def _(sp):
                    sp.dma_start(d, ap).then_inc(sem, 16)
                    sp.wait_ge(sem, 16)

    def vec(self, name, k, p0=0, p1=P):
        c = VEC[name] + k
        return self.vecs[p0:p1, c:c + 1]

    def mask(self, name, w=P, rows=P):
        return self.masks[0:rows, MK[name]:MK[name] + w]


def third(ap, n):
    return ap[:, n * C3:(n + 1) * C3]


def rms_stage(k, name, src, nk, gain, dst, eps_d, T_=T, cols=(C3, 3)):
    nc = k.nc
    cw, cn = cols
    sq_done, sum_done, rt_done, rc_done, sq_free = [k.sem(f"{name}_{s}") for s in ("sq", "sum", "rt", "rc", "sqfree")]
    with ExitStack() as ctx:
        sq = k.sb(ctx, f"{name}_sq", [P, 2, T_])
        rt = k.sb(ctx, f"{name}_rt", [P, T_])
        with nc.Block() as block:
            @block.scalar
            def _(act):
                for i in range(nk):
                    if i >= 2:
                        act.wait_ge(sq_free, i - 1)
                    act.activation(sq[:, i % 2, :], src[:, i, :], ACT.Square).then_inc(sq_done, 1)
                act.wait_ge(sum_done, 1)
                for n in range(cn):
                    act.activation(rt[:, n * cw:(n + 1) * cw], k.bank[n][:, 0:cw], ACT.Sqrt, bias=k.mask("eps", 1),
                                   scale=1.0 / eps_d).then_inc(rt_done, 1)

            @block.tensor
            def _(pe):
                for i in range(nk):
                    pe.wait_ge(sq_done, i + 1)
                    for n in range(cn):
                        mm = pe.matmul(k.bank[n][:, 0:cw], k.mask("ones"), sq[:, i % 2, n * cw:(n + 1) * cw],
                                       start=(i == 0), stop=(i == nk - 1))
                    if i < nk - 1:
                        mm.then_inc(sq_free, 1)
                mm.then_inc(sum_done, 1)

            @block.vector
            def _(dve):
                for n in range(cn):
                    dve.wait_ge(rt_done, n + 1)
                    c = slice(n * cw, (n + 1) * cw)
                    dve.reciprocal(rt[:, c], rt[:, c]).then_inc(rc_done, 1)
                    dve.wait_ge(rc_done, n + 1)
                    for i in range(nk):
                        dve.scalar_tensor_tensor(dst[:, i, c], src[:, i, c], k.vec(gain, i), rt[:, c],
                                                 ALU.mult, ALU.mult)


def memory_keys_stage(k, name, w, nk, n_m, rhs, epilogue, engine="vector", cols=(C3, 3), m_of=None, after=None, ahead=2):
    nc = k.nc
    cw, cn = cols
    w_in = [k.sem(f"{name}_w{j}") for j in range(2)]
    made, taken = k.sem(f"{name}_made"), k.sem(f"{name}_taken")
    wv = w.rearrange("(k p) m -> p k m", p=P)
    m_of = m_of or (lambda m: m)
    with ExitStack() as ctx:
        slot = k.sb(ctx, f"{name}_slot", [P, 2, nk, P])
        with nc.Block() as block:
            @block.sync
            def _(sp):
                for j in range(min(2, n_m)):
                    sp.dma_start(slot[:, j], wv[:, :, m_of(j) * P:(m_of(j) + 1) * P]).then_inc(w_in[j], 16)

                def step(m, j):
                    sp.wait_ge(made, cn * (m - 1))
                    sp.dma_start(slot[:, j], wv[:, :, bass.ds(m_of(m) * P, P)]).then_inc(w_in[j], 16)
                if n_m >= 4:
                    with sp.Fori(1, n_m // 2) as i:
                        for j in range(2):
                            step(2 * i + j, j)
                if n_m % 2:
                    step(n_m - 1, 0)

            @block.tensor
            def _(pe):
                def step(i, m, j):
                    pe.wait_ge(w_in[j], 16 * (i + 1))
                    pe.wait_ge(taken, m + 1)
                    for n in range(cn):
                        for kk in range(nk):
                            mm = pe.matmul(k.bank[3 * j + n][:, 0:cw], slot[:, j, kk, :], rhs(kk, n),
                                           start=(kk == 0), stop=(kk == nk - 1))
                        if n < cn - 1:
                            mm.then_inc(made, 1)
                    mm.then_inc(made, 1)
                with pe.Fori(0, n_m // 2) as i:
                    for j in range(2):
                        step(i, 2 * i + j, j)
                if n_m % 2:
                    step(n_m // 2, n_m - 1, 0)

            def take(eng):
                eng.sem_inc(taken, 2)

                def step(m, j):
                    for n in range(cn):
                        eng.wait_ge(made, cn * m + n + 1)
                        last = epilogue(eng, m, j, n, k.bank[3 * j + n][:, 0:cw])
                    last.then_inc(taken, 1)
                with eng.Fori(0, n_m // 2) as i:
                    for j in range(2):
                        step(2 * i + j, j)
                if n_m % 2:
                    step(n_m - 1, 0)
                if after:
                    after(eng)
            if engine == "vector":
                block.vector(take)
            else:
                block.scalar(take)


class Norm:

    def __init__(self, k, name, src, gain, H, L, full, sq, acc, plain=(), src_wait=None, bank=5):
        self.bank = k.bank[bank:bank + 3]
        self.k, self.src, self.gain, self.H, self.L, self.full, self.sq, self.acc = k, src, gain, H, L, full, sq, acc
        self.plain, self.src_wait, self.n = plain, src_wait, len(src)
        self.S = {x: k.sem(f"{name}_{x}") for x in ("sq", "added", "sums", "root", "inv", "full", "high", "low",
                                                    "plain_high", "plain_low")}

    def act(self, act):
        k, S = self.k, self.S
        for t, ap in self.plain:
            act.activation(self.H[:, t, :], ap, ACT.Copy).then_inc(S["plain_high"], 1)
        for i in range(self.n):
            if self.src_wait:
                act.wait_ge(*self.src_wait(i))
            if i >= 2:
                act.wait_ge(S["added"], max(1, i - 2))
            act.activation(self.sq[:, i % 2, :], self.src[i], ACT.Square).then_inc(S["sq"], 1)
        for n in range(3):
            act.wait_ge(S["sums"], n + 1)
            act.activation(third(self.acc, n), self.bank[n][:, 0:C3], ACT.Sqrt, bias=k.mask("eps", 1),
                           scale=1.0 / (self.n * P)).then_inc(S["root"], 1)
        if self.H is not None:
            for n in range(3):
                for i in range(self.n):
                    act.wait_ge(S["full"], n * self.n + i + 1)
                    act.activation(third(self.H[:, i + len(self.plain), :], n), third(self.full[:, i + len(self.plain), :], n),
                                   ACT.Copy).then_inc(S["high"], 1)

    def pe(self, pe):
        k, S = self.k, self.S
        pe.wait_ge(S["added"], self.n - 1)
        for n in range(3):
            pe.matmul(self.bank[n][:, 0:C3], k.mask("ones"), third(self.acc, n), start=True, stop=True).then_inc(S["sums"], 1)

    def wait_parts(self, pe, n):
        if self.plain:
            pe.wait_ge(self.S["plain_low"], len(self.plain))
        pe.wait_ge(self.S["low"], self.n * (n + 1))

    def dve(self, dve):
        k, S, o = self.k, self.S, len(self.plain)
        for i in range(1, self.n):
            dve.wait_ge(S["sq"], i + 1)
            if i == 1:
                a = self.sq[:, 0, :]
            else:
                a = self.acc
                dve.wait_ge(S["added"], i - 1)
            dve.tensor_tensor(self.acc, a, self.sq[:, i % 2, :], ALU.add).then_inc(S["added"], 1)
        for j, (t, ap) in enumerate(self.plain):
            dve.wait_ge(S["plain_high"], j + 1)
            dve.tensor_tensor(self.L[:, t, :], ap, self.H[:, t, :].bitcast(F32), ALU.subtract).then_inc(S["plain_low"], 1)

        def low(j):
            n, i = divmod(j, self.n)
            dve.wait_ge(S["high"], j + 1)
            dve.tensor_tensor(third(self.L[:, i + o, :], n), third(self.full[:, i + o, :], n),
                              third(self.H[:, i + o, :], n).bitcast(F32), ALU.subtract).then_inc(S["low"], 1)
        for n in range(3):
            dve.wait_ge(S["root"], n + 1)
            dve.reciprocal(third(self.acc, n), third(self.acc, n)).then_inc(S["inv"], 1)
            dve.wait_ge(S["inv"], n + 1)
            for i in range(self.n):
                dve.scalar_tensor_tensor(third(self.full[:, i + o, :], n), third(self.src[i], n), k.vec(self.gain, i),
                                         third(self.acc, n), ALU.mult, ALU.mult).then_inc(S["full"], 1)
                if self.H is not None and n * self.n + i >= 1:
                    low(n * self.n + i - 1)
        if self.H is not None:
            low(3 * self.n - 1)


def products(pe, ps, w, rhs, nk, inc):
    for kk in range(nk):
        for n, (a, b) in enumerate(((0, 0), (0, 1), (1, 0))):
            mm = pe.matmul(ps, w(a, kk), rhs(b, kk), start=(kk == 0 and n == 0), stop=(kk == nk - 1 and n == 2))
    mm.then_inc(inc, 1)


def linear_stage(k, name, w, n_m, groups, H, L, engine="vector", norm=None, first=(), then=(), after=None, drain_wait=None):
    nc = k.nc
    w_in = [k.sem(f"{name}_w{j}") for j in range(2)]
    w_high, w_low, made, taken = [k.sem(f"{name}_{s}") for s in ("w_high", "w_low", "made", "taken")]

    def pairs(eng, lo, step):
        with eng.Fori(lo // 2, n_m // 2) as i:
            for j in range(2):
                step(i, 2 * i + j, j)
        if n_m % 2:
            step(n_m // 2, n_m - 1, 0)
    with ExitStack() as ctx:
        slot = k.sb(ctx, f"{name}_slot", [P, 2, DK * P])
        part = k.sb(ctx, f"{name}_part", [P, 2, 2, DK * P], FR)
        with nc.Block() as block:
            @block.sync
            def _(sp):
                for dst, src, sem in first:
                    sp.dma_start(dst, src).then_inc(sem, 16)
                for j in range(2):
                    sp.dma_start(slot[:, j], w[j]).then_inc(w_in[j], 16)
                for dst, src, sem in then:
                    sp.dma_start(dst, src).then_inc(sem, 16)

                def load(i, m, j):
                    sp.wait_ge(w_low, m - 1)
                    sp.dma_start(slot[:, j], w[bass.ds(m, 1)].rearrange("a p n -> p (a n)")).then_inc(w_in[j], 16)
                pairs(sp, 2, load)

            @block.gpsimd
            def _(pool):
                def divide(i, m, j, free=True):
                    pool.wait_ge(w_in[j], 16 * (i + 1))
                    if free:
                        pool.wait_ge(made, 3 * (m - 1))
                    pool.tensor_tensor(part[:, j, 0], slot[:, j], k.mask("ones", 1).broadcast_to([P, D]), ALU.mult).then_inc(w_high, 1)
                    pool.wait_ge(w_high, m + 1)
                    pool.tensor_tensor(part[:, j, 1], slot[:, j], part[:, j, 0].bitcast(F32), ALU.subtract).then_inc(w_low, 1)
                divide(0, 0, 0, False)
                divide(0, 1, 1, False)
                pairs(pool, 2, divide)

            @block.tensor
            def _(pe):
                if norm:
                    norm.pe(pe)

                def step(i, m, j):
                    pe.wait_ge(w_low, m + 1)
                    pe.wait_ge(taken, m + 1)
                    for n in range(3):
                        if norm:
                            norm.wait_parts(pe, n)
                        products(pe, k.bank[3 * j + n][:, 0:C3], lambda a, kk: part[:, j, a, kk * P:(kk + 1) * P],
                                 lambda b, kk: third((H, L)[b][:, kk, :], n), DK, made)
                pairs(pe, 0, step)

            def drain(eng):
                eng.sem_inc(taken, 2)
                if drain_wait:
                    eng.wait_ge(*drain_wait)
                m0 = 0
                for count, ep in groups:
                    def step(m, j):
                        for n in range(3):
                            eng.wait_ge(made, 3 * (m0 + m) + n + 1)
                            last = ep(eng, m, n, k.bank[3 * j + n][:, 0:C3])
                        last.then_inc(taken, 1)
                    if count > 1:
                        with eng.Fori(0, count // 2) as i:
                            for a in range(2):
                                step(2 * i + a, (m0 + a) % 2)
                    if count % 2:
                        step(count - 1, (m0 + count - 1) % 2)
                    m0 += count

            @block.scalar
            def _(act):
                if norm:
                    norm.act(act)
                if engine == "scalar":
                    drain(act)

            @block.vector
            def _(dve):
                if norm:
                    norm.dve(dve)
                if engine == "vector":
                    drain(dve)
                if after:
                    after(dve, made)


def load_stage(k):
    nc, io = k.nc, k.io
    s_load = k.sem("s_load")
    with nc.Block() as block:
        @block.sync
        def _(sp):
            sp.dma_start(k.masks[:, :], io["masks"]).then_inc(s_load, 16)
            sp.dma_start(k.vecs[:, :], io["vecs"]).then_inc(s_load, 16)
            sp.wait_ge(s_load, 32)


def proj_stage(k, H, L, x):
    nc, io = k.nc, k.io

    def to(dst):
        def ep(eng, m, n, ps):
            return eng.activation(dst[:, bass.ds(m, 1), n * C3:(n + 1) * C3], ps, ACT.Copy)
        return ep
    s_x = [k.sem(f"x0_{i}") for i in range(4)]
    s_rot, s_zero, s_kr = [k.sem(f"kr_{x}") for x in ("rot", "zero", "own")]
    xv = io["x"].rearrange("(k p) t -> p k t", p=P)
    n_main = QK + KK + RWK

    def rope_key(dve, made):
        dve.memset(k.rw[:, :, T:TR], 0.0).then_inc(s_zero, 1)
        dve.wait_ge(s_rot, 16)
        own = Chain(dve, s_kr)
        for n in range(3):
            dve.wait_ge(made, 3 * n_main + n + 1)
            c, ps = slice(n * C3, (n + 1) * C3), k.bank[3 * (n_main % 2) + n]
            own(dve.tensor_tensor(k.krope[64:96, c], ps[64:96, 0:C3], k.rot[64:96, 0, c], ALU.mult))
            own(dve.tensor_tensor(u[64:96, c], ps[96:128, 0:C3], k.rot[96:128, 1, c], ALU.mult))
            own(dve.tensor_tensor(k.krope[64:96, c], k.krope[64:96, c], u[64:96, c], ALU.add))
    with ExitStack() as ctx:
        acc = k.sb(ctx, "x0_acc", [P, T])
        u = k.sb(ctx, "x0_u", [P, T])
        norm = Norm(k, "nmix", [x[:, i, :] for i in range(DK)], "g_mix", H, L, x, k.rw[:, 0:2, 0:T], acc[:, :],
                    src_wait=lambda i: (s_x[i // 2], 16))

        linear_stage(k, "pj", io["w_in"], QK + KK + RWK + 1, [(QK + KK, to(k.cqkv)), (RWK, to(k.rw))], H, L, engine="scalar", norm=norm,
                     first=[(x[:, 2 * i:2 * i + 2, :], xv[:, 2 * i:2 * i + 2, :], s_x[i]) for i in range(4)],
                     then=[(k.rot[:, :, :].rearrange("p a t -> p (a t)"), io["rot"], s_rot)], after=rope_key)


TILES = TP // P
GROUPS = [(i + 4) // 4 for i in range(TILES)]
GSUM = [sum(GROUPS[:i + 1]) for i in range(TILES)]
NG = GSUM[-1]


def mla_prompt_stage(k, cq_low, qabs, qrope):
    nc, io = k.nc, k.io
    S = {n: k.sem(f"mp_{n}") for n in (
        "w_high", "w_low", "q_made", "k_made", "v_made", "ukt_made", "qabs_made", "q_taken", "qr_cos", "qr_sin", "qr_taken",
        "k_taken", "v_taken", "ukt_taken", "qabs_taken", "s_made", "maxed", "m_ready", "e_done", "r_done",
        "t_made", "t_taken", "o_made", "o_taken", "ot_made", "ot_taken", "kr_there", "out")}
    w_in = [k.sem(f"mp_w{j}") for j in range(2)]
    cq, lat = k.cqkv[:, 0:QK, :], k.cqkv[:, QK:QK + KK, :]
    B, QH, UKV = k.bank, NOPE + ROPE, 2 * HD
    with ExitStack() as ctx:
        cq_high = k.sb(ctx, "mp_cq", [P, QK, T], FR)
        uq = k.sb(ctx, "mp_uq", [P, 2, QK * P])
        uqp = k.sb(ctx, "mp_uqp", [P, 2, 2, QK * P], FR)
        ukv = k.sb(ctx, "mp_ukv", [P, 2, KK, UKV])
        qT = k.sb(ctx, "mp_qT", [P, 2, T])
        kT = k.sb(ctx, "mp_kT", [P, 2, TP])
        v = k.sb(ctx, "mp_v", [P, 2, 512])
        ukT = k.sb(ctx, "mp_ukT", [HD, 2, KVL])
        u = k.sb(ctx, "mp_u", [P, C3])
        pr = k.sb(ctx, "mp_pr", [P, 2, T])
        pT = k.sb(ctx, "mp_pT", [P, 2, T])
        ot = k.sb(ctx, "mp_ot", [P, TILES, 2 * HD])
        stat = k.sb(ctx, "mp_stat", [P, 4, TILES])
        mx, negm, rsum, rinv = [stat[:, n, :] for n in range(4)]
        nq = Norm(k, "nq", [cq[:, i, :] for i in range(QK)], "q_norm_g", cq_high, cq_low, cq, qT[:, :, :], pr[:, 0, :])
        nkv = Norm(k, "nkv", [lat[:, i, :] for i in range(KK)], "kv_norm_g", None, None, lat, pT[:, :, :], pr[:, 1, :], bank=2)
        with nc.Block() as block:
            @block.sync
            def _(sp):
                def load(h, j):
                    sp.dma_start(uq[:, j], io["w_uq"][bass.ds(h, 1)].rearrange("a p n -> p (a n)")).then_inc(w_in[j], 16)
                    sp.dma_start(ukv[:, j].rearrange("p k n -> p (k n)"),
                                 io["w_ukv"][bass.ds(h, 1)].rearrange("a p n -> p (a n)")).then_inc(w_in[j], 16)
                load(0, 0)
                load(1, 1)
                sp.dma_start(io["o_krope"], k.krope[64:96, :]).then_inc(S["out"], 16)
                sp.wait_ge(nkv.S["full"], 3 * KK)
                sp.dma_start(io["o_lat"].rearrange("(k p) t -> p k t", p=P), lat).then_inc(S["out"], 16)
                with sp.Fori(1, NH // 2) as i:
                    for j in range(2):
                        sp.wait_ge(S["w_low"], 2 * i + j - 1)
                        sp.wait_ge(S["ukt_made"], 2 * i + j - 1)
                        load(2 * i + j, j)
                sp.wait_ge(S["out"], 32)

            @block.gpsimd
            def _(pool):
                def divide(i, j, free=True):
                    h = 2 * i + j
                    pool.wait_ge(w_in[j], 32 * (i + 1))
                    if free:
                        pool.wait_ge(S["q_made"], 3 * (h - 1))
                    pool.tensor_tensor(uqp[:, j, 0], uq[:, j], k.mask("ones", 1).broadcast_to([P, QK * P]), ALU.mult)\
                        .then_inc(S["w_high"], 1)
                    pool.wait_ge(S["w_high"], h + 1)
                    pool.tensor_tensor(uqp[:, j, 1], uq[:, j], uqp[:, j, 0].bitcast(F32), ALU.subtract).then_inc(S["w_low"], 1)
                divide(0, 0, False)
                divide(0, 1, False)
                with pool.Fori(1, NH // 2) as i:
                    divide(i, 0)
                    divide(i, 1)

            @block.tensor
            def _(pe):
                nkv.pe(pe)
                nq.pe(pe)

                def piece(h, j, p):
                    if p < 3:
                        if p == 0:
                            pe.wait_ge(S["w_low"], h + 1)
                        else:
                            pe.wait_ge(S["q_taken"], 3 * h + p)
                            pe.wait_ge(S["qr_taken"], 3 * h + p)
                        nq.wait_parts(pe, p)
                        products(pe, B[7][:, 0:C3], lambda a, kk: uqp[:, j, a, kk * P:(kk + 1) * P],
                                 lambda b, kk: third((cq_high, cq_low)[b][:, kk, :], p), QK, S["q_made"])
                    elif p < 5:
                        n = p - 3
                        if n == 0:
                            pe.wait_ge(S["q_taken"], 3 * h + 3)
                            pe.wait_ge(S["qr_taken"], 3 * h + 3)
                            pe.wait_ge(nkv.S["full"], 3 * KK)
                        else:
                            pe.wait_ge(S["k_taken"], 2 * h + 1)
                        for kk in range(KK):
                            mm = pe.matmul(B[7][0:NOPE, :], ukv[:, j, kk, 0:NOPE], lat[:, kk, n * 512:(n + 1) * 512],
                                           start=(kk == 0), stop=(kk == KK - 1))
                        mm.then_inc(S["k_made"], 1)
                    elif p == 5:
                        pe.wait_ge(S["k_taken"], 2 * h + 2)
                        for t in range(TILES):
                            for kk in range(KK):
                                mm = pe.matmul(B[7][:, t * HD:(t + 1) * HD], lat[:, kk, t * P:(t + 1) * P],
                                               ukv[:, j, kk, NOPE:], start=(kk == 0), stop=(kk == KK - 1))
                        mm.then_inc(S["v_made"], 1)
                    elif p == 6:
                        pe.wait_ge(S["v_taken"], h + 1)
                        for kk in range(KK):
                            mm = pe.transpose(B[7][:, kk * P:(kk + 1) * P], ukv[:, j, kk, :], k.mask("ident"))
                        mm.then_inc(S["ukt_made"], 1)
                    else:
                        pe.wait_ge(S["ukt_taken"], h + 1)
                        for kk in range(KK):
                            mm = pe.matmul(B[7][:, kk * TS:(kk + 1) * TS], ukT[:, j, kk * P:(kk + 1) * P], qT[0:NOPE, j, TP:T],
                                           start=True, stop=True)
                        mm.then_inc(S["qabs_made"], 1)

                def scores(h, j, i):
                    n_keys = (i + 1) * P
                    for c in range(0, n_keys, 512):
                        w = min(512, n_keys - c)
                        pe.matmul(B[2 * (i % 2) + c // 512][:, 0:w], qT[0:QH, j, i * P:(i + 1) * P],
                                  kT[0:QH, j, c:c + w], start=True, stop=True)
                    mm = pe.matmul(B[2 * (i % 2) + i // 4][:, i % 4 * P:(i % 4 + 1) * P], k.mask("ident"), k.mask("causal"),
                                   start=False, stop=True, skip_group_check=True)
                    mm.then_inc(S["s_made"], 1)

                def transposes(h, i):
                    pe.wait_ge(S["e_done"], TILES * h + i + 1)
                    for g in range(GROUPS[i]):
                        n = GSUM[i] - GROUPS[i] + g
                        pe.wait_ge(S["t_taken"], NG * h + n + 1)
                        for t in range(4 * g, min(4 * g + 4, i + 1)):
                            mm = pe.transpose(B[4 + n % 2][:, (t % 4) * P:(t % 4 + 1) * P], pr[:, i % 2, t * P:(t + 1) * P],
                                              k.mask("ident"))
                        mm.then_inc(S["t_made"], 1)

                def values(h, j, i):
                    pe.wait_ge(S["t_taken"], NG * h + GSUM[i] + 2)
                    pe.wait_ge(S["o_taken"], TILES * h + i + 1)
                    for t in range(i + 1):
                        mm = pe.matmul(B[6][:, 0:HD], pT[:, i % 2, t * P:(t + 1) * P], v[:, j, t * HD:(t + 1) * HD],
                                       start=(t == 0), stop=(t == i))
                    mm.then_inc(S["o_made"], 1)

                def outputs(h, g):
                    pe.wait_ge(S["o_taken"], TILES * h + 4 * g + 5)
                    for t in range(4):
                        mm = pe.transpose(B[7][:, t * P:(t + 1) * P], ot[:, 4 * g + t, :], k.mask("ident"))
                    mm.then_inc(S["ot_made"], 1)

                def head(it, j, follows=True):
                    h = 2 * it + j
                    for i in range(TILES):
                        transposes(h, i)
                        if i + 2 < TILES:
                            scores(h, j, i + 2)
                        elif follows:
                            scores(h + 1, 1 - j, i + 2 - TILES)
                        if follows:
                            if i == 0:
                                pe.wait_ge(S["qabs_taken"], h + 1)
                                if j == 0:
                                    pe.wait_ge(S["ot_taken"], 2 * it + 1)
                            if i == 6 and j == 1:
                                pe.wait_ge(S["ot_taken"], 2 * it + 2)
                            piece(h + 1, 1 - j, i)
                        values(h, j, i)
                        if j == 1 and i == 5:
                            pe.wait_ge(S["v_taken"] if follows else S["qabs_taken"], h + 2 if follows else NH)
                            outputs(h, 0)
                        if j == 1 and i == 7:
                            pe.wait_ge(S["qabs_taken"], h + 2 if follows else NH)
                            if not follows:
                                pe.wait_ge(S["ot_taken"], 2 * it + 2)
                            outputs(h, 1)
                pe.wait_ge(S["kr_there"], 2)
                pe.wait_ge(nq.S["root"], 3)
                for p in range(8):
                    piece(0, 0, p)
                scores(0, 0, 0)
                scores(0, 0, 1)
                with pe.Fori(0, NH // 2 - 1) as it:
                    head(it, 0)
                    head(it, 1)
                head(NH // 2 - 1, 0)
                head(NH // 2 - 1, 1, False)

            @block.scalar
            def _(act):
                nkv.act(act)
                nq.act(act)
                act.sem_inc(S["t_taken"], 2)

                def exponential(h, i):
                    act.wait_ge(S["m_ready"], TILES * h + i + 1)
                    act.activation(pr[:, i % 2, 0:(i + 1) * P], k.psum[:, 1024 * (i % 2):1024 * (i % 2) + (i + 1) * P],
                                   ACT.Exp, bias=negm[:, i:i + 1], scale=SCALE,
                                   accum_out=rsum[:, i:i + 1]).then_inc(S["e_done"], 1)

                def copy_out(h, i):
                    for g in range(GROUPS[i]):
                        n = GSUM[i] - GROUPS[i] + g
                        act.wait_ge(S["t_made"], NG * h + n + 1)
                        w = min(4, i + 1 - 4 * g) * P
                        act.activation(pT[:, i % 2, 512 * g:512 * g + w], B[4 + n % 2][:, 0:w], ACT.Copy)\
                           .then_inc(S["t_taken"], 1)

                def piece(h, j, p):
                    if p < 3:
                        act.wait_ge(S["q_made"], 3 * h + p + 1)
                        act.activation(third(qT[0:NOPE, j, :], p), B[7][0:NOPE, 0:C3], ACT.Copy).then_inc(S["q_taken"], 1)
                    elif p < 5:
                        n = p - 3
                        act.wait_ge(S["k_made"], 2 * h + n + 1)
                        act.activation(kT[0:NOPE, j, n * 512:(n + 1) * 512], B[7][0:NOPE, :], ACT.Copy)\
                           .then_inc(S["k_taken"], 1)
                    elif p == 5:
                        act.wait_ge(S["v_made"], h + 1)
                        act.activation(v[:, j, :], B[7], ACT.Copy).then_inc(S["v_taken"], 1)
                    elif p == 6:
                        act.wait_ge(S["ukt_made"], h + 1)
                        act.activation(ukT[:, j, :], B[7][0:HD, 0:KVL], ACT.Copy).then_inc(S["ukt_taken"], 1)

                def head(it, j, follows=True):
                    h = 2 * it + j
                    for i in range(TILES):
                        if i + 1 < TILES:
                            exponential(h, i + 1)
                        elif follows:
                            exponential(h + 1, 0)
                        copy_out(h, i)
                        if follows:
                            piece(h + 1, 1 - j, i)
                for p in range(8):
                    piece(0, 0, p)
                exponential(0, 0)
                with act.Fori(0, NH // 2 - 1) as it:
                    head(it, 0)
                    head(it, 1)
                head(NH // 2 - 1, 0)
                head(NH // 2 - 1, 1, False)

            @block.vector
            def _(dve):
                nkv.dve(dve)
                nq.dve(dve)
                dve.sem_inc(S["o_taken"], 1)
                dve.sem_inc(S["ot_taken"], 1)
                for j in range(2):
                    dve.tensor_copy(kT[NOPE:QH, j, :], k.krope[64:96, 0:TP]).then_inc(S["kr_there"], 1)

                def maximum(h, i):
                    ps = k.psum[:, 1024 * (i % 2):1024 * (i % 2) + (i + 1) * P]
                    dve.wait_ge(S["s_made"], TILES * h + i + 1)
                    dve.reduce_max(mx[:, i:i + 1], ps, AX).then_inc(S["maxed"], 1)
                    dve.wait_ge(S["maxed"], TILES * h + i + 1)
                    dve.tensor_scalar(negm[:, i:i + 1], mx[:, i:i + 1], -SCALE, None, ALU.mult).then_inc(S["m_ready"], 1)

                def piece(h, j, p):
                    if p < 3:
                        n, c = 3 * h + p + 1, slice(p * C3, (p + 1) * C3)
                        dve.wait_ge(S["q_made"], n)
                        dve.tensor_tensor(qT[64:96, j, c], B[7][64:96, 0:C3], k.rot[64:96, 0, c], ALU.mult)\
                           .then_inc(S["qr_cos"], 1)
                        dve.tensor_tensor(u[64:96, :], B[7][96:128, 0:C3], k.rot[96:128, 1, c], ALU.mult)\
                           .then_inc(S["qr_sin"], 1)
                        dve.wait_ge(S["qr_cos"], n)
                        dve.wait_ge(S["qr_sin"], n)
                        dve.tensor_tensor(qT[64:96, j, c], qT[64:96, j, c], u[64:96, :], ALU.add)\
                           .then_inc(S["qr_taken"], 1)
                        dve.wait_ge(S["qr_taken"], n)
                    elif p == 7:
                        dve.wait_ge(S["qabs_made"], h + 1)
                        for kk in range(KK):
                            last = dve.tensor_copy(
                                qabs[:, kk, :, bass.ds(h, 1), :],
                                B[7][:, kk * TS:(kk + 1) * TS].rearrange("p (b t) -> p b t", b=NB))
                        dve.tensor_copy(qrope[0:ROPE, :, bass.ds(h, 1), :],
                                        qT[64:96, j, TP:T].rearrange("p (b t) -> p b t", b=NB))
                        last.then_inc(S["qabs_taken"], 1)

                def head(it, j, follows=True):
                    h = 2 * it + j
                    for i in range(TILES):
                        dve.wait_ge(S["e_done"], TILES * h + i + 1)
                        dve.reciprocal(rinv[:, i:i + 1], rsum[:, i:i + 1]).then_inc(S["r_done"], 1)
                        if i + 2 < TILES:
                            maximum(h, i + 2)
                        elif follows:
                            maximum(h + 1, i + 2 - TILES)
                        if follows:
                            piece(h + 1, 1 - j, i)
                        dve.wait_ge(S["o_made"], TILES * h + i + 1)
                        dve.wait_ge(S["r_done"], TILES * h + i + 1)
                        dve.tensor_scalar(ot[:, i, j * HD:(j + 1) * HD], B[6][:, 0:HD], rinv[:, i:i + 1], None, ALU.mult)\
                           .then_inc(S["o_taken"], 1)
                        if j == 1 and i in (5, 7):
                            g = (i - 5) // 2
                            dve.wait_ge(S["ot_made"], 2 * it + g + 1)
                            dve.tensor_copy(k.mla[:, bass.ds(it, 1), g * 512:(g + 1) * 512], B[7].unsqueeze(1))\
                               .then_inc(S["ot_taken"], 1)
                for p in range(8):
                    piece(0, 0, p)
                maximum(0, 0)
                maximum(0, 1)
                with dve.Fori(0, NH // 2 - 1) as it:
                    head(it, 0)
                    head(it, 1)
                head(NH // 2 - 1, 0)
                head(NH // 2 - 1, 1, False)


def mla_sample_stage(k, free_y, free_cq, qabs, qrope):
    nc, io = k.nc, k.io
    R = NH * TSEQ
    GP, LW, GC = 4, KVL + ROPE, 4 * PAGE
    NGP = NPG // GP
    S = {n: k.sem(f"ms_{n}") for n in (
        "pg", "w", "kr0", "q_there", "t_made", "t_taken", "s_made", "s_copied", "s_taken", "n_made", "n_masked", "new_taken",
        "maxed", "m_ready", "e_done", "r_done", "pt_made", "pt_taken", "x_made", "x_taken", "o_made", "o_taken", "ot_made", "ot_taken", "uv_made")}
    LOADED = (0, 1, 3, 4, 6), (2, 5, 7)
    k_in = [[[k.sem(f"ms_k{e}{j}{g}") for g in range(NGP)] for j in range(2)] for e in "sp"]
    loads = [[2 * sum(n % 8 in mine for n in range(GP * g, GP * (g + 1))) for g in range(NGP)] for mine in LOADED]
    B = k.bank
    lat = k.cqkv[:, QK:QK + KK, :]
    sc = k.at(free_y, "ms_sc", [R, 2, PAST + TSEQ])
    kT = k.at(free_cq, "ms_kT", [P, 2, KK, GC])
    krT = k.at(free_cq, "ms_krT", [ROPE, 2, GC], words=2 * KK * GC)
    with ExitStack() as ctx:
        pages = k.sb(ctx, "ms_pages", [1, NB * NPG], I32)
        keys = k.sb(ctx, "ms_keys", [P, 2, NPG, LW])
        kr0 = k.sb(ctx, "ms_kr0", [ROPE, TS])
        qb = k.sb(ctx, "ms_qb", [P, 2, KK, R])
        qrb = k.sb(ctx, "ms_qrb", [ROPE, 2, R])
        krn = k.sb(ctx, "ms_krn", [ROPE, 2, TSEQ])
        newT = k.sb(ctx, "ms_newT", [P, 2, KK, TSEQ])
        new = k.sb(ctx, "ms_new", [TSEQ, KVL])
        pT = k.sb(ctx, "ms_pT", [P, NPG * R])
        pnT = k.sb(ctx, "ms_pnT", [TSEQ, R])
        ol = k.sb(ctx, "ms_ol", [R, KVL])
        olT = k.sb(ctx, "ms_olT", [P, KK, NH, NB, TSEQ])
        gmax = k.sb(ctx, "ms_gmax", [R, NGP + 1])
        stat = k.sb(ctx, "ms_stat", [R, 4])
        wuv = k.sb(ctx, "ms_wuv", [P, KK, NH, HD])
        new_sc, new_tr, x_tr = B[7][0:R, 0:TSEQ], B[7][0:TSEQ, 16:16 + KVL], B[7][0:TSEQ, 288:288 + R]
        o_ps, o_tr = B[7][0:R, 0:KVL], B[7][:, 384:384 + KK * R]

        def batches(eng, step, tail):
            step(0, 0, False)
            with eng.Fori(0, (NB - 2) // 2) as i:
                step(2 * i + 1, 1, True)
                step(2 * i + 2, 0, True)
            step(NB - 1, 1, True)
            tail(NB - 1, 1)

        def load_keys(eng, e):
            eng.wait_ge(S["pg"], 16)

            def load(b, j):
                for n in range(NPG):
                    if n % 8 in LOADED[e]:
                        page = eng.value_load(pages[0:1, bass.ds(b * NPG + n, 1)], min_val=0, max_val=io["lat"].shape[0] - 1)
                        eng.dma_start(keys[:, j, n, 0:KVL], io["lat"][bass.ds(page, 1)].rearrange("a p c -> p (a c)"))\
                           .then_inc(k_in[e][j][n // GP], 16)
                        eng.dma_start(keys[:, j, n, KVL:LW], io["kr"][bass.ds(page, 1)].rearrange("a p c -> p (a c)"))\
                           .then_inc(k_in[e][j][n // GP], 16)
            load(0, 0)
            load(1, 1)
            with eng.Fori(1, NB // 2) as i:
                for j in range(2):
                    eng.wait_ge(S["o_made"], 2 * i + j - 1)
                    load(2 * i + j, j)
        with nc.Block() as block:
            @block.sync
            def _(sp):
                sp.dma_start(pages[:, :], io["pages"]).then_inc(S["pg"], 16)
                load_keys(sp, 0)
                for kk in range(KK):
                    sp.dma_start(wuv[:, kk, :, :], io["w_ukv"].rearrange("h p (k m) -> p k h m", k=KK)[:, kk, :, HD:])\
                      .then_inc(S["w"], 16)

            @block.gpsimd
            def _(pool):
                load_keys(pool, 1)

            @block.tensor
            def _(pe):
                def transposes(b, j, g):
                    for e in range(2):
                        pe.wait_ge(k_in[e][j][g], 8 * loads[e][g] * (b - j + 2))
                    pe.wait_ge(S["t_taken"], 3 * (NGP * b + g + 1))
                    for n in range(GP):
                        pg, c = GP * g + n, slice(n * PAGE, (n + 1) * PAGE)
                        for kk in range(KK):
                            pe.transpose(B[2 * (g % 2) + kk][:, c], keys[:, j, pg, kk * P:(kk + 1) * P], k.mask("ident"))
                        mm = pe.transpose(B[4][0:ROPE, c], keys[:, j, pg, KVL:LW], k.mask("ident"))
                    mm.then_inc(S["t_made"], 1)

                def scores(b, j, g):
                    pe.wait_ge(S["q_there"], 4 * (b + 1))
                    pe.wait_ge(S["t_taken"], 3 * (NGP * b + g + 2))
                    pe.wait_ge(S["s_taken"], NGP * b + g + 1)
                    for kk in range(KK):
                        pe.matmul(B[5][0:R, :], qb[:, j, kk, :], kT[:, g % 2, kk, :], start=(kk == 0), stop=False)
                    pe.matmul(B[5][0:R, :], qrb[:, j, :], krT[:, g % 2, :], start=False, stop=True).then_inc(S["s_made"], 1)

                def new_tokens(b, j):
                    pe.wait_ge(S["ot_taken"], b + 1)
                    for kk in range(KK):
                        pe.matmul(new_sc, qb[:, j, kk, :], newT[:, j, kk, :], start=(kk == 0), stop=False)
                    pe.matmul(new_sc, qrb[:, j, :], krn[:, j, :], start=False, stop=True)
                    for kk in range(KK):
                        mm = pe.transpose(new_tr[:, kk * P:(kk + 1) * P], newT[:, j, kk, :], k.mask("ident"))
                    mm.then_inc(S["n_made"], 1)

                def probabilities(b, j):
                    pe.wait_ge(S["e_done"], b + 1)
                    pe.wait_ge(S["new_taken"], b + 1)
                    pe.transpose(B[6][:, 0:P], k.mask("ident"), k.mask("ident"))
                    for n in range(NPG):
                        mm = pe.transpose(B[6][:, n * R:(n + 1) * R], sc[:, j, n * PAGE:(n + 1) * PAGE], k.mask("ident", R, R))
                    mm.then_inc(S["pt_made"], 1)
                    pe.transpose(x_tr, sc[:, j, PAST:], k.mask("ident", R, R)).then_inc(S["x_made"], 1)

                def outputs(b, j):
                    pe.wait_ge(S["pt_taken"], b + 1)
                    pe.wait_ge(S["x_taken"], b + 1)
                    for n in range(NPG):
                        pe.matmul(o_ps, pT[:, n * R:(n + 1) * R], keys[:, j, n, 0:KVL], start=(n == 0), stop=False)
                    pe.matmul(o_ps, pnT[:, :], new[:, :], start=False, stop=True).then_inc(S["o_made"], 1)

                def turn_outputs(b):
                    pe.wait_ge(S["o_taken"], b + 1)
                    for kk in range(KK):
                        mm = pe.matmul(o_tr[:, kk * R:(kk + 1) * R], ol[:, kk * P:(kk + 1) * P], k.mask("ident", R, R),
                                       start=True, stop=True)
                    mm.then_inc(S["ot_made"], 1)

                def step(b, j, before):
                    transposes(b, j, 0)
                    if before:
                        scores(b - 1, 1 - j, NGP - 1)
                        new_tokens(b - 1, 1 - j)
                    transposes(b, j, 1)
                    scores(b, j, 0)
                    if before:
                        probabilities(b - 1, 1 - j)
                    transposes(b, j, 2)
                    if before:
                        outputs(b - 1, 1 - j)
                    scores(b, j, 1)
                    if before:
                        turn_outputs(b - 1)
                    transposes(b, j, 3)
                    scores(b, j, 2)

                def tail(b, j):
                    scores(b, j, NGP - 1)
                    new_tokens(b, j)
                    probabilities(b, j)
                    outputs(b, j)
                    turn_outputs(b)
                pe.wait_ge(S["kr0"], 1)
                batches(pe, step, tail)
                pe.wait_ge(S["ot_taken"], NB + 1)
                pe.wait_ge(S["w"], 16 * KK)
                for h in range(NH):
                    for kk in range(KK):
                        mm = pe.matmul(B[h % 2][h % 2 * HD:(h % 2 + 1) * HD, h // 2 * TS:(h // 2 + 1) * TS],
                                       wuv[:, kk, h, :], olT[:, kk, h, :, :].rearrange("p b t -> p (b t)"),
                                       start=(kk == 0), stop=(kk == KK - 1))
                mm.then_inc(S["uv_made"], 1)

            @block.scalar
            def _(act):
                act.activation(kr0[:, :], k.krope[64:96, TP:T], ACT.Copy).then_inc(S["kr0"], 1)
                act.sem_inc(S["t_taken"], 3)
                act.sem_inc(S["ot_taken"], 1)
                act.wait_ge(S["kr0"], 1)

                def copy_keys(b, j, g):
                    act.wait_ge(S["t_made"], NGP * b + g + 1)
                    act.activation(krT[:, g % 2, :], B[4][0:ROPE, :], ACT.Copy).then_inc(S["t_taken"], 1)
                    for kk in range(KK):
                        act.activation(kT[:, g % 2, kk, :], B[2 * (g % 2) + kk], ACT.Copy).then_inc(S["t_taken"], 1)

                def exponential(b, j):
                    act.wait_ge(S["m_ready"], b + 1)
                    act.activation(sc[:, j, :], sc[:, j, :], ACT.Exp, bias=stat[:, 1:2], scale=SCALE, accum_out=stat[:, 2:3])\
                       .then_inc(S["e_done"], 1)

                def copy_probabilities(b):
                    act.wait_ge(S["pt_made"], b + 1)
                    act.activation(pT[:, :], B[6], ACT.Copy).then_inc(S["pt_taken"], 1)

                def copy_outputs(b):
                    act.wait_ge(S["ot_made"], b + 1)
                    for kk in range(KK):
                        last = act.activation(olT[:, kk, :, bass.ds(b, 1), :],
                                              o_tr[:, kk * R:(kk + 1) * R].rearrange("p (h t) -> p h t", h=NH), ACT.Copy)
                    last.then_inc(S["ot_taken"], 1)

                def step(b, j, before):
                    act.activation(qb[:, j, :, :], qabs[:, :, bass.ds(b, 1), :, :].rearrange("p k b h t -> p k (b h t)"),
                                   ACT.Copy).then_inc(S["q_there"], 1)
                    act.activation(qrb[:, j, :], qrope[:, bass.ds(b, 1), :, :].rearrange("p b h t -> p (b h t)"),
                                   ACT.Copy).then_inc(S["q_there"], 1)
                    act.activation(krn[:, j, :], kr0[:, bass.ds(b * TSEQ, TSEQ)], ACT.Copy).then_inc(S["q_there"], 1)
                    act.activation(newT[:, j, :, :], lat[:, :, bass.ds(TP + b * TSEQ, TSEQ)], ACT.Copy)\
                       .then_inc(S["q_there"], 1)
                    copy_keys(b, j, 0)
                    copy_keys(b, j, 1)
                    if before:
                        exponential(b - 1, 1 - j)
                        copy_probabilities(b - 1)
                    copy_keys(b, j, 2)
                    if before:
                        copy_outputs(b - 1)
                    copy_keys(b, j, 3)

                def tail(b, j):
                    exponential(b, j)
                    copy_probabilities(b)
                    copy_outputs(b)
                batches(act, step, tail)

            @block.vector
            def _(dve):
                dve.sem_inc(S["s_taken"], 1)

                def scores(b, j, g):
                    dve.wait_ge(S["s_made"], NGP * b + g + 1)
                    dve.tensor_copy(sc[:, j, g * GC:(g + 1) * GC], B[5][0:R, :]).then_inc(S["s_copied"], 1)
                    dve.reduce_max(gmax[:, g:g + 1], B[5][0:R, :], AX).then_inc(S["s_taken"], 1)

                def maximum(b, j):
                    dve.wait_ge(S["n_made"], b + 1)
                    dve.tensor_tensor(sc[:, j, PAST:], new_sc, k.mask("new_causal", TSEQ, R), ALU.add).then_inc(S["n_masked"], 1)
                    dve.wait_ge(S["n_masked"], 2 * b + 1)
                    dve.reduce_max(gmax[:, NGP:], sc[:, j, PAST:], AX).then_inc(S["n_masked"], 1)
                    dve.wait_ge(S["n_masked"], 2 * b + 2)
                    dve.wait_ge(S["s_taken"], NGP * (b + 1) + 1)
                    dve.reduce_max(stat[:, 0:1], gmax[:, :], AX).then_inc(S["maxed"], 1)
                    dve.wait_ge(S["maxed"], b + 1)
                    dve.tensor_scalar(stat[:, 1:2], stat[:, 0:1], -SCALE, None, ALU.mult).then_inc(S["m_ready"], 1)
                    dve.tensor_copy(new[:, :], new_tr).then_inc(S["new_taken"], 1)

                def divide(b, j):
                    dve.wait_ge(S["e_done"], b + 1)
                    dve.reciprocal(stat[:, 3:4], stat[:, 2:3]).then_inc(S["r_done"], 1)

                def new_probabilities(b):
                    dve.wait_ge(S["x_made"], b + 1)
                    dve.wait_ge(S["new_taken"], b + 1)
                    dve.tensor_copy(pnT[:, :], x_tr).then_inc(S["x_taken"], 1)

                def take_outputs(b):
                    dve.wait_ge(S["o_made"], b + 1)
                    dve.wait_ge(S["r_done"], b + 1)
                    dve.tensor_scalar(ol[:, :], o_ps, stat[:, 3:4], None, ALU.mult).then_inc(S["o_taken"], 1)

                def step(b, j, before):
                    if before:
                        scores(b - 1, 1 - j, NGP - 1)
                        maximum(b - 1, 1 - j)
                        divide(b - 1, 1 - j)
                    scores(b, j, 0)
                    if before:
                        new_probabilities(b - 1)
                        take_outputs(b - 1)
                    scores(b, j, 1)
                    scores(b, j, 2)

                def tail(b, j):
                    scores(b, j, NGP - 1)
                    maximum(b, j)
                    divide(b, j)
                    new_probabilities(b)
                    take_outputs(b)
                batches(dve, step, tail)
                dve.wait_ge(S["uv_made"], 1)
                for j in range(2):
                    dve.tensor_copy(k.mla[j * HD:(j + 1) * HD, :, TP:T],
                                    B[j][j * HD:(j + 1) * HD, 0:4 * TS].rearrange("p (h n) -> p h n", h=4))


def rwkv_prep_stage(k, c, a, kk, keep):
    nc, io, rw = k.nc, k.io, k.rw
    B = k.bank
    S = {n: k.sem(f"rp_{n}") for n in (
        "in", "w", "own", "zero", "last", "shifted", "half", "tanh", "z_made", "z_taken", "a_made", "a_taken", "kk", "sq", "ss_made",
        "root", "inv", "bc_made", "bc_taken", "out")}
    G = 4
    with ExitStack() as ctx:
        sh0 = k.sb(ctx, "rp_sh0", [P, RWK, NB])
        last = k.sb(ctx, "rp_last", [P, RWK, 1 + NB])
        tmp = k.sb(ctx, "rp_tmp", [P, 2, T])
        w2 = k.sb(ctx, "rp_w2", [P, 512])
        hb = k.sb(ctx, "rp_hb", [P, 2 * G])
        with nc.Block() as block:
            @block.sync
            def _(sp):
                sp.dma_start(sh0[:, :, :], io["shift0"]).then_inc(S["in"], 16)
                sp.dma_start(keep[:, :], io["keep"]).then_inc(S["in"], 16)
                sp.dma_start(w2[0:64, :], io["rw_w2"]).then_inc(S["w"], 16)
                sp.dma_start(w2[64:128, :], io["rw_a2"]).then_inc(S["w"], 16)
                sp.wait_ge(S["last"], 2)
                sp.dma_start(io["o_shift"], last[:, :, :]).then_inc(S["out"], 16)
                sp.wait_ge(S["out"], 16)

            @block.gpsimd
            def _(pool):
                pool.memset(c[:, :, 0:1], 0.0).then_inc(S["zero"], 1)
                pool.memset(c[:, :, 1 + T:], 0.0).then_inc(S["zero"], 1)
                pool.memset(a[:, :, T:], 0.0).then_inc(S["zero"], 1)
                pool.memset(kk[:, :, T:], 0.0).then_inc(S["zero"], 1)

            @block.tensor
            def _(pe):
                pe.wait_ge(S["w"], 32)
                pe.wait_ge(S["tanh"], 1)
                pe.wait_ge(S["shifted"], RWK)
                for q in range(G):
                    for n in range(3):
                        i = 3 * q + n
                        if i >= 2:
                            pe.wait_ge(S["z_taken"], i - 1)
                        pe.matmul(B[i % 2][:, 0:C3], w2[0:64, q * P:(q + 1) * P], third(rw[0:64, 12, 0:T], n),
                                  start=True, stop=True).then_inc(S["z_made"], 1)
                        if i >= 2:
                            pe.wait_ge(S["a_taken"], i - 1)
                        pe.matmul(B[2 + i % 2][:, 0:C3], w2[64:128, q * P:(q + 1) * P], third(rw[64:128, 12, 0:T], n),
                                  start=True, stop=True).then_inc(S["a_made"], 1)
                for q in range(G):
                    pe.wait_ge(S["sq"], q + 1)
                    for n in range(3):
                        mm = pe.matmul(B[4 + n][32 * q:32 * q + 32, 0:C3], k.mask("pick", 32), third(tmp[:, q % 2, :], n),
                                       start=True, stop=True)
                    mm.then_inc(S["ss_made"], 1)
                for q in range(G):
                    for n in range(3):
                        i = 3 * q + n
                        pe.wait_ge(S["inv"], 3)
                        if i >= 4:
                            pe.wait_ge(S["bc_taken"], i - 3)
                        pe.matmul(B[i % 4][:, 0:C3], k.masks[32 * q:32 * q + 32, MK["spread"]:MK["spread"] + P],
                                  third(tmp[32 * q:32 * q + 32, 0, :], n), start=True, stop=True).then_inc(S["bc_made"], 1)

            @block.scalar
            def _(act):
                act.wait_ge(S["shifted"], 13)
                act.activation(rw[0:64, 12, 0:T], rw[0:64, 12, 0:T], ACT.Tanh).then_inc(S["tanh"], 1)
                act.wait_ge(S["half"], 1)
                act.wait_ge(S["zero"], 4)
                for q in range(G):
                    for n in range(3):
                        i = 3 * q + n
                        act.wait_ge(S["z_made"], i + 1)
                        act.activation(c[:, q, 1 + n * C3:1 + (n + 1) * C3], B[i % 2][:, 0:C3], ACT.Tanh,
                                       bias=hb[:, q:q + 1], scale=0.5).then_inc(S["z_taken"], 1)
                        act.wait_ge(S["a_made"], i + 1)
                        act.activation(a[:, q, n * C3:(n + 1) * C3], B[2 + i % 2][:, 0:C3], ACT.Tanh,
                                       bias=hb[:, G + q:G + q + 1], scale=0.5).then_inc(S["a_taken"], 1)
                for q in range(G):
                    act.wait_ge(S["kk"], q + 1)
                    if q >= 2:
                        act.wait_ge(S["ss_made"], q - 1)
                    act.activation(tmp[:, q % 2, :], kk[:, q, 0:T], ACT.Square).then_inc(S["sq"], 1)
                act.wait_ge(S["ss_made"], G)
                for n in range(3):
                    act.activation(tmp[:, 0, n * C3:(n + 1) * C3], B[4 + n][:, 0:C3], ACT.Sqrt).then_inc(S["root"], 1)

            @block.vector
            def _(dve):
                own = Chain(dve, S["own"])
                dve.wait_ge(S["in"], 32)
                dve.tensor_copy(last[:, :, 0:1], rw[:, :, TP - 1:TP]).then_inc(S["last"], 1)
                dve.tensor_copy(last[:, :, 1:], rw[:, :, TP + TSEQ - 1:T:TSEQ]).then_inc(S["last"], 1)
                dve.wait_ge(S["last"], 2)
                order = [12] + [m for m in range(RWK) if m != 12]
                for n, m in enumerate(order):
                    p, t = rw[:, m, :], tmp[:, n % 2, :]
                    own(dve.tensor_tensor(t[:, 1:T], p[:, 0:T - 1], p[:, 1:T], ALU.subtract))
                    dve.tensor_scalar(t[:, 0:1], p[:, 0:1], -1.0, None, ALU.mult)
                    own(dve.tensor_tensor(t[:, TP:T:TSEQ], sh0[:, m, :], p[:, TP:T:TSEQ], ALU.subtract))
                    dve.scalar_tensor_tensor(p[:, 0:T], t[:, 0:T], k.vec("rw_mu", m), p[:, 0:T], ALU.mult, ALU.add)\
                       .then_inc(S["shifted"], 13 if n == 0 else 1)
                own(dve.tensor_scalar(hb[:, 0:G], k.vecs[:, VEC["rw_w0"]:VEC["rw_w0"] + G], 0.5, None, ALU.mult))
                dve.tensor_scalar(hb[:, G:], k.vecs[:, VEC["rw_a0"]:VEC["rw_a0"] + G], 0.5, None, ALU.mult)\
                   .then_inc(S["half"], 1)
                dve.wait_ge(S["shifted"], 12 + RWK)
                for q in range(G):
                    dve.tensor_scalar(kk[:, q, 0:T], rw[:, 4 + q, 0:T], k.vec("rw_k_k", q), None, ALU.mult)\
                       .then_inc(S["kk"], 1)
                w = -0.5 * float(np.exp(-0.5))
                for q in range(G):
                    dve.wait_ge(S["z_taken"], 3 * (q + 1))
                    dve.wait_ge(S["a_taken"], 3 * (q + 1))
                    own(dve.tensor_scalar(c[:, q, 1:1 + T], c[:, q, 1:1 + T], w, w, ALU.mult, ALU.add))
                    own(dve.tensor_tensor_scan(c[:, q, 1:1 + TR], keep[:, :], c[:, q, 1:1 + TR], 0.0, ALU.mult, ALU.add))
                    own(dve.tensor_scalar(a[:, q, 0:T], a[:, q, 0:T], 0.5, 0.5, ALU.mult, ALU.add))
                for n in range(3):
                    t = tmp[:, 0, n * C3:(n + 1) * C3]
                    dve.wait_ge(S["root"], n + 1)
                    own(dve.tensor_scalar(t, t, 1e-12, None, ALU.max))
                    dve.reciprocal(t, t).then_inc(S["inv"], 1)
                dve.wait_ge(S["inv"], 3)
                for q in range(G):
                    for n in range(3):
                        x = third(kk[:, q, 0:T], n)
                        dve.wait_ge(S["bc_made"], 3 * q + n + 1)
                        dve.tensor_tensor(x, x, B[(3 * q + n) % 4][:, 0:C3], ALU.mult).then_inc(S["bc_taken"], 1)
                    t, kq, aq = tmp[:, 1, :], rw[:, 4 + q, 0:T], a[:, q, 0:T]
                    own(dve.tensor_scalar(t, aq, k.vec("rw_k_a", q), k.vec("rw_k_a", q), ALU.mult, ALU.subtract))
                    own(dve.scalar_tensor_tensor(kq, t, 1.0, kq, ALU.add, ALU.mult))
                    dve.wait_ge(S["bc_taken"], 3 * (q + 1))
                    own(dve.tensor_tensor(aq, aq, kk[:, q, 0:T], ALU.mult))


LEVELS = 6


def rwkv_chunk_stage(k, c, b, kk, keep, free_b, free_kk):
    nc, io, rw = k.nc, k.io, k.rw
    B = k.bank
    S = {n: k.sem(f"rc_{n}") for n in (
        "masks", "zero", "prev", "exp", "bd", "a_made", "vt_made", "a_taken", "l_taken", "vt_taken", 
        "kkt_taken", "lev_made", "n_taken", "t_taken", "mv_made", "mv_taken", "wt_made", "wt_taken", "sa_made", "sa_taken",
        "o_made", "o_taken", "st_made", "s1", "s_ready", "out",
        "ut_made", "ut_taken", "sb_zero", "sx_made", "sx_taken", "ex", "ns_made", "sum", "ns_done")}
    sb_in = [k.sem(f"rc_sb_in{j}") for j in range(2)]
    s_out = [k.sem(f"rc_s_out{j}") for j in range(2)]
    ps = k.psum[:, :].rearrange("p (b n) -> p b n", b=8)
    NT_, N_, TT_ = 0, 1, 2
    with ExitStack() as ctx:
        rm = k.sb(ctx, "rc_masks", [P, 2, 3, P])
        ex_ = k.sb(ctx, "rc_exp", [P, 2, 3, 4, CH])
        prev = k.sb(ctx, "rc_prev", [P, 4, CH])
        KR_ = k.sb(ctx, "rc_KR", [P, 2, 4, 2, P])
        BK_ = k.sb(ctx, "rc_BK", [P, 2, 4, 3, P])
        A4 = k.sb(ctx, "rc_A4", [P, 4, 4, P])
        W = k.sb(ctx, "rc_W", [P, 4, 3, P])
        tm = k.sb(ctx, "rc_tm", [P, 4, 4, P])
        MV = k.sb(ctx, "rc_MV", [P, 4, P])
        WT = k.sb(ctx, "rc_WT", [P, 4, P])
        SA = k.sb(ctx, "rc_SA", [P, 4, P])
        St = k.sb(ctx, "rc_S", [P, 4, P])
        S1 = k.sb(ctx, "rc_S1", [P, 4, P])

        def pe_common(pe, c_, sl):
            KR, BK = KR_[:, sl], BK_[:, sl]
            pe.wait_ge(S["bd"], 10 * (c_ + 1))
            for hf in range(2):
                for p in (2 * hf, 2 * hf + 1):
                    kr = KR[:, p].rearrange("p a n -> p (a n)")
                    pe.matmul(B[4 + p][:, 0:256], BK[:, p, 0, :], kr, start=True, stop=True)
                    pe.matmul(B[4 + p][:, 256:512], BK[:, p, 1, :], kr, start=True, stop=True)
                pe.wait_ge(S["s_ready"], 4 * (c_ + 1))
                pe.wait_ge(S["o_taken"], 4 * (c_ + 1))
                for p in (2 * hf, 2 * hf + 1):
                    mm = pe.matmul(B[p][:, 0:P], KR[:, p, 0, :], BK[:, p, 0, :], start=True, stop=True)
                mm.then_inc(S["a_made"], 1)
                for p in (2 * hf, 2 * hf + 1):
                    for j in range(3):
                        mm = pe.transpose(B[p][:, (1 + j) * P:(2 + j) * P], BK[:, p, j, :], k.mask("ident"))
                mm.then_inc(S["vt_made"], 1)
            for lev in range(LEVELS):
                for hf in range(2):
                    i = 2 * c_ + hf + 1
                    if lev == 0:
                        pe.wait_ge(S["a_taken"], i)
                        pe.wait_ge(S["l_taken"], i)
                    else:
                        if lev == 1:
                            pe.wait_ge(S["mv_taken"], i)
                            pe.wait_ge(S["kkt_taken"], i)
                        pe.wait_ge(S["n_taken"], 10 * c_ + 2 * (lev - 1) + hf + 1)
                        pe.wait_ge(S["t_taken"], 12 * c_ + 2 * (lev - 1) + hf + 1)
                    for p in (2 * hf, 2 * hf + 1):
                        o = B[4 + p]
                        if lev == 0:
                            pe.matmul(o[:, 0:P], W[:, p, N_, :], A4[:, p, 0, :], start=True, stop=True)
                            pe.matmul(o[:, P:256], A4[:, p, 0, :], W[:, p, N_, :], start=True, stop=True)
                            mm = pe.transpose(o[:, 384:512], KR[:, p, 0, :], k.mask("ident"))
                            continue
                        mm = pe.matmul(B[p][:, 0:P], W[:, p, N_, :], W[:, p, TT_, :], start=True, stop=True)
                        if lev < LEVELS - 2:
                            pe.matmul(o[:, 0:P], W[:, p, N_, :], W[:, p, NT_, :], start=True, stop=True)
                        if lev < LEVELS - 1:
                            mm = pe.matmul(o[:, P:256], W[:, p, NT_, :], W[:, p, N_, :], start=True, stop=True)
                    mm.then_inc(S["lev_made"], 1)
                    if lev == 0:
                        pe.wait_ge(S["vt_taken"], i)
                        for p in (2 * hf, 2 * hf + 1):
                            mm = pe.matmul(B[p][:, 0:P], A4[:, p, 2, :], tm[:, p, 2, :], start=True, stop=True)
                        mm.then_inc(S["mv_made"], 1)
            for hf in range(2):
                i = 2 * c_ + hf + 1
                pe.wait_ge(S["t_taken"], 12 * c_ + 10 + hf + 1)
                pe.wait_ge(S["kkt_taken"], i)
                for p in (2 * hf, 2 * hf + 1):
                    mm = pe.matmul(B[p][:, P:2 * P], tm[:, p, 3, :], W[:, p, TT_, :], start=True, stop=True)
                mm.then_inc(S["wt_made"], 1)

        def exponential(act, c_, sl, n):
            tok = bass.ds(1 + c_ * CH, CH)
            if n == 0:
                act.wait_ge(S["s_ready"], 4 * c_ if not isinstance(c_, int) or c_ else 4)
                act.activation(ex_[:, sl, 0], c[:, :, tok], ACT.Exp).then_inc(S["exp"], 1)
            elif n == 1:
                act.activation(ex_[:, sl, 1], c[:, :, tok], ACT.Exp, scale=-1.0).then_inc(S["exp"], 1)
            else:
                act.wait_ge(S["prev"], c_ + 1)
                act.activation(ex_[:, sl, 2], prev[:, :, :], ACT.Exp).then_inc(S["exp"], 1)

        def act_common(act, c_, sl, ahead=True):
            for hf in range(2):
                i, pp = 2 * c_ + hf + 1, slice(2 * hf, 2 * hf + 2)
                act.wait_ge(S["l_taken"], i)
                act.activation(tm[:, pp, 0:3, :].rearrange("p a b n -> p a (b n)"), ps[:, pp, P:512], ACT.Copy)\
                   .then_inc(S["vt_taken"], 1)
            for lev in range(LEVELS - 1):
                for hf in range(2):
                    i, pp = 2 * c_ + hf + 1, slice(2 * hf, 2 * hf + 2)
                    bk = slice(4 + 2 * hf, 6 + 2 * hf)
                    act.wait_ge(S["lev_made"], 12 * c_ + 2 * lev + hf + 1)
                    if lev < LEVELS - 2:
                        act.activation(W[:, pp, 0:2, :].rearrange("p b a n -> p b (a n)"), ps[:, bk, 0:256], ACT.Copy)\
                           .then_inc(S["n_taken"], 1)
                    else:
                        act.activation(W[:, pp, N_, :], ps[:, bk, P:256], ACT.Copy).then_inc(S["n_taken"], 1)
                    if lev == 0:
                        act.activation(tm[:, pp, 3, :], ps[:, bk, 384:512], ACT.Copy).then_inc(S["kkt_taken"], 1)
                        act.wait_ge(S["mv_made"], i)
                        act.activation(MV[:, pp, :], ps[:, pp, 0:P], ACT.Copy).then_inc(S["mv_taken"], 1)
                if ahead and lev < 3:
                    exponential(act, c_ + 1, 1 - sl, lev)
            for hf in range(2):
                pp = slice(2 * hf, 2 * hf + 2)
                act.wait_ge(S["wt_made"], 2 * c_ + hf + 1)
                act.activation(WT[:, pp, :], ps[:, pp, P:2 * P], ACT.Copy).then_inc(S["wt_taken"], 1)

        def decay_before(dve, c_):
            tok = bass.ds(c_ * CH, CH)
            dve.tensor_tensor(prev[:, :, :], c[:, :, tok], keep[:, tok].unsqueeze(1).broadcast_to([P, 4, CH]), ALU.mult)\
               .then_inc(S["prev"], 1)

        def scaled(dve, c_, sl, n):
            tok = bass.ds(c_ * CH, CH)
            KR, BK, ex = KR_[:, sl], BK_[:, sl], ex_[:, sl]
            for hh in range(2):
                h, o = slice(hh * CH, (hh + 1) * CH), slice(hh * CH, (hh + 1) * CH)
                if n == 0:
                    ins = dve.tensor_copy(BK[h, :, 2, o], rw[h, 8:12, tok])
                elif n == 1:
                    dve.wait_ge(S["exp"], 3 * c_ + 1)
                    ins = dve.tensor_tensor(KR[h, :, 1, o], rw[h, 0:4, tok], ex[h, 0], ALU.mult)
                elif n == 2:
                    dve.wait_ge(S["exp"], 3 * c_ + 2)
                    ins = dve.tensor_tensor(BK[h, :, 0, o], b[h, :, tok], ex[h, 1], ALU.mult)
                elif n == 3:
                    ins = dve.tensor_tensor(BK[h, :, 1, o], rw[h, 4:8, tok], ex[h, 1], ALU.mult)
                else:
                    dve.wait_ge(S["exp"], 3 * c_ + 3)
                    ins = dve.tensor_tensor(KR[h, :, 0, o], kk[h, :, tok], ex[h, 2], ALU.mult)
                ins.then_inc(S["bd"], 1)

        def dve_common(dve, c_, sl, g, ahead=True):
            if ahead:
                decay_before(dve, c_ + 1)
            for hf in range(2):
                i, pp, bk = 2 * c_ + hf + 1, slice(2 * hf, 2 * hf + 2), slice(4 + 2 * hf, 6 + 2 * hf)
                dve.wait_ge(S["a_made"], i)
                for j in range(2):
                    q = slice(2 * j, 2 * j + 2)
                    last = dve.tensor_tensor(
                        A4[:, pp, q, :].rearrange("p b a n -> p b (a n)"), ps[:, bk, 256 * j:256 * (j + 1)],
                        rm[:, g, 1:3, :].rearrange("p a n -> p (a n)").unsqueeze(1).broadcast_to([P, 2, 256]), ALU.mult)
                last.then_inc(S["a_taken"], 1)
                dve.wait_ge(S["vt_made"], i)
                dve.tensor_tensor(W[:, pp, N_, :], ps[:, pp, 0:P], rm[:, g, 0, :].unsqueeze(1).broadcast_to([P, 2, P]),
                                  ALU.mult).then_inc(S["l_taken"], 1)
                dve.wait_ge(S["a_taken"], i)
                dve.scalar_tensor_tensor(W[:, pp, TT_, :], A4[:, pp, 0, :], -1.0,
                                         k.mask("ident").unsqueeze(1).broadcast_to([P, 2, P]), ALU.mult, ALU.add)\
                   .then_inc(S["t_taken"], 1)
            for lev in range(1, LEVELS):
                for hf in range(2):
                    pp, bk = slice(2 * hf, 2 * hf + 2), slice(4 + 2 * hf, 6 + 2 * hf)
                    dve.wait_ge(S["lev_made"], 12 * c_ + 2 * lev + hf + 1)
                    dve.wait_ge(S["t_taken"], 12 * c_ + 2 * (lev - 1) + hf + 1)
                    dve.tensor_tensor(W[:, pp, TT_, :], W[:, pp, TT_, :], ps[:, pp, 0:P], ALU.add)\
                       .then_inc(S["t_taken"], 1)
                if ahead:
                    scaled(dve, c_ + 1, 1 - sl, lev - 1)

        with nc.Block() as block:
            @block.sync
            def _(sp):
                sp.dma_start(rm[:, :, :, :].rearrange("p a b n -> p (a b n)"), io["rwmasks"]).then_inc(S["masks"], 16)
                sp.wait_ge(S["s_ready"], 4 * (NCH + 1))
                for j in range(2):
                    h = slice(j * HD, (j + 1) * HD)
                    sp.dma_start(io["o_rwkv_p"].rearrange("(q j) k v -> j k q v", j=2)[j], St[h, :, h]).then_inc(S["out"], 16)
                sp.wait_ge(S["out"], 32)

            @block.gpsimd
            def _(pool):
                pool.memset(KR_[:, :, :, :, :], 0.0).then_inc(S["zero"], 1)
                pool.memset(BK_[:, :, :, :, :], 0.0).then_inc(S["zero"], 1)
                pool.memset(St[:, :, :], 0.0).then_inc(S["zero"], 1)

            @block.tensor
            def _(pe):
                pe.wait_ge(S["zero"], 3)

                def chunk(c_, sl):
                    KR = KR_[:, sl]
                    pe_common(pe, c_, sl)
                    for hf in range(2):
                        i = 2 * c_ + hf + 1
                        pe.wait_ge(S["mv_taken"], i)
                        pe.wait_ge(S["wt_taken"], i)
                        for p in (2 * hf, 2 * hf + 1):
                            pe.matmul(B[p][:, 256:384], W[:, p, TT_, :], MV[:, p, :], start=True, stop=False)
                            mm = pe.matmul(B[p][:, 256:384], WT[:, p, :], St[:, p, :], start=False, stop=True)
                        mm.then_inc(S["sa_made"], 1)
                    for hf in range(2):
                        i = 2 * c_ + hf + 1
                        pe.wait_ge(S["sa_taken"], i)
                        for p in (2 * hf, 2 * hf + 1):
                            pe.matmul(B[p][:, 0:P], tm[:, p, 0, :], SA[:, p, :], start=True, stop=False)
                            mm = pe.matmul(B[p][:, 0:P], tm[:, p, 1, :], tm[:, p, 2, :], start=False, stop=True)
                            pe.matmul(B[p][:, 384:512], St[:, p, :], KR[:, p, 1, :], start=True, stop=False)
                            pe.matmul(B[p][:, 384:512], SA[:, p, :], A4[:, p, 1, :], start=False, stop=False)
                            mm = pe.matmul(B[p][:, 384:512], tm[:, p, 2, :], A4[:, p, 3, :], start=False, stop=True)
                        mm.then_inc(S["o_made"], 1)
                with pe.Fori(0, NCH // 2) as i:
                    chunk(2 * i, 0)
                    chunk(2 * i + 1, 1)

            @block.scalar
            def _(act):
                def chunk(c_, sl):
                    act_common(act, c_, sl)
                    act.wait_ge(S["exp"], 3 * (c_ + 1))
                    act.wait_ge(S["s_ready"], 4 * (c_ + 1))
                    for p in range(4):
                        act.activation(S1[:, p, :], St[:, p, :], ACT.Copy, scale=ex_[:, sl, 0, p, CH - 1:CH]).then_inc(S["s1"], 1)
                for n in range(3):
                    exponential(act, 0, 0, n)
                with act.Fori(0, NCH // 2) as i:
                    chunk(2 * i, 0)
                    chunk(2 * i + 1, 1)

            @block.vector
            def _(dve):
                dve.wait_ge(S["masks"], 16)
                dve.wait_ge(S["zero"], 3)
                dve.sem_inc(S["s_ready"], 4)
                dve.sem_inc(S["o_taken"], 4)

                def chunk(c_, sl):
                    ex = ex_[:, sl]
                    dve_common(dve, c_, sl, 0)
                    for hf in range(2):
                        pp = slice(2 * hf, 2 * hf + 2)
                        dve.wait_ge(S["sa_made"], 2 * c_ + hf + 1)
                        dve.tensor_scalar(SA[:, pp, :], ps[:, pp, 256:384], -1.0, None, ALU.mult).then_inc(S["sa_taken"], 1)
                    dve.wait_ge(S["s1"], 4 * (c_ + 1))
                    for hf in range(2):
                        dve.wait_ge(S["o_made"], 2 * c_ + hf + 1)
                        for p in (2 * hf, 2 * hf + 1):
                            dve.scalar_tensor_tensor(St[:, p, :], B[p][:, 0:P], ex[:, 0, p, CH - 1:CH], S1[:, p, :],
                                                     ALU.mult, ALU.add).then_inc(S["s_ready"], 1)
                        for hh in range(2):
                            h, pp = slice(hh * HD, (hh + 1) * HD), slice(2 * hf, 2 * hf + 2)
                            dve.tensor_copy(c[h, pp, bass.ds(1 + c_ * CH, CH)], ps[h, pp, 384 + hh * CH:384 + (hh + 1) * CH])\
                               .then_inc(S["o_taken"], 1)
                decay_before(dve, 0)
                for n in range(5):
                    scaled(dve, 0, 0, n)
                with dve.Fori(0, NCH // 2) as i:
                    chunk(2 * i, 0)
                    chunk(2 * i + 1, 1)

        SB = k.at(free_b, "rc_SB", [P, 2, NB, P])
        EX = k.at(free_kk, "rc_EX", [P, 2, NB, P])
        bm = k.sb(ctx, "rc_bm", [P, NB])
        G = NCH
        KR, ex = KR_[:, 0], ex_[:, 0]
        with nc.Block() as block:
            @block.sync
            def _(sp):
                sp.dma_start(bm[:, :], io["batchmask"]).then_inc(S["masks"], 16)
                sp.wait_ge(S["sb_zero"], 1)
                for p in range(4):
                    if p >= 2:
                        sp.wait_ge(s_out[p % 2], 32)
                    for j in range(2):
                        h = slice(j * HD, (j + 1) * HD)
                        sp.dma_start(SB[h, p % 2, :, h], io["s0"][:, 2 * p + j].rearrange("b k v -> k b v"))\
                          .then_inc(sb_in[p % 2], 16)

            @block.gpsimd
            def _(pool):
                pool.memset(SB[:, :, :, :], 0.0).then_inc(S["sb_zero"], 1)
                for p in range(4):
                    pool.wait_ge(S["ns_done"], p + 1)
                    for j in range(2):
                        h = slice(j * HD, (j + 1) * HD)
                        pool.dma_start(io["o_rwkv_s"][:, 2 * p + j].rearrange("b k v -> k b v"), SB[h, p % 2, :, h])\
                            .then_inc(s_out[p % 2], 16)
                for j in range(2):
                    pool.wait_ge(s_out[j], 64)

            @block.tensor
            def _(pe):
                pe_common(pe, G, 0)
                for p in range(4):
                    own = (2 * G + p // 2 + 1)
                    pe.wait_ge(S["mv_taken"], own)
                    pe.wait_ge(S["wt_taken"], own)
                    pe.wait_ge(sb_in[p % 2], 32 * (p // 2 + 1))
                    sa = B[p][:, 256:384]
                    sav = sa.rearrange("p (h t) -> p h t", h=2)
                    wt = WT[:, p, :].rearrange("p (h t) -> p h t", h=2)
                    r = KR[:, p, 1, :].rearrange("p (h t) -> p h t", h=2)
                    pe.matmul(sa, MV[:, p, :], W[:, p, TT_, :], start=True, stop=True)
                    for n in range(NB):
                        t = slice(n * TSEQ, (n + 1) * TSEQ)
                        mm = pe.matmul(sav[:, :, t], SB[:, p % 2, n, :], wt[:, :, t], start=False, stop=True,
                                       skip_group_check=True)
                    mm.then_inc(S["ut_made"], 1)
                    pe.wait_ge(S["ut_taken"], p + 1)
                    pe.transpose(B[p][:, P:2 * P], S1[:, p, :], k.mask("ident")).then_inc(S["sx_made"], 1)
                    pe.wait_ge(S["sx_taken"], p + 1)
                    o = B[p][:, 384:512]
                    ov = o.rearrange("p (h t) -> p h t", h=2)
                    pe.matmul(o, SA[:, p, :], A4[:, p, 1, :], start=True, stop=False)
                    pe.matmul(o, tm[:, p, 2, :], A4[:, p, 3, :], start=False, stop=True)
                    for n in range(NB):
                        t = slice(n * TSEQ, (n + 1) * TSEQ)
                        mm = pe.matmul(ov[:, :, t], SB[:, p % 2, n, :], r[:, :, t], start=False, stop=True,
                                       skip_group_check=True)
                    mm.then_inc(S["o_made"], 1)
                    pe.wait_ge(S["ex"], 2 * (p + 1))
                    if p >= 2:
                        pe.wait_ge(S["sum"], p - 1)
                    for n in range(2):
                        o = B[4 + 2 * (p % 2) + n]
                        bt = slice(4 * n, 4 * n + 4)
                        pe.matmul(o, tm[:, p, 0, :], EX[:, 0, bt, :].rearrange("p b v -> p (b v)"), start=True, stop=False)
                        mm = pe.matmul(o, tm[:, p, 1, :], EX[:, 1, bt, :].rearrange("p b v -> p (b v)"), start=False, stop=True)
                    mm.then_inc(S["ns_made"], 1)

            @block.scalar
            def _(act):
                act_common(act, G, 0, False)
                for p in range(4):
                    act.wait_ge(S["sx_made"], p + 1)
                    act.activation(SA[:, p, :], B[p][:, P:2 * P], ACT.Copy).then_inc(S["sx_taken"], 1)

            @block.vector
            def _(dve):
                dve.wait_ge(S["masks"], 32)
                dve_common(dve, G, 0, 1, False)
                for p in range(4):
                    dve.wait_ge(S["ut_made"], p + 1)
                    dve.tensor_scalar(S1[:, p, :], B[p][:, 256:384], -1.0, None, ALU.mult).then_inc(S["ut_taken"], 1)
                    dve.wait_ge(S["sx_taken"], p + 1)
                    if p >= 1:
                        dve.wait_ge(S["ns_made"], p)
                    for j, x in enumerate((SA[:, p, :], tm[:, p, 2, :])):
                        dve.tensor_tensor(EX[:, j], x.unsqueeze(1).broadcast_to([P, NB, P]),
                                          bm[:, :].unsqueeze(2).broadcast_to([P, NB, P]), ALU.mult).then_inc(S["ex"], 1)
                    dve.wait_ge(S["o_made"], 2 * NCH + p + 1)
                    for hh in range(2):
                        h = slice(hh * HD, (hh + 1) * HD)
                        dve.tensor_copy(c[h, p, 1 + TP:1 + T], B[p][h, 384 + hh * CH:384 + hh * CH + TS])
                    dve.wait_ge(S["ns_made"], p + 1)
                    sb = SB[:, p % 2]
                    new = ps[:, 4 + 2 * (p % 2):6 + 2 * (p % 2), :].rearrange("p a n -> p (a n)").rearrange("p (b v) -> p b v", b=NB)
                    dve.tensor_tensor(sb, sb, new, ALU.add).then_inc(S["sum"], 1)
                    dve.wait_ge(S["sum"], p + 1)
                    end = ex[:, 0, p, TSEQ - 1:TS:TSEQ]
                    dve.tensor_tensor(sb, sb, end.unsqueeze(2).broadcast_to([P, NB, P]), ALU.mult).then_inc(S["ns_done"], 1)


def rwkv_out_stage(k, y):
    nc, io, rw = k.nc, k.io, k.rw
    B = k.bank
    S = {n: k.sem(f"ro_{n}") for n in ("w", "sig", "gated", "mean", "c_done", "sq", "var", "root", "inv", "rk", "made",
                                       "own", "aff")}
    Y = lambda q, n=None: y[:, q, 1:1 + T] if n is None else y[:, q, 1 + n * C3:1 + (n + 1) * C3]
    G = 4
    with ExitStack() as ctx:
        g2 = k.sb(ctx, "ro_g2", [P, 512])
        sq = k.sb(ctx, "ro_sq", [P, 2, T])
        inv = k.sb(ctx, "ro_inv", [P, T])
        rk = k.sb(ctx, "ro_rk", [P, 2, T])
        t = k.sb(ctx, "ro_t", [P, 2, C3])
        with nc.Block() as block:
            @block.sync
            def _(sp):
                sp.dma_start(g2[:, :], io["rw_g2"]).then_inc(S["w"], 16)

            @block.tensor
            def _(pe):
                for q in range(G):
                    for n in range(3):
                        i = 3 * q + n
                        if i >= 4:
                            pe.wait_ge(S["c_done"], i - 3)
                        pe.matmul(B[i % 4][:, 0:C3], k.mask("headones"), Y(q, n), start=True, stop=True).then_inc(S["mean"], 1)
                for q in range(G):
                    pe.wait_ge(S["sq"], q + 1)
                    for n in range(3):
                        mm = pe.matmul(B[4 + n][32 * q:32 * q + 32, 0:C3], k.mask("pick", 32), third(sq[:, q % 2, :], n),
                                       start=True, stop=True)
                    mm.then_inc(S["var"], 1)
                pe.wait_ge(S["inv"], 3)
                pe.wait_ge(S["w"], 16)
                pe.wait_ge(S["gated"], 1)
                pe.wait_ge(S["c_done"], 3 * G)
                for q in range(G):
                    pe.wait_ge(S["rk"], q + 1)
                    for n in range(3):
                        i = 3 * q + n
                        j = 3 * (i % 2)
                        if i >= 2:
                            pe.wait_ge(S["own"], i - 1)
                        pe.matmul(B[j][:, 0:C3], k.masks[32 * q:32 * q + 32, MK["spread"]:MK["spread"] + P],
                                  third(inv[32 * q:32 * q + 32, :], n), start=True, stop=True)
                        pe.matmul(B[j + 1][:, 0:C3], k.mask("headones"), third(rk[:, q % 2, :], n), start=True, stop=True)
                        pe.matmul(B[j + 2][:, 0:C3], g2[:, q * P:(q + 1) * P], third(rw[:, 13, 0:T], n),
                                  start=True, stop=True).then_inc(S["made"], 1)

            @block.scalar
            def _(act):
                act.activation(rw[:, 13, 0:T], rw[:, 13, 0:T], ACT.Tanh, scale=0.5).then_inc(S["sig"], 1)
                for q in range(G):
                    act.wait_ge(S["c_done"], 3 * (q + 1))
                    if q >= 2:
                        act.wait_ge(S["var"], q - 1)
                    act.activation(sq[:, q % 2, :], Y(q), ACT.Square).then_inc(S["sq"], 1)
                act.wait_ge(S["var"], G)
                for n in range(3):
                    act.activation(third(inv, n), B[4 + n][:, 0:C3], ACT.Sqrt, bias=k.mask("lnx_eps", 1), scale=1.0 / HD)\
                       .then_inc(S["root"], 1)

            @block.vector
            def _(dve):
                dve.wait_ge(S["sig"], 1)
                dve.tensor_scalar(rw[:, 13, 0:T], rw[:, 13, 0:T], 0.5, 0.5, ALU.mult, ALU.add).then_inc(S["gated"], 1)

                def bonus(q):
                    if q >= 2:
                        dve.wait_ge(S["made"], 3 * (q - 1))
                    dve.scalar_tensor_tensor(rk[:, q % 2, :], rw[:, q, 0:T], k.vec("rw_r_k", q), rw[:, 4 + q, 0:T],
                                             ALU.mult, ALU.mult).then_inc(S["rk"], 1)
                for q in range(G):
                    for n in range(3):
                        i = 3 * q + n
                        dve.wait_ge(S["mean"], i + 1)
                        dve.scalar_tensor_tensor(Y(q, n), B[i % 4][:, 0:C3], -1.0 / HD, Y(q, n), ALU.mult, ALU.add)\
                           .then_inc(S["c_done"], 1)
                bonus(0)
                bonus(1)
                for n in range(3):
                    dve.wait_ge(S["root"], n + 1)
                    dve.reciprocal(third(inv, n), third(inv, n)).then_inc(S["inv"], 1)
                step = Chain(dve, S["aff"])
                for q in range(G):
                    if q >= 2:
                        bonus(q)
                    for n in range(3):
                        i = 3 * q + n
                        j = 3 * (i % 2)
                        dve.wait_ge(S["made"], i + 1)
                        u, v = t[:, 0, :], third(rw[:, 8 + q, 0:T], n)
                        step(dve.tensor_tensor(Y(q, n), Y(q, n), B[j][:, 0:C3], ALU.mult))
                        dve.tensor_tensor(u, v, B[j + 1][:, 0:C3], ALU.mult)
                        step(dve.tensor_scalar(Y(q, n), Y(q, n), k.vec("rw_lnx_g", q), k.vec("rw_lnx_b", q), ALU.mult, ALU.add))
                        step(dve.tensor_tensor(Y(q, n), Y(q, n), u, ALU.add))
                        dve.tensor_tensor(Y(q, n), Y(q, n), B[j + 2][:, 0:C3], ALU.mult).then_inc(S["own"], 1)


def residual(k):
    def ep(eng, m, n, ps):
        xs = k.x[:, bass.ds(m, 1), n * C3:(n + 1) * C3].rearrange("p a t -> p (a t)")
        return eng.tensor_tensor(xs, xs, ps, ALU.add)
    return ep


def memory_kv_stage(k, kmT, vm):
    nc, io = k.nc, k.io
    S = {n: k.sem(f"mk_{n}") for n in ("in", "w", "v_made", "v_taken", "out")}
    with ExitStack() as ctx:
        mem = k.sb(ctx, "mk_mem", [P, DK, NM])
        wv = k.sb(ctx, "mk_wv", [P, DK, D])
        with nc.Block() as block:
            @block.sync
            def _(sp):
                sp.dma_start(mem[:, :, :], io["memT"].rearrange("(k p) m -> p k m", p=P)).then_inc(S["in"], 16)
                sp.dma_start(wv[:, :, :], io["w_mv"].rearrange("(k p) m -> p k m", p=P)).then_inc(S["w"], 16)
                sp.wait_ge(S["in"], 16)
        rms_stage(k, "nmem", mem, DK, "g_mem_kv", mem, D, T_=NM, cols=(NM, 1))

        def ep(eng, m, j, n, ps):
            return eng.activation(kmT[:, bass.ds(m, 1), :], ps, ACT.Copy)
        memory_keys_stage(k, "mk", io["w_mk"], DK, DK, lambda kk, n: mem[:, kk, :], ep, engine="scalar", cols=(NM, 1))
        with nc.Block() as block:
            @block.tensor
            def _(pe):
                pe.wait_ge(S["w"], 16)
                for mt in range(2):
                    for n in range(2):
                        for kk in range(DK):
                            mm = pe.matmul(k.bank[2 * mt + n], mem[:, kk, mt * P:(mt + 1) * P], wv[:, kk, n * 512:(n + 1) * 512],
                                           start=(kk == 0), stop=(kk == DK - 1))
                        mm.then_inc(S["v_made"], 1)

            @block.scalar
            def _(act):
                for mt in range(2):
                    for n in range(2):
                        act.wait_ge(S["v_made"], 2 * mt + n + 1)
                        act.activation(vm[:, mt, n * 512:(n + 1) * 512], k.bank[2 * mt + n], ACT.Copy).then_inc(S["v_taken"], 1)

            @block.sync
            def _(sp):
                sp.dma_start(io["o_memk"].rearrange("(k p) m -> p k m", p=P), kmT[:, :, :]).then_inc(S["out"], 16)
                sp.wait_ge(S["v_taken"], 4)
                sp.dma_start(io["o_memv"].rearrange("(a p) d -> p a d", p=P), vm[:, :, :]).then_inc(S["out"], 16)
                sp.wait_ge(S["out"], 32)


def memory_attention_stage(k, q, kmT, vm, H, L):
    nc, io = k.nc, k.io
    B = k.bank
    N = TILES
    assert N == NB
    names = ("s_made", "maxed", "m_ready", "e_done", "r_done", "p_scaled", "t_made", "t_taken", "o_made", "o_high", "o_taken")
    S = {n: k.sem(f"ma_{n}") for n in names + ("q_there",)}
    Z = {n: k.sem(f"mz_{n}") for n in names}
    kv_in = [k.sem(f"mz_kv{j}") for j in range(2)]
    HALF = MH // 2
    with ExitStack() as ctx:
        qt = k.sb(ctx, "ma_q", [P, 2, DK, P])
        pr = k.sb(ctx, "ma_p", [P, 2, MH, NM])
        pT = k.sb(ctx, "ma_pT", [P, MH, 2, P])
        st = k.sb(ctx, "ma_st", [P, 2, 4, MH])
        ks = k.sb(ctx, "mz_k", [P, 2, DK, NM])
        vs = k.sb(ctx, "mz_v", [P, 2, 2, D])
        zpr = k.sb(ctx, "mz_p", [P, NM])
        zpT = k.sb(ctx, "mz_pT", [P, 2, P])
        zst = k.sb(ctx, "mz_st", [P, 4])
        z_s, z_t, z_o = B[5][:, 0:NM], B[5][:, NM:2 * NM], B[5][:, 0:DK * TSEQ]

        def steps(eng, step):
            with eng.Fori(0, N // 2 - 2) as it:
                for j in range(2):
                    step(2 * it + j, j, True, True, True)
            for i in range(N - 4, N):
                step(i, i % 2, i + 1 < N, i + 2 < N, i + 3 < N)
        with nc.Block() as block:
            @block.sync
            def _(sp):
                def load(b, j):
                    bb = bass.ds(b, 1)
                    sp.dma_start(ks[:, j], io["memk"][bb].rearrange("a (k p) m -> p (a k) m", p=P)).then_inc(kv_in[j], 16)
                    sp.dma_start(vs[:, j], io["memv"][bb].rearrange("a (k p) d -> p (a k) d", p=P)).then_inc(kv_in[j], 16)
                load(0, 0)
                load(1, 1)
                with sp.Fori(1, NB // 2) as it:
                    for j in range(2):
                        sp.wait_ge(Z["o_made"], 2 * it + j - 1)
                        load(2 * it + j, j)

            @block.tensor
            def _(pe):
                def scores(i, j):
                    pe.wait_ge(S["q_there"], i + 1)
                    for h in range(MH):
                        for dk in range(2):
                            mm = pe.matmul(B[2 * j + h // 2][:, h % 2 * NM:(h % 2 + 1) * NM], qt[:, j, 2 * h + dk, :],
                                           kmT[:, 2 * h + dk, :], start=(dk == 0), stop=(dk == 1))
                    mm.then_inc(S["s_made"], 1)

                def transposes(i, j, a):
                    pe.wait_ge(S["p_scaled"], i + 1)
                    pe.wait_ge(S["t_taken"], 2 * i + a + 1)
                    for h in range(HALF * a, HALF * (a + 1)):
                        for mt in range(2):
                            mm = pe.transpose(B[4][:, (h % 2 * 2 + mt) * P:(h % 2 * 2 + mt + 1) * P],
                                              pr[:, j, h, mt * P:(mt + 1) * P], k.mask("ident"))
                    mm.then_inc(S["t_made"], 1)

                def values(i, a):
                    pe.wait_ge(S["t_taken"], 2 * i + a + 2)
                    pe.wait_ge(S["o_taken"], 2 * i + a + 1)
                    for c in range(4 * a, 4 * a + 4):
                        for mt in range(2):
                            mm = pe.matmul(B[6 + a][:, c % 4 * P:(c % 4 + 1) * P], vm[:, mt, c * P:(c + 1) * P],
                                           pT[:, c // 2, mt, :], start=(mt == 0), stop=(mt == 1))
                    mm.then_inc(S["o_made"], 1)

                def step(i, j, next1, next2, next3):
                    pe.wait_ge(kv_in[j], 16 * (i - j + 2))
                    pe.wait_ge(Z["o_taken"], i + 1)
                    for h in range(MH):
                        for dk in range(2):
                            mm = pe.matmul(z_s[32 * h:32 * h + 32, :], q[:, 2 * h + dk, TP:T], ks[:, j, 2 * h + dk, :],
                                           start=(dk == 0), stop=(dk == 1))
                    mm.then_inc(Z["s_made"], 1)
                    transposes(i, j, 0)
                    if next2:
                        scores(i + 2, j)
                    pe.wait_ge(Z["p_scaled"], i + 1)
                    for mt in range(2):
                        mm = pe.transpose(z_t[:, mt * P:(mt + 1) * P], zpr[:, mt * P:(mt + 1) * P], k.mask("ident"))
                    mm.then_inc(Z["t_made"], 1)
                    transposes(i, j, 1)
                    values(i, 0)
                    pe.wait_ge(Z["t_taken"], i + 1)
                    for c in range(DK):
                        for mt in range(2):
                            mm = pe.matmul(z_o[:, c * TSEQ:(c + 1) * TSEQ], vs[:, j, mt, c * P:(c + 1) * P],
                                           zpT[:, mt, bass.ds(c // 2 * TS + i * TSEQ, TSEQ)], start=(mt == 0), stop=(mt == 1))
                    mm.then_inc(Z["o_made"], 1)
                    values(i, 1)
                scores(0, 0)
                scores(1, 1)
                steps(pe, step)

            @block.scalar
            def _(act):
                act.sem_inc(S["t_taken"], 1)

                def queries(i, j):
                    act.wait_ge(S["s_made"], i - 1)
                    act.activation(qt[:, j, :, :], q[:, :, bass.ds(i * P, P)], ACT.Copy).then_inc(S["q_there"], 1)

                def exponentials(i, j):
                    act.wait_ge(S["m_ready"], i + 1)
                    for h in range(MH):
                        act.activation(pr[:, j, h, :], B[2 * j + h // 2][:, h % 2 * NM:(h % 2 + 1) * NM], ACT.Exp,
                                       bias=st[:, j, 1, h:h + 1], scale=MSCALE, accum_out=st[:, j, 2, h:h + 1])\
                           .then_inc(S["e_done"], 1)

                def turned(i, a):
                    act.wait_ge(S["t_made"], 2 * i + a + 1)
                    act.activation(pT[:, HALF * a:HALF * (a + 1), :, :].rearrange("p h a n -> p (h a n)"), B[4], ACT.Copy)\
                       .then_inc(S["t_taken"], 1)

                def step(i, j, next1, next2, next3):
                    turned(i, 0)
                    act.wait_ge(Z["m_ready"], i + 1)
                    act.activation(zpr[:, :], z_s, ACT.Exp, bias=zst[:, 1:2], scale=MSCALE, accum_out=zst[:, 2:3])\
                       .then_inc(Z["e_done"], 1)
                    if next1:
                        exponentials(i + 1, 1 - j)
                    act.wait_ge(Z["t_made"], i + 1)
                    act.activation(zpT[:, :, :].rearrange("p a n -> p (a n)"), z_t, ACT.Copy).then_inc(Z["t_taken"], 1)
                    turned(i, 1)
                    if next3:
                        queries(i + 3, 1 - j)
                for i in range(2):
                    act.activation(qt[:, i, :, :], q[:, :, i * P:(i + 1) * P], ACT.Copy).then_inc(S["q_there"], 1)
                exponentials(0, 0)
                queries(2, 0)
                steps(act, step)

            @block.vector
            def _(dve):
                dve.sem_inc(S["o_taken"], 2)
                dve.sem_inc(Z["o_taken"], 1)

                def maxima(i, j):
                    dve.wait_ge(S["s_made"], i + 1)
                    dve.reduce_max(st[:, j, 0, :], k.psum[:, 1024 * j:1024 * (j + 1)].rearrange("p (h n) -> p h n", h=MH), AX)\
                       .then_inc(S["maxed"], 1)
                    dve.wait_ge(S["maxed"], i + 1)
                    dve.tensor_scalar(st[:, j, 1, :], st[:, j, 0, :], -MSCALE, None, ALU.mult).then_inc(S["m_ready"], 1)

                def divide(i, j):
                    dve.wait_ge(S["e_done"], MH * (i + 1))
                    dve.reciprocal(st[:, j, 3, :], st[:, j, 2, :]).then_inc(S["r_done"], 1)
                    dve.wait_ge(S["r_done"], i + 1)
                    dve.tensor_tensor(pr[:, j, :, :], pr[:, j, :, :], st[:, j, 3, :].unsqueeze(2).broadcast_to([P, MH, NM]), ALU.mult)\
                       .then_inc(S["p_scaled"], 1)

                def put(tiles, cols, ps, S, n):
                    dve.wait_ge(S["o_made"], n + 1)
                    dve.tensor_copy(H[:, tiles, cols], ps).then_inc(S["o_high"], 1)
                    dve.wait_ge(S["o_high"], n + 1)
                    dve.tensor_tensor(L[:, tiles, cols], ps, H[:, tiles, cols].bitcast(F32), ALU.subtract).then_inc(S["o_taken"], 1)

                def step(i, j, next1, next2, next3):
                    dve.wait_ge(Z["s_made"], i + 1)
                    dve.reduce_max(zst[:, 0:1], z_s, AX).then_inc(Z["maxed"], 1)
                    dve.wait_ge(Z["maxed"], i + 1)
                    dve.tensor_scalar(zst[:, 1:2], zst[:, 0:1], -MSCALE, None, ALU.mult).then_inc(Z["m_ready"], 1)
                    if next1:
                        maxima(i + 1, 1 - j)
                    dve.wait_ge(Z["e_done"], i + 1)
                    dve.reciprocal(zst[:, 3:4], zst[:, 2:3]).then_inc(Z["r_done"], 1)
                    dve.wait_ge(Z["r_done"], i + 1)
                    dve.tensor_scalar(zpr[:, :], zpr[:, :], zst[:, 3:4], None, ALU.mult).then_inc(Z["p_scaled"], 1)
                    if next1:
                        divide(i + 1, 1 - j)
                    cols = bass.ds(i * P, P)
                    put(slice(0, 4), cols, B[6].rearrange("p (c n) -> p c n", c=4), S, 2 * i)
                    put(slice(0, DK), bass.ds(TP + i * TSEQ, TSEQ), z_o.rearrange("p (c n) -> p c n", c=DK), Z, i)
                    put(slice(4, DK), cols, B[7].rearrange("p (c n) -> p c n", c=4), S, 2 * i + 1)
                maxima(0, 0)
                divide(0, 0)
                steps(dve, step)


def ffn_stage(k, H, L, full, hid, hid_full):
    nc, io = k.nc, k.io
    B = k.bank
    UP, US = 2 + TP, 2 + TSEQ
    U = UP + NB * US
    CV = U - 2
    ROUNDS = FK // 2
    S = {n: k.sem(f"ff_{n}") for n in (
        "past_in", "zero", "w_high", "w_low", "up_made", "up_taken", "past", "u_free", "c_first", "c_mid", "c_done", "cap", "tanh",
        "g_done", "hid_full", "hid_high", "hid_low", "down_made", "down_taken", "out")}
    w_in = [k.sem(f"ff_w{j}") for j in range(2)]
    DG = 3 * DK
    with ExitStack() as ctx:
        slot = k.sb(ctx, "ff_slot", [P, 2, D])
        up = k.sb(ctx, "ff_up", [P, 2, 2, D], FR)
        down = k.sb(ctx, "ff_down", [P, 2, 2, D], FR)
        u = k.sb(ctx, "ff_u", [P, 2, U])
        cv_ = k.sb(ctx, "ff_c", [P, 2, U])
        th_ = k.sb(ctx, "ff_t", [P, U])
        cv, th = cv_[:, :, 0:CV], th_[:, 0:CV]
        past = k.sb(ctx, "ff_past", [P, F2K, NB, 2])
        cap = k.sb(ctx, "ff_cap", [P, F2K, 1 + NB, 2])
        seg = lambda ap, lo: ap[:, UP:U].rearrange("p (b n) -> p b n", b=NB)[:, :, lo:lo + TSEQ]
        norm = Norm(k, "nffn", [k.x[:, i, :] for i in range(DK)], "g_ffn", H, L, full, cv_[:, :, 0:T], th_[:, 0:T])
        with nc.Block() as block:
            @block.sync
            def _(sp):
                row = lambda w, m: w[bass.ds(m, 1)].rearrange("a p n -> p (a n)")
                for e in range(4):
                    if e >= 2:
                        sp.wait_ge(S["w_low"], e - 1)
                    sp.dma_start(slot[:, e % 2], io["w_up"][e]).then_inc(w_in[e % 2], 16)
                    if e == 1:
                        sp.dma_start(past[:, :, :, :], io["conv0"]).then_inc(S["past_in"], 16)

                def next_tile(r, e, src):
                    sp.wait_ge(S["w_low"], 6 * r + e - 3)
                    sp.dma_start(slot[:, e % 2], src).then_inc(w_in[e % 2], 16)
                with sp.Fori(1, ROUNDS) as r:
                    for e, src in ((0, row(io["w_up"], 4 * r)), (1, row(io["w_up"], 4 * r + 1)),
                                   (2, row(io["w_down"], 2 * r - 2)), (3, row(io["w_down"], 2 * r - 1)),
                                   (4, row(io["w_up"], 4 * r + 2)), (5, row(io["w_up"], 4 * r + 3))):
                        next_tile(r, e, src)
                for e in range(2):
                    next_tile(ROUNDS, e, io["w_down"][FK - 2 + e])
                sp.wait_ge(S["cap"], F2K + 1)
                sp.dma_start(io["o_conv"], cap[:, :, :, :].rearrange("p m s j -> p m (s j)")).then_inc(S["out"], 16)
                sp.wait_ge(S["out"], 16)

            @block.gpsimd
            def _(pool):
                def divide(dst, j, count, n_tile):
                    pool.wait_ge(w_in[j], 16 * count)
                    pool.tensor_tensor(dst[:, 0], slot[:, j], k.mask("ones", 1).broadcast_to([P, D]), ALU.mult).then_inc(S["w_high"], 1)
                    pool.wait_ge(S["w_high"], n_tile + 1)
                    pool.tensor_tensor(dst[:, 1], slot[:, j], dst[:, 0].bitcast(F32), ALU.subtract).then_inc(S["w_low"], 1)
                for e in range(4):
                    if e >= 2:
                        pool.wait_ge(S["up_made"], 3 * (e - 1))
                    divide(up[:, e % 2], e % 2, e // 2 + 1, e)

                def up_tile(r, e, t):
                    pool.wait_ge(S["up_made"], 3 * (4 * r + t - 1))
                    divide(up[:, e % 2], e % 2, 3 * r + e // 2, 6 * r - 2 + e)

                def down_tile(r, e, j):
                    pool.wait_ge(S["down_taken"], DG * (r - 1) + 4)
                    divide(down[:, j], e % 2, 3 * r + e // 2, 6 * r - 2 + e)
                with pool.Fori(1, ROUNDS) as r:
                    up_tile(r, 0, 0)
                    up_tile(r, 1, 1)
                    down_tile(r, 2, 0)
                    down_tile(r, 3, 1)
                    up_tile(r, 4, 2)
                    up_tile(r, 5, 3)
                down_tile(ROUNDS, 0, 0)
                down_tile(ROUNDS, 1, 1)

            @block.tensor
            def _(pe):
                norm.pe(pe)

                def round_up(r, q, w_count):
                    for j in range(2):
                        pe.wait_ge(S["w_low"], w_count + j)
                        t = 4 * r + 2 * q + j
                        for n in range(3):
                            norm.wait_parts(pe, n)
                            pe.wait_ge(S["up_taken"], 3 * t + n + 1)
                            products(pe, B[(3 * (2 * q + j) + n) % 4][:, 0:C3], lambda a, kk: up[:, j, a, kk * P:(kk + 1) * P],
                                     lambda b, kk: third((H, L)[b][:, kk, :], n), DK, S["up_made"])

                def round_down(r, buf, w_count):
                    pe.wait_ge(S["w_low"], w_count)
                    pe.wait_ge(S["hid_low"], 2 * (r + 1))
                    for m in range(DK):
                        for n in range(3):
                            g = 3 * m + n
                            pe.wait_ge(S["down_taken"], DG * r + g + 1)
                            products(pe, B[4 + g % 4][:, 0:C3], lambda a, kk: down[:, kk, a, m * P:(m + 1) * P],
                                     lambda b, kk: third(hid[:, buf, b, kk, :], n), 2, S["down_made"])
                round_up(0, 0, 1)
                round_up(0, 1, 3)
                with pe.Fori(0, (ROUNDS - 1) // 2) as i:
                    for a in range(2):
                        r = 2 * i + a + 1
                        round_up(r, 0, 6 * r - 1)
                        round_down(r - 1, a, 6 * r + 2)
                        round_up(r, 1, 6 * r + 3)
                round_down(ROUNDS - 1, (ROUNDS - 1) % 2, 6 * ROUNDS)

            @block.scalar
            def _(act):
                norm.act(act)
                act.sem_inc(S["up_taken"], 4)
                act.wait_ge(S["past_in"], 16)
                act.wait_ge(S["zero"], 1)

                def hidden(i, q):
                    for j in range(2):
                        t = 2 * i + j
                        act.wait_ge(S["u_free"], t + 1)
                        act.activation(u[:, j, UP:U].rearrange("p (b n) -> p b n", b=NB)[:, :, 0:2],
                                       past[:, bass.ds(i + FK * j, 1), :, :].rearrange("p a b n -> p (a b) n"), ACT.Copy)\
                           .then_inc(S["past"], 1)
                        w = TP - 2 * C3
                        for n in range(3):
                            ps = B[(3 * (2 * q + j) + n) % 4]
                            act.wait_ge(S["up_made"], 3 * t + n + 1)
                            if n < 2:
                                last = act.activation(u[:, j, 2 + n * C3:2 + (n + 1) * C3], ps[:, 0:C3], ACT.Copy)
                            else:
                                act.activation(u[:, j, 2 + 2 * C3:UP], ps[:, 0:w], ACT.Copy)
                                last = act.activation(seg(u[:, j, :], 2), ps[:, w:C3].rearrange("p (b n) -> p b n", b=NB), ACT.Copy)
                            last.then_inc(S["up_taken"], 1)
                        act.wait_ge(S["past"], t + 1)
                        act.wait_ge(S["up_taken"], 3 * t + 7)
                        act.wait_ge(S["hid_full"], 2 * (i + 1))
                        b0 = VEC["conv_b"] + i + FK * j
                        w2 = VEC["conv_w"] + 2 * F2K + i + FK * j
                        act.activation(cv[:, j, :], u[:, j, 2:U], ACT.Identity, bias=k.vecs[:, bass.ds(b0, 1)],
                                       scale=k.vecs[:, bass.ds(w2, 1)]).then_inc(S["c_first"], 1)
                    act.wait_ge(S["c_done"], 2 * i + 1)
                    act.activation(th[:, :], cv[:, 0, :], ACT.Tanh, scale=0.5).then_inc(S["tanh"], 1)
                with act.Fori(0, ROUNDS) as r:
                    hidden(2 * r, 0)
                    hidden(2 * r + 1, 1)

            @block.vector
            def _(dve):
                norm.dve(dve)
                dve.sem_inc(S["u_free"], 2)
                dve.sem_inc(S["cap"], 1)
                dve.sem_inc(S["hid_full"], 2)
                dve.sem_inc(S["down_taken"], 4)
                dve.memset(u[:, :, 0:2], 0.0).then_inc(S["zero"], 1)

                def convolve(i, j):
                    t = 2 * i + j
                    dve.wait_ge(S["c_first"], t + 1)
                    dst = cap[:, bass.ds(i + FK * j, 1), :, :].rearrange("p a s j -> p (a s) j")
                    dve.tensor_copy(dst[:, 0:1, :], u[:, j, UP - 2:UP].unsqueeze(1))
                    dve.tensor_copy(dst[:, 1:, :], u[:, j, UP:U].rearrange("p (b n) -> p b n", b=NB)[:, :, US - 2:US])\
                       .then_inc(S["cap"], 1)
                    tap = lambda n: k.vecs[:, bass.ds(VEC["conv_w"] + n * F2K + i + FK * j, 1)]
                    dve.scalar_tensor_tensor(cv[:, j, :], u[:, j, 1:U - 1], tap(1), cv[:, j, :], ALU.mult, ALU.add)\
                       .then_inc(S["c_mid"], 1)
                    dve.wait_ge(S["c_mid"], t + 1)
                    dve.scalar_tensor_tensor(cv[:, j, :], u[:, j, 0:U - 2], tap(0), cv[:, j, :], ALU.mult, ALU.add)\
                       .then_inc(S["c_done"], 1)
                    dve.wait_ge(S["c_done"], t + 1)
                    dve.wait_ge(S["cap"], t + 2)
                    dve.sem_inc(S["u_free"], 1)

                def multiply(i, q, buf):
                    dve.wait_ge(S["tanh"], i + 1)
                    dve.scalar_tensor_tensor(th[:, :], th[:, :], 1.0, cv[:, 0, :], ALU.add, ALU.mult).then_inc(S["g_done"], 1)
                    dve.wait_ge(S["g_done"], i + 1)
                    high, low, full = hid[:, buf, 0, q, :], hid[:, buf, 1, q, :], hid_full[:, buf, 1, q, :]
                    dve.scalar_tensor_tensor(full[:, 0:TP], th[:, 0:TP], 0.5, cv[:, 1, 0:TP], ALU.mult, ALU.mult)\
                       .then_inc(S["hid_full"], 1)
                    dve.scalar_tensor_tensor(full[:, TP:T].rearrange("p (b n) -> p b n", b=NB), seg(th_[:, :], 0), 0.5,
                                             seg(cv_[:, 1, :], 0), ALU.mult, ALU.mult).then_inc(S["hid_full"], 1)
                    dve.wait_ge(S["hid_full"], 2 * (i + 2))
                    dve.tensor_copy(high, full).then_inc(S["hid_high"], 1)
                    dve.wait_ge(S["hid_high"], i + 1)
                    dve.tensor_tensor(low, full, high.bitcast(F32), ALU.subtract).then_inc(S["hid_low"], 1)

                def add_down(r):
                    for m in range(DK):
                        for n in range(3):
                            g = 3 * m + n
                            dve.wait_ge(S["down_made"], DG * r + g + 1)
                            xs = third(k.x[:, m, :], n)
                            dve.tensor_tensor(xs, xs, B[4 + g % 4][:, 0:C3], ALU.add).then_inc(S["down_taken"], 1)

                def hidden_pair(r, buf, add):
                    convolve(2 * r, 0)
                    if add:
                        add_down(r - 1)
                    convolve(2 * r, 1)
                    multiply(2 * r, 0, buf)
                    convolve(2 * r + 1, 0)
                    convolve(2 * r + 1, 1)
                    multiply(2 * r + 1, 1, buf)
                hidden_pair(0, 0, False)
                with dve.Fori(0, (ROUNDS - 1) // 2) as i:
                    for a in range(2):
                        hidden_pair(2 * i + a + 1, (a + 1) % 2, True)
                add_down(ROUNDS - 1)


def final_stage(k, y):
    s = k.sem("y_out")
    with ExitStack() as ctx:
        sq = k.sb(ctx, "nf_sq", [P, 2, T])
        acc = k.sb(ctx, "nf_acc", [P, T])
        norm = Norm(k, "nfin", [k.x[:, i, :] for i in range(DK)], "g_final", None, None, y, sq[:, :, :], acc[:, :])
        with k.nc.Block() as block:
            @block.sync
            def _(sp):
                for n in range(3):
                    sp.wait_ge(norm.S["full"], DK * (n + 1))
                    sp.dma_start(third(k.io["o_y"], n).rearrange("(k p) t -> p k t", p=P),
                                 norm.full[:, :, n * C3:(n + 1) * C3]).then_inc(s, 16)
                sp.wait_ge(s, 48)
            block.scalar(norm.act)
            block.tensor(norm.pe)
            block.vector(norm.dve)


def program(nc, io):
    with ExitStack() as ctx:
        k = K(nc, ctx, io)
        k.masks = k.sb(ctx, "masks", [P, NMK])
        k.vecs = k.sb(ctx, "vecs", [P, NVEC])
        start = lambda: (nc.sbuf_base + 31) // 32 * 32
        wide = start()
        k.sb(ctx, "wide_area", [P, 2 * DK * T])
        mix = start()
        k.sb(ctx, "mix_area", [P, Y_WORDS + 4 * T])
        k.rw = k.at(wide, "rw", [P, RWK, TR])
        H, L = k.at(wide, "high", [P, DK, T], FR), k.at(wide, "low", [P, DK, T], FR, words=DK * T)
        full = k.at(wide, "full", [P, DK, T], words=DK * T)
        k.y, k.mla = k.at(mix, "y", [P, 4, 1 + TR]), k.at(mix, "mla", [P, 4, T], words=Y_WORDS)
        load_stage(k)
        with ExitStack() as mctx:
            cqkv = start()
            k.cqkv = k.sb(mctx, "cqkv", [P, QK + KK, T])
            k.krope = k.sb(mctx, "krope", [P, T])
            qabs = k.sb(mctx, "qabs", [P, KK, NB, NH, TSEQ])
            qrope = k.sb(mctx, "qrope", [ROPE, NB, NH, TSEQ])
            with ExitStack() as tctx:
                k.rot = k.sb(tctx, "rot", [P, 2, T])
                with ExitStack() as hctx:
                    h_high = k.sb(hctx, "h_high", [P, DK, T], FR)
                    proj_stage(k, h_high, k.at(mix, "h_low", [P, DK, T], FR), k.at(mix, "h_full", [P, DK, T]))
                mla_prompt_stage(k, k.at(cqkv, "cq_low", [P, QK, T], FR), qabs, qrope)
            mla_sample_stage(k, mix, cqkv, qabs, qrope)
            k.debug("mla", k.mla[:, :, :])
        k.recycle()
        with ExitStack() as rctx:
            at_a = start()
            a = k.sb(rctx, "rw_a", [P, 4, TR])
            at_kk = start()
            kk = k.sb(rctx, "rw_kk", [P, 4, TR])
            keep = k.sb(rctx, "rw_keep", [P, TR])
            rwkv_prep_stage(k, k.y, a, kk, keep)
            rwkv_chunk_stage(k, k.y, a, kk, keep, at_a, at_kk)
        k.recycle()
        rwkv_out_stage(k, k.y)
        k.debug("rw", k.y[:, :, 1:1 + T])
        k.x = k.sb(ctx, "x", [P, DK, T])
        s_x = k.sem("x1")
        with ExitStack() as octx:
            sq = k.sb(octx, "nmla_tile", [P, 2, T])
            acc = k.sb(octx, "nmla_row", [P, T])
            norm = Norm(k, "nmla", [k.mla[:, i, :] for i in range(4)], "g_mla_out", H, L, full, sq[:, :, :], acc[:, :],
                        plain=[(i, k.y[:, i, 1:1 + T]) for i in range(4)])
            linear_stage(k, "wo", io["w_o"], DK, [(DK, residual(k))], H, L, norm=norm, drain_wait=(s_x, 16),
                         then=[(k.x[:, :, :], io["x"].rearrange("(k p) t -> p k t", p=P), s_x)])
        k.debug("x1", k.x[:, :, :])
        k.recycle()
        with ExitStack() as actx:
            kmT = k.sb(actx, "kmT", [P, DK, NM])
            vm = k.sb(actx, "vm", [P, 2, D])
            memory_kv_stage(k, kmT, vm)
            q = k.at(mix, "q", [P, DK, T])

            def to_q(eng, m, n, ps):
                return eng.activation(q[:, bass.ds(m, 1), n * C3:(n + 1) * C3], ps, ACT.Copy)
            with ExitStack() as nctx:
                sq = k.sb(nctx, "nmq_tile", [P, 2, T])
                acc = k.sb(nctx, "nmq_row", [P, T])
                norm = Norm(k, "nmq", [k.x[:, i, :] for i in range(DK)], "g_mem_q", H, L, full, sq[:, :, :], acc[:, :])
                linear_stage(k, "mq", io["w_mq"], DK, [(DK, to_q)], H, L, engine="scalar", norm=norm)
            memory_attention_stage(k, q, kmT, vm, H, L)
        linear_stage(k, "mo", io["w_mo"], DK, [(DK, residual(k))], H, L)
        k.debug("x2", k.x[:, :, :])
        k.recycle()
        hid = [P, 2, 2, 2, T]
        ffn_stage(k, H, L, full, k.at(mix, "hid", hid, FR), k.at(mix, "hid_full", hid))
        final_stage(k, full)


OUTS = {
    "o_y": (D, T), "o_lat": (KVL, T), "o_krope": (ROPE, T),
    "o_memk": (D, NM), "o_memv": (NM, D),
    "o_rwkv_p": (NH, HD, HD), "o_rwkv_s": (NB, NH, HD, HD),
    "o_shift": (P, RWK, 1 + NB), "o_conv": (P, F2K, 2 * (1 + NB)),
}


DEBUG = {}


def build(nc, arrays):
    io = {}
    for name, a in arrays.items():
        io[name] = nc.dram_tensor(f"in_{name}", a.shape, mybir.dt.from_np(a.dtype), kind="ExternalInput").ap()
    for name, shape in OUTS.items():
        io[name] = nc.dram_tensor(name, shape, F32, kind="ExternalOutput").ap()
    for name, shape in DEBUG.items():
        io["dbg_" + name] = nc.dram_tensor("dbg_" + name, shape, F32, kind="ExternalOutput").ap()
    program(nc, io)


def kernel(**inputs):
    import numpy as _np
    import concourse.bacc as _bacc
    from concourse.bass_utils import run_bass_kernel_spmd as _run

    x = {n: _np.asarray(a) for n, a in inputs.items()}
    tile = lambda a: _np.ascontiguousarray(a)
    m, rw, rot, keep, batch = tables()
    arrays = {"masks": m, "rwmasks": rw, "rot": rot, "keep": keep, "batchmask": batch}
    arrays["vecs"] = tile(_np.concatenate([x[n].reshape(-1, P) for n in VEC]).T)
    arrays["x"] = tile(_np.concatenate([x["x_prompt"][0], x["x_sample"].reshape(TS, D)]).T)
    arrays["memT"] = tile(x["mem_prompt"][0].T)
    arrays["lat"] = x["cache_mla_latent"][0]
    arrays["kr"] = x["cache_mla_krope"][0]
    arrays["pages"] = x["page_table"].reshape(1, -1)
    arrays["memk"] = tile(x["cache_mem_k"][0].reshape(NB, NM, D).transpose(0, 2, 1))
    arrays["memv"] = x["cache_mem_v"][0].reshape(NB, NM, D)
    arrays["s0"] = tile(x["state_rwkv"][0].transpose(0, 1, 3, 2))
    arrays["shift0"] = tile(x["state_rwkv_shift"][0].reshape(NB, RWK, P).transpose(2, 1, 0))
    arrays["conv0"] = tile(x["state_ffn_conv"][0].reshape(NB, 2, F2K, P).transpose(3, 2, 0, 1))
    for n in ("rw_w2", "rw_a2", "rw_g2", "w_mk", "w_mv"):
        arrays[n] = x[n][0]
    by_tile = lambda w: tile(w.reshape(DK, P, -1, P).transpose(2, 1, 0, 3)).reshape(-1, P, D)
    for n in ("w_o", "w_mq", "w_mo"):
        arrays[n] = by_tile(x[n][0])
    w = x["w_in"][0]
    key, half = w[:, QL + KVL:MLA_PROJ], ROPE // 2
    swapped = _np.concatenate([key[:, half:], key[:, :half]], 1)
    arrays["w_in"] = by_tile(_np.concatenate([w[:, :QL + KVL], w[:, MLA_PROJ:], key, swapped, key, swapped], 1))
    by_head = lambda w, n: tile(w.reshape(n, P, NH, -1).transpose(2, 1, 0, 3)).reshape(NH, P, -1)
    w = x["w_uq"][0].reshape(QL, NH, NOPE + ROPE)
    arrays["w_uq"] = by_head(_np.concatenate([w, w[:, :, NOPE + half:], w[:, :, NOPE:NOPE + half]], 2).reshape(QL, -1), QK)
    arrays["w_ukv"] = by_head(x["w_ukv"][0], KK)
    arrays["w_up"] = tile(by_tile(x["w_up"][0]).reshape(2, FK, P, D).transpose(1, 0, 2, 3)).reshape(F2K, P, D)
    arrays["w_down"] = x["w_down"][0].reshape(FK, P, D)
    nc = _bacc.Bacc("TRN2", target_bir_lowering=False, num_devices=1)
    build(nc, arrays)
    r = _run(nc, [{f"in_{n}": a for n, a in arrays.items()}], core_ids=[0]).results[0]
    T_ = lambda a: tile(a.T)
    y, lat, kr = T_(r["o_y"]), T_(r["o_lat"]), T_(r["o_krope"])
    sh = r["o_shift"].transpose(2, 1, 0).reshape(1 + NB, RWP)
    cv = r["o_conv"].transpose(2, 1, 0).reshape(1 + NB, 2, 2 * FF)
    st = lambda a, n: tile(a.reshape(n, NH, HD, HD).transpose(0, 1, 3, 2))[None]
    return (y[None, :TP], y[TP:].reshape(NB, TSEQ, D),
            lat[None, None, :TP], kr[None, None, :TP],
            T_(r["o_memk"]).reshape(1, 1, NM, MH, MD), r["o_memv"].reshape(1, 1, NM, MH, MD),
            st(r["o_rwkv_p"], 1), sh[None, :1], cv[None, :1],
            lat[TP:].reshape(1, NB, TSEQ, KVL), kr[TP:].reshape(1, NB, TSEQ, ROPE),
            st(r["o_rwkv_s"], NB), sh[None, 1:], cv[None, 1:])
```

```python
from contextlib import ExitStack

import numpy as np

import concourse.bass as bass
from concourse import mybir

F32 = mybir.dt.float32
FR = mybir.dt.float32r
I32 = mybir.dt.int32
ALU = mybir.AluOpType
ACT = mybir.ActivationFunctionType
AX = mybir.AxisListType.X

P = 128
D = 1024
TP, NB, TSEQ = 1024, 8, 4
TS = NB * TSEQ
T = TP + TS
C3 = T // 3
DK = D // P
NH, HD = 8, 64
NOPE, ROPE = 64, 32
QL, KVL = 384, 256
QK, KK = QL // P, KVL // P
MLA_PROJ = QL + KVL + ROPE
RWP = 3 * 512 + 64 + 64 + 128
RWK = RWP // P
CH = 64
NCH = TP // CH
TR = TP + CH
PAST, PAGE = 2048, 128
NPG = PAST // PAGE
NM, MH, MD = 256, 4, 256
FF = 2816
FK = FF // P
F2K = 2 * FK
EPS = 1e-6
LNX_EPS = 64e-5
SCALE = (NOPE + ROPE) ** -0.5
MSCALE = MD ** -0.5
NEG = -1e30

VEC = {}
_n = 0
for _name, _w in (("g_mix", 8), ("q_norm_g", 3), ("kv_norm_g", 2), ("g_mla_out", 4), ("rw_mu", 14), ("rw_w0", 4),
                  ("rw_a0", 4), ("rw_k_k", 4), ("rw_k_a", 4), ("rw_r_k", 4), ("rw_lnx_g", 4), ("rw_lnx_b", 4),
                  ("g_mem_q", 8), ("g_mem_kv", 8), ("g_ffn", 8), ("g_final", 8), ("conv_b", 44), ("conv_w", 132)):
    VEC[_name] = _n
    _n += _w
NVEC = _n

MK = {}
_n = 0
for _name, _w in (("ident", P), ("headones", P), ("ones", P), ("causal", P), ("new_causal", TSEQ * NB),
                  ("pick", 32), ("spread", P), ("eps", 1), ("lnx_eps", 1)):
    MK[_name] = _n
    _n += _w
NMK = _n
RWM = 3 * P
Y_WORDS = (4 * (1 + TR) + 7) // 8 * 8


def tables():
    t = np.arange(P) % CH
    head = np.arange(P) // CH
    same = head[:, None] == head[None, :]
    m = np.zeros((P, NMK), np.float32)
    m[:, MK["ident"]:MK["ident"] + P] = np.eye(P)
    m[:, MK["headones"]:MK["headones"] + P] = same
    m[:, MK["ones"]:MK["ones"] + P] = 1
    q = np.arange(P)
    m[:, MK["causal"]:MK["causal"] + P] = np.where(q[None, :] <= q[:, None], 0, NEG)
    r = np.arange(NH * TSEQ) % TSEQ
    for b in range(NB):
        m[:NH * TSEQ, MK["new_causal"] + b * TSEQ:MK["new_causal"] + (b + 1) * TSEQ] = np.where(
            np.arange(TSEQ)[None, :] <= r[:, None], 0, NEG)
    m[:, MK["pick"]], m[:, MK["pick"] + 1] = head == 0, head == 1
    m[0::32, MK["spread"]:MK["spread"] + P] = head == 0
    m[1::32, MK["spread"]:MK["spread"] + P] = head == 1
    m[:, MK["eps"]] = EPS
    m[:, MK["lnx_eps"]] = LNX_EPS
    rw = np.zeros((P, 2 * RWM), np.float32)
    for g in range(2):
        ok = same if g == 0 else same & (t[:, None] // TSEQ == t[None, :] // TSEQ) & (t[:, None] < TS) & (t[None, :] < TS)
        rw[:, g * RWM:g * RWM + P] = ok & (t[None, :] < t[:, None])
        rw[:, g * RWM + P:g * RWM + 2 * P] = ok & (t[None, :] > t[:, None])
        rw[:, g * RWM + 2 * P:g * RWM + 3 * P] = ok & (t[None, :] >= t[:, None])
    pos = np.concatenate([np.arange(TP), np.tile(PAST + np.arange(TSEQ), NB)]).astype(np.float32)
    half = ROPE // 2
    inv = (np.float32(1) / (np.float32(10000.0) ** (np.arange(half, dtype=np.float32) / np.float32(half)))).astype(np.float32)
    ang = (inv[:, None] * pos[None, :]).astype(np.float32)
    rot = np.zeros((P, 2, T), np.float32)
    for base in (0, 32, 64, 96):
        rot[base:base + half, 0] = rot[base + half:base + ROPE, 0] = np.cos(ang)
        rot[base:base + half, 1] = -np.sin(ang)
        rot[base + half:base + ROPE, 1] = np.sin(ang)
    keep = np.ones((P, TR), np.float32)
    keep[:, 0:TP:CH] = 0
    keep[:, TP:TR:TSEQ] = 0
    batch = ((t[:, None] // TSEQ == np.arange(NB)[None, :]) & (t[:, None] < TS)).astype(np.float32)
    return m, rw, rot.reshape(P, 2 * T), keep, batch


class Chain:

    def __init__(self, eng, sem, base=0):
        self.eng, self.sem, self.n, self.base = eng, sem, 0, base

    def __call__(self, ins):
        ins.then_inc(self.sem, 1)
        self.n += 1
        self.eng.wait_ge(self.sem, self.base + self.n)


class K:

    def __init__(self, nc, ctx, io):
        self.nc, self.ctx, self.io = nc, ctx, io
        self.sems = []
        self.psum = ctx.enter_context(nc.psum_tensor("psum", [P, 8 * 512], F32))
        self.bank = [self.psum[:, i * 512:(i + 1) * 512] for i in range(8)]

    def sb(self, ctx, name, shape, dt=F32):
        return ctx.enter_context(self.nc.sbuf_tensor(name, shape, dt))

    def at(self, base, name, shape, dt=F32, words=0):
        return self.nc.alloc_sbuf_tensor_at(name, shape, dt, offset=base + 4 * words)

    def sem(self, name):
        self.sems.append(self.nc.alloc_semaphore(name=name))
        return self.sems[-1]

    def recycle(self):
        self.nc.clear_and_free_semaphores(self.sems)
        self.sems = []
        self.nc.all_engine_barrier()

    def vec(self, name, k, p0=0, p1=P):
        c = VEC[name] + k
        return self.vecs[p0:p1, c:c + 1]

    def mask(self, name, w=P, rows=P):
        return self.masks[0:rows, MK[name]:MK[name] + w]


def third(ap, n):
    return ap[:, n * C3:(n + 1) * C3]


class Norm:

    def __init__(self, k, name, src, gain, H, L, full, sq, acc, bank):
        self.bank = k.bank[bank:bank + 3]
        self.k, self.src, self.gain, self.H, self.L, self.full, self.sq, self.acc = k, src, gain, H, L, full, sq, acc
        self.n = len(src)
        self.S = {x: k.sem(f"{name}_{x}") for x in ("sq", "added", "sums", "root", "inv", "full", "high", "low")}

    def act(self, act):
        k, S = self.k, self.S
        for i in range(self.n):
            if i >= 2:
                act.wait_ge(S["added"], max(1, i - 2))
            act.activation(self.sq[:, i % 2, :], self.src[i], ACT.Square).then_inc(S["sq"], 1)
        for n in range(3):
            act.wait_ge(S["sums"], n + 1)
            act.activation(third(self.acc, n), self.bank[n][:, 0:C3], ACT.Sqrt, bias=k.mask("eps", 1),
                           scale=1.0 / (self.n * P)).then_inc(S["root"], 1)
        if self.H is not None:
            for n in range(3):
                for i in range(self.n):
                    act.wait_ge(S["full"], n * self.n + i + 1)
                    act.activation(third(self.H[:, i, :], n), third(self.full[:, i, :], n), ACT.Copy).then_inc(S["high"], 1)

    def pe(self, pe):
        k, S = self.k, self.S
        pe.wait_ge(S["added"], self.n - 1)
        for n in range(3):
            pe.matmul(self.bank[n][:, 0:C3], k.mask("ones"), third(self.acc, n), start=True, stop=True).then_inc(S["sums"], 1)

    def wait_parts(self, pe, n):
        pe.wait_ge(self.S["low"], self.n * (n + 1))

    def dve(self, dve):
        k, S = self.k, self.S
        for i in range(1, self.n):
            dve.wait_ge(S["sq"], i + 1)
            if i >= 2:
                dve.wait_ge(S["added"], i - 1)
            dve.tensor_tensor(self.acc, self.sq[:, 0, :] if i == 1 else self.acc, self.sq[:, i % 2, :], ALU.add)\
               .then_inc(S["added"], 1)

        def low(j):
            n, i = divmod(j, self.n)
            dve.wait_ge(S["high"], j + 1)
            dve.tensor_tensor(third(self.L[:, i, :], n), third(self.full[:, i, :], n), third(self.H[:, i, :], n).bitcast(F32),
                              ALU.subtract).then_inc(S["low"], 1)
        for n in range(3):
            dve.wait_ge(S["root"], n + 1)
            dve.reciprocal(third(self.acc, n), third(self.acc, n)).then_inc(S["inv"], 1)
            dve.wait_ge(S["inv"], n + 1)
            for i in range(self.n):
                dve.scalar_tensor_tensor(third(self.full[:, i, :], n), third(self.src[i], n), k.vec(self.gain, i),
                                         third(self.acc, n), ALU.mult, ALU.mult).then_inc(S["full"], 1)
                if self.H is not None and n * self.n + i >= 1:
                    low(n * self.n + i - 1)
        if self.H is not None:
            low(3 * self.n - 1)


class RowScale:

    def __init__(self, k, name):
        self.k, self.S = k, {x: k.sem(f"{name}_{x}") for x in ("sums", "root", "inv")}

    def pe(self, pe):
        for n in range(3):
            pe.matmul(self.k.bank[5 + n][:, 0:C3], self.k.mask("ones"), third(self.k.acc, n), start=True, stop=True)\
              .then_inc(self.S["sums"], 1)

    def act(self, act):
        for n in range(3):
            act.wait_ge(self.S["sums"], n + 1)
            act.activation(third(self.k.acc, n), self.k.bank[5 + n][:, 0:C3], ACT.Sqrt, bias=self.k.mask("eps", 1),
                           scale=1.0 / D).then_inc(self.S["root"], 1)

    def dve(self, dve):
        for n in range(3):
            dve.wait_ge(self.S["root"], n + 1)
            dve.reciprocal(third(self.k.acc, n), third(self.k.acc, n)).then_inc(self.S["inv"], 1)
        dve.wait_ge(self.S["inv"], 3)


class NextInput:

    def __init__(self, k, name, gain, H, L, sq):
        self.k, self.gain, self.H, self.L, self.sq = k, gain, H, L, sq
        self.S = {x: k.sem(f"{name}_{x}") for x in ("high", "squared", "low", "added")}

    def act(self, act, m):
        x = self.k.x[:, bass.ds(m, 1), :]
        act.activation(self.H[:, bass.ds(m, 1), :], x, ACT.Copy, scale=self.k.vecs[:, bass.ds(VEC[self.gain] + m, 1)])\
           .then_inc(self.S["high"], 1)
        act.activation(self.sq[:, :].unsqueeze(1), x, ACT.Square).then_inc(self.S["squared"], 1)

    def start(self, dve):
        dve.memset(self.k.acc[:, :], 0.0).then_inc(self.S["added"], 1)

    def dve(self, dve, m):
        x = self.k.x[:, bass.ds(m, 1), :]
        dve.wait_ge(self.S["high"], m + 1)
        dve.scalar_tensor_tensor(self.L[:, bass.ds(m, 1), :], x, self.k.vecs[:, bass.ds(VEC[self.gain] + m, 1)],
                                 self.H[:, bass.ds(m, 1), :].bitcast(F32), ALU.mult, ALU.subtract).then_inc(self.S["low"], 1)
        dve.wait_ge(self.S["squared"], m + 1)
        dve.wait_ge(self.S["added"], m + 1)
        dve.tensor_tensor(self.k.acc, self.k.acc, self.sq, ALU.add).then_inc(self.S["added"], 1)


class TwoParts:

    def __init__(self, k, name, src, H, L):
        self.k, self.src, self.H, self.L = k, src, H, L
        self.S = {x: k.sem(f"{name}_{x}") for x in ("high", "low")}

    def act(self, act):
        for n in range(3):
            for i, (x, g) in enumerate(self.src):
                act.activation(third(self.H[:, i, :], n), third(x, n), ACT.Copy, scale=1.0 if g is None else g)\
                   .then_inc(self.S["high"], 1)

    def dve(self, dve):
        for n in range(3):
            for i, (x, g) in enumerate(self.src):
                dve.wait_ge(self.S["high"], len(self.src) * n + i + 1)
                dst, x, high = third(self.L[:, i, :], n), third(x, n), third(self.H[:, i, :], n).bitcast(F32)
                if g is None:
                    ins = dve.tensor_tensor(dst, x, high, ALU.subtract)
                else:
                    ins = dve.scalar_tensor_tensor(dst, x, g, high, ALU.mult, ALU.subtract)
                ins.then_inc(self.S["low"], 1)

    def wait_parts(self, pe, n):
        pe.wait_ge(self.S["low"], len(self.src) * (n + 1))


def products(pe, ps, w, rhs, nk, inc):
    for kk in range(nk):
        for n, (a, b) in enumerate(((0, 0), (0, 1), (1, 0))):
            mm = pe.matmul(ps, w(a, kk), rhs(b, kk), start=(kk == 0 and n == 0), stop=(kk == nk - 1 and n == 2))
    mm.then_inc(inc, 1)


def linear_stage(k, name, w, n_m, groups, H, L, rows=None, prepare=None, nxt=None, first=(), then=(), after=None,
                 drain_wait=None):
    nc = k.nc
    w_in = [k.sem(f"{name}_w{j}") for j in range(2)]
    w_high, w_low, made, taken = [k.sem(f"{name}_{s}") for s in ("w_high", "w_low", "made", "taken")]

    def pairs(eng, lo, step):
        with eng.Fori(lo // 2, n_m // 2) as i:
            for j in range(2):
                step(i, 2 * i + j, j)
        if n_m % 2:
            step(n_m // 2, n_m - 1, 0)
    with ExitStack() as ctx:
        slot = k.sb(ctx, f"{name}_slot", [P, 2, DK * P])
        part = k.sb(ctx, f"{name}_part", [P, 2, 2, DK * P], FR)
        with nc.Block() as block:
            @block.sync
            def _(sp):
                for dst, src, sem in first:
                    sp.dma_start(dst, src).then_inc(sem, 16)
                for j in range(2):
                    sp.dma_start(slot[:, j], w[j]).then_inc(w_in[j], 16)
                for dst, src, sem in then:
                    sp.dma_start(dst, src).then_inc(sem, 16)

                def load(i, m, j):
                    sp.wait_ge(w_low, m - 1)
                    sp.dma_start(slot[:, j], w[bass.ds(m, 1)].rearrange("a p n -> p (a n)")).then_inc(w_in[j], 16)
                pairs(sp, 2, load)

            @block.gpsimd
            def _(pool):
                def divide(i, m, j, free=True):
                    pool.wait_ge(w_in[j], 16 * (i + 1))
                    if free:
                        pool.wait_ge(made, 3 * (m - 1))
                    pool.tensor_tensor(part[:, j, 0], slot[:, j], k.mask("ones", 1).broadcast_to([P, D]), ALU.mult).then_inc(w_high, 1)
                    pool.wait_ge(w_high, m + 1)
                    pool.tensor_tensor(part[:, j, 1], slot[:, j], part[:, j, 0].bitcast(F32), ALU.subtract).then_inc(w_low, 1)
                divide(0, 0, 0, False)
                divide(0, 1, 1, False)
                pairs(pool, 2, divide)

            @block.tensor
            def _(pe):
                def step(i, m, j):
                    pe.wait_ge(w_low, m + 1)
                    pe.wait_ge(taken, m + 1)
                    for n in range(3):
                        if prepare and isinstance(m, int) and m == 0:
                            prepare.wait_parts(pe, n)
                        if rows and n == 2 and not (isinstance(m, int) and m == 0):
                            pe.wait_ge(rows.S["root"], 3)
                        products(pe, k.bank[3 * j + n][:, 0:C3], lambda a, kk: part[:, j, a, kk * P:(kk + 1) * P],
                                 lambda b, kk: third((H, L)[b][:, kk, :], n), DK, made)
                if rows and not prepare:
                    rows.pe(pe)
                step(0, 0, 0)
                if rows and prepare:
                    prepare.wait_squares(pe)
                    rows.pe(pe)
                step(0, 1, 1)
                pairs(pe, 2, step)

            def drain(eng):
                if drain_wait:
                    eng.wait_ge(*drain_wait)
                m0 = 0
                for count, ep in groups:
                    def step(m, j):
                        for n in range(3):
                            eng.wait_ge(made, 3 * (m0 + m) + n + 1)
                            last = ep(eng, m, n, k.bank[3 * j + n][:, 0:C3])
                        last.then_inc(taken, 1)
                        if nxt:
                            nxt.dve(eng, m)
                    if count > 1:
                        with eng.Fori(0, count // 2) as i:
                            for a in range(2):
                                step(2 * i + a, (m0 + a) % 2)
                    if count % 2:
                        step(count - 1, (m0 + count - 1) % 2)
                    m0 += count

            @block.scalar
            def _(act):
                if prepare:
                    prepare.act(act)
                if rows:
                    rows.act(act)
                if nxt:
                    def following(i, m, j):
                        act.wait_ge(taken, m + 3)
                        nxt.act(act, m)
                    pairs(act, 0, following)

            @block.vector
            def _(dve):
                dve.sem_inc(taken, 2)
                if prepare:
                    prepare.dve(dve)
                if rows:
                    rows.dve(dve)
                if nxt:
                    nxt.start(dve)
                drain(dve)
                if after:
                    after(dve, made)


def load_stage(k):
    nc, io = k.nc, k.io
    s_load = k.sem("s_load")
    with nc.Block() as block:
        @block.sync
        def _(sp):
            sp.dma_start(k.masks[:, :], io["masks"]).then_inc(s_load, 16)
            sp.dma_start(k.vecs[:, :], io["vecs"]).then_inc(s_load, 16)
            sp.wait_ge(s_load, 32)


def scaled(k, dst):
    def ep(eng, m, n, ps):
        return eng.tensor_tensor(dst[:, bass.ds(m, 1), n * C3:(n + 1) * C3], ps.unsqueeze(1),
                                 third(k.acc, n).unsqueeze(1), ALU.mult)
    return ep


def proj_stage(k, H, L, x):
    nc, io = k.nc, k.io

    s_x = [k.sem(f"x0_{i}") for i in range(3)]
    s_rot, s_zero, s_kr = [k.sem(f"kr_{x}") for x in ("rot", "zero", "own")]
    xv = io["x"].rearrange("(k p) t -> p k t", p=P)
    n_main = QK + KK + RWK

    def rope_key(dve, made):
        dve.memset(k.rw[:, :, T:TR], 0.0).then_inc(s_zero, 1)
        dve.wait_ge(s_rot, 16)
        own = Chain(dve, s_kr)
        for n in range(3):
            dve.wait_ge(made, 3 * n_main + n + 1)
            c, ps = slice(n * C3, (n + 1) * C3), k.bank[3 * (n_main % 2) + n]
            own(dve.tensor_tensor(k.krope[64:96, c], ps[64:96, 0:C3], k.rot[64:96, 0, c], ALU.mult))
            own(dve.tensor_tensor(u[64:96, c], ps[96:128, 0:C3], k.rot[96:128, 1, c], ALU.mult))
            own(dve.tensor_tensor(k.krope[64:96, c], k.krope[64:96, c], u[64:96, c], ALU.add))
            own(dve.tensor_tensor(k.krope[64:96, c], k.krope[64:96, c], k.acc[64:96, c], ALU.mult))
    sq = k.rw[:, 0:2, 0:T]

    class Prepare:
        S = {n: k.sem(f"x0_{n}") for n in ("high", "squared", "added", "low")}

        def act(self, act):
            for n in range(3):
                act.wait_ge(s_x[n], 16)
                for i in range(DK):
                    act.activation(third(H[:, i, :], n), third(x[:, i, :], n), ACT.Copy, scale=k.vec("g_mix", i))\
                       .then_inc(self.S["high"], 1)
                    if i >= 2:
                        act.wait_ge(self.S["added"], (DK - 1) * n + max(1, i - 2))
                    act.activation(third(sq[:, i % 2, :], n), third(x[:, i, :], n), ACT.Square).then_inc(self.S["squared"], 1)

        def dve(self, dve):
            for n in range(3):
                for i in range(DK):
                    dve.wait_ge(self.S["squared"], DK * n + i + 1)
                    dve.wait_ge(self.S["high"], DK * n + i + 1)
                    dve.scalar_tensor_tensor(third(L[:, i, :], n), third(x[:, i, :], n), k.vec("g_mix", i),
                                             third(H[:, i, :], n).bitcast(F32), ALU.mult, ALU.subtract).then_inc(self.S["low"], 1)
                    if i >= 1:
                        if i >= 2:
                            dve.wait_ge(self.S["added"], (DK - 1) * n + i - 1)
                        dve.tensor_tensor(third(k.acc, n), third(sq[:, 0, :] if i == 1 else k.acc, n), third(sq[:, i % 2, :], n),
                                          ALU.add).then_inc(self.S["added"], 1)

        def wait_parts(self, pe, n):
            pe.wait_ge(self.S["low"], DK * (n + 1))

        def wait_squares(self, pe):
            pe.wait_ge(self.S["added"], 3 * (DK - 1))
    with ExitStack() as ctx:
        u = k.sb(ctx, "x0_u", [P, T])

        linear_stage(k, "pj", io["w_in"], QK + KK + RWK + 1, [(QK + KK, scaled(k, k.cqkv)), (RWK, scaled(k, k.rw))], H, L,
                     prepare=Prepare(), rows=RowScale(k, "nmix"),
                     first=[(x[:, :, n * C3:(n + 1) * C3], xv[:, :, n * C3:(n + 1) * C3], s_x[n]) for n in range(3)],
                     then=[(k.rot[:, :, :].rearrange("p a t -> p (a t)"), io["rot"], s_rot)], after=rope_key)


TILES = TP // P
GROUPS = [(i + 4) // 4 for i in range(TILES)]
GSUM = [sum(GROUPS[:i + 1]) for i in range(TILES)]
NG = GSUM[-1]


def mla_prompt_stage(k, cq_low, qabs, qrope):
    nc, io = k.nc, k.io
    S = {n: k.sem(f"mp_{n}") for n in (
        "w_high", "w_low", "q_made", "k_made", "v_made", "ukt_made", "qabs_made", "q_taken", "qr_cos", "qr_sin", "qr_taken",
        "k_taken", "v_taken", "ukt_taken", "qabs_taken", "s_made", "maxed", "m_ready", "e_done", "r_done",
        "t_made", "t_taken", "o_made", "o_taken", "ot_made", "ot_taken", "kr_there", "out")}
    w_in = [k.sem(f"mp_w{j}") for j in range(2)]
    cq, lat = k.cqkv[:, 0:QK, :], k.cqkv[:, QK:QK + KK, :]
    B, QH, UKV = k.bank, NOPE + ROPE, 2 * HD
    with ExitStack() as ctx:
        cq_high = k.sb(ctx, "mp_cq", [P, QK, T], FR)
        uq = k.sb(ctx, "mp_uq", [P, 2, QK * P])
        uqp = k.sb(ctx, "mp_uqp", [P, 2, 2, QK * P], FR)
        ukv = k.sb(ctx, "mp_ukv", [P, 2, KK, UKV])
        qT = k.sb(ctx, "mp_qT", [P, 2, T])
        kT = k.sb(ctx, "mp_kT", [P, 2, TP])
        v = k.sb(ctx, "mp_v", [P, 2, 512])
        ukT = k.sb(ctx, "mp_ukT", [HD, 2, KVL])
        u = k.sb(ctx, "mp_u", [P, C3])
        pr = k.sb(ctx, "mp_pr", [P, 2, T])
        pT = k.sb(ctx, "mp_pT", [P, 2, T])
        ot = k.acc[:, 0:TP].rearrange("p (i f) -> p i f", i=TILES)
        stat = k.sb(ctx, "mp_stat", [P, 4, TILES])
        mx, negm, rsum, rinv = [stat[:, n, :] for n in range(4)]
        nq = Norm(k, "nq", [cq[:, i, :] for i in range(QK)], "q_norm_g", cq_high, cq_low, cq, qT[:, :, :], pr[:, 0, :], bank=5)
        nkv = Norm(k, "nkv", [lat[:, i, :] for i in range(KK)], "kv_norm_g", None, None, lat, pT[:, :, :], pr[:, 1, :], bank=2)
        with nc.Block() as block:
            @block.sync
            def _(sp):
                def load(h, j):
                    sp.dma_start(uq[:, j], io["w_uq"][bass.ds(h, 1)].rearrange("a p n -> p (a n)")).then_inc(w_in[j], 16)
                    sp.dma_start(ukv[:, j].rearrange("p k n -> p (k n)"),
                                 io["w_ukv"][bass.ds(h, 1)].rearrange("a p n -> p (a n)")).then_inc(w_in[j], 16)
                load(0, 0)
                load(1, 1)
                sp.dma_start(io["o_krope"], k.krope[64:96, :]).then_inc(S["out"], 16)
                sp.wait_ge(nkv.S["full"], 3 * KK)
                sp.dma_start(io["o_lat"].rearrange("(k p) t -> p k t", p=P), lat).then_inc(S["out"], 16)
                with sp.Fori(1, NH // 2) as i:
                    for j in range(2):
                        sp.wait_ge(S["w_low"], 2 * i + j - 1)
                        sp.wait_ge(S["ukt_made"], 2 * i + j - 1)
                        load(2 * i + j, j)
                sp.wait_ge(S["out"], 32)

            @block.gpsimd
            def _(pool):
                def divide(i, j, free=True):
                    h = 2 * i + j
                    pool.wait_ge(w_in[j], 32 * (i + 1))
                    if free:
                        pool.wait_ge(S["q_made"], 3 * (h - 1))
                    pool.tensor_tensor(uqp[:, j, 0], uq[:, j], k.mask("ones", 1).broadcast_to([P, QK * P]), ALU.mult)\
                        .then_inc(S["w_high"], 1)
                    pool.wait_ge(S["w_high"], h + 1)
                    pool.tensor_tensor(uqp[:, j, 1], uq[:, j], uqp[:, j, 0].bitcast(F32), ALU.subtract).then_inc(S["w_low"], 1)
                divide(0, 0, False)
                divide(0, 1, False)
                with pool.Fori(1, NH // 2) as i:
                    divide(i, 0)
                    divide(i, 1)

            @block.tensor
            def _(pe):
                nkv.pe(pe)
                nq.pe(pe)

                def piece(h, j, p):
                    if p < 3:
                        if p == 0:
                            pe.wait_ge(S["w_low"], h + 1)
                        else:
                            pe.wait_ge(S["q_taken"], 3 * h + p)
                            pe.wait_ge(S["qr_taken"], 3 * h + p)
                        nq.wait_parts(pe, p)
                        products(pe, B[7][:, 0:C3], lambda a, kk: uqp[:, j, a, kk * P:(kk + 1) * P],
                                 lambda b, kk: third((cq_high, cq_low)[b][:, kk, :], p), QK, S["q_made"])
                    elif p < 5:
                        n = p - 3
                        if n == 0:
                            pe.wait_ge(S["q_taken"], 3 * h + 3)
                            pe.wait_ge(S["qr_taken"], 3 * h + 3)
                            pe.wait_ge(nkv.S["full"], 3 * KK)
                        else:
                            pe.wait_ge(S["k_taken"], 2 * h + 1)
                        for kk in range(KK):
                            mm = pe.matmul(B[7][0:NOPE, :], ukv[:, j, kk, 0:NOPE], lat[:, kk, n * 512:(n + 1) * 512],
                                           start=(kk == 0), stop=(kk == KK - 1))
                        mm.then_inc(S["k_made"], 1)
                    elif p == 5:
                        pe.wait_ge(S["k_taken"], 2 * h + 2)
                        for t in range(TILES):
                            for kk in range(KK):
                                mm = pe.matmul(B[7][:, t * HD:(t + 1) * HD], lat[:, kk, t * P:(t + 1) * P],
                                               ukv[:, j, kk, NOPE:], start=(kk == 0), stop=(kk == KK - 1))
                        mm.then_inc(S["v_made"], 1)
                    elif p == 6:
                        pe.wait_ge(S["v_taken"], h + 1)
                        for kk in range(KK):
                            mm = pe.transpose(B[7][:, kk * P:(kk + 1) * P], ukv[:, j, kk, :], k.mask("ident"))
                        mm.then_inc(S["ukt_made"], 1)
                    else:
                        pe.wait_ge(S["ukt_taken"], h + 1)
                        for kk in range(KK):
                            mm = pe.matmul(B[7][:, kk * TS:(kk + 1) * TS], ukT[:, j, kk * P:(kk + 1) * P], qT[0:NOPE, j, TP:T],
                                           start=True, stop=True)
                        mm.then_inc(S["qabs_made"], 1)

                def scores(h, j, i):
                    n_keys = (i + 1) * P
                    for c in range(0, n_keys, 512):
                        w = min(512, n_keys - c)
                        pe.matmul(B[2 * (i % 2) + c // 512][:, 0:w], qT[0:QH, j, i * P:(i + 1) * P],
                                  kT[0:QH, j, c:c + w], start=True, stop=True)
                    mm = pe.matmul(B[2 * (i % 2) + i // 4][:, i % 4 * P:(i % 4 + 1) * P], k.mask("ident"), k.mask("causal"),
                                   start=False, stop=True, skip_group_check=True)
                    mm.then_inc(S["s_made"], 1)

                def transposes(h, i):
                    pe.wait_ge(S["e_done"], TILES * h + i + 1)
                    for g in range(GROUPS[i]):
                        n = GSUM[i] - GROUPS[i] + g
                        pe.wait_ge(S["t_taken"], NG * h + n + 1)
                        for t in range(4 * g, min(4 * g + 4, i + 1)):
                            mm = pe.transpose(B[4 + n % 2][:, (t % 4) * P:(t % 4 + 1) * P], pr[:, i % 2, t * P:(t + 1) * P],
                                              k.mask("ident"))
                        mm.then_inc(S["t_made"], 1)

                def values(h, j, i):
                    pe.wait_ge(S["t_taken"], NG * h + GSUM[i] + 2)
                    pe.wait_ge(S["o_taken"], TILES * h + i + 1)
                    for t in range(i + 1):
                        mm = pe.matmul(B[6][:, 0:HD], pT[:, i % 2, t * P:(t + 1) * P], v[:, j, t * HD:(t + 1) * HD],
                                       start=(t == 0), stop=(t == i))
                    mm.then_inc(S["o_made"], 1)

                def outputs(h, g):
                    pe.wait_ge(S["o_taken"], TILES * h + 4 * g + 5)
                    for t in range(4):
                        mm = pe.transpose(B[7][:, t * P:(t + 1) * P], ot[:, 4 * g + t, :], k.mask("ident"))
                    mm.then_inc(S["ot_made"], 1)

                def head(it, j, follows=True):
                    h = 2 * it + j
                    for i in range(TILES):
                        transposes(h, i)
                        if i + 2 < TILES:
                            scores(h, j, i + 2)
                        elif follows:
                            scores(h + 1, 1 - j, i + 2 - TILES)
                        if follows:
                            if i == 0:
                                pe.wait_ge(S["qabs_taken"], h + 1)
                                if j == 0:
                                    pe.wait_ge(S["ot_taken"], 2 * it + 1)
                            if i == 6 and j == 1:
                                pe.wait_ge(S["ot_taken"], 2 * it + 2)
                            piece(h + 1, 1 - j, i)
                        values(h, j, i)
                        if j == 1 and i == 5:
                            pe.wait_ge(S["v_taken"] if follows else S["qabs_taken"], h + 2 if follows else NH)
                            outputs(h, 0)
                        if j == 1 and i == 7:
                            pe.wait_ge(S["qabs_taken"], h + 2 if follows else NH)
                            if not follows:
                                pe.wait_ge(S["ot_taken"], 2 * it + 2)
                            outputs(h, 1)
                pe.wait_ge(S["kr_there"], 2)
                pe.wait_ge(nq.S["root"], 3)
                for p in range(8):
                    piece(0, 0, p)
                scores(0, 0, 0)
                scores(0, 0, 1)
                with pe.Fori(0, NH // 2 - 1) as it:
                    head(it, 0)
                    head(it, 1)
                head(NH // 2 - 1, 0)
                head(NH // 2 - 1, 1, False)

            @block.scalar
            def _(act):
                nkv.act(act)
                nq.act(act)
                act.sem_inc(S["t_taken"], 2)

                def exponential(h, i):
                    act.wait_ge(S["m_ready"], TILES * h + i + 1)
                    act.activation(pr[:, i % 2, 0:(i + 1) * P], k.psum[:, 1024 * (i % 2):1024 * (i % 2) + (i + 1) * P],
                                   ACT.Exp, bias=negm[:, i:i + 1], scale=SCALE,
                                   accum_out=rsum[:, i:i + 1]).then_inc(S["e_done"], 1)

                def copy_out(h, i):
                    for g in range(GROUPS[i]):
                        n = GSUM[i] - GROUPS[i] + g
                        act.wait_ge(S["t_made"], NG * h + n + 1)
                        w = min(4, i + 1 - 4 * g) * P
                        act.activation(pT[:, i % 2, 512 * g:512 * g + w], B[4 + n % 2][:, 0:w], ACT.Copy)\
                           .then_inc(S["t_taken"], 1)

                def piece(h, j, p):
                    if p < 3:
                        act.wait_ge(S["q_made"], 3 * h + p + 1)
                        act.activation(third(qT[0:NOPE, j, :], p), B[7][0:NOPE, 0:C3], ACT.Copy).then_inc(S["q_taken"], 1)
                    elif p < 5:
                        n = p - 3
                        act.wait_ge(S["k_made"], 2 * h + n + 1)
                        act.activation(kT[0:NOPE, j, n * 512:(n + 1) * 512], B[7][0:NOPE, :], ACT.Copy)\
                           .then_inc(S["k_taken"], 1)
                    elif p == 5:
                        act.wait_ge(S["v_made"], h + 1)
                        act.activation(v[:, j, :], B[7], ACT.Copy).then_inc(S["v_taken"], 1)
                    elif p == 6:
                        act.wait_ge(S["ukt_made"], h + 1)
                        act.activation(ukT[:, j, :], B[7][0:HD, 0:KVL], ACT.Copy).then_inc(S["ukt_taken"], 1)

                def head(it, j, follows=True):
                    h = 2 * it + j
                    for i in range(TILES):
                        if i + 1 < TILES:
                            exponential(h, i + 1)
                        elif follows:
                            exponential(h + 1, 0)
                        copy_out(h, i)
                        if follows:
                            piece(h + 1, 1 - j, i)
                for p in range(8):
                    piece(0, 0, p)
                exponential(0, 0)
                with act.Fori(0, NH // 2 - 1) as it:
                    head(it, 0)
                    head(it, 1)
                head(NH // 2 - 1, 0)
                head(NH // 2 - 1, 1, False)

            @block.vector
            def _(dve):
                nkv.dve(dve)
                nq.dve(dve)
                dve.sem_inc(S["o_taken"], 1)
                dve.sem_inc(S["ot_taken"], 1)
                for j in range(2):
                    dve.tensor_copy(kT[NOPE:QH, j, :], k.krope[64:96, 0:TP]).then_inc(S["kr_there"], 1)

                def maximum(h, i):
                    ps = k.psum[:, 1024 * (i % 2):1024 * (i % 2) + (i + 1) * P]
                    dve.wait_ge(S["s_made"], TILES * h + i + 1)
                    dve.reduce_max(mx[:, i:i + 1], ps, AX).then_inc(S["maxed"], 1)
                    dve.wait_ge(S["maxed"], TILES * h + i + 1)
                    dve.tensor_scalar(negm[:, i:i + 1], mx[:, i:i + 1], -SCALE, None, ALU.mult).then_inc(S["m_ready"], 1)

                def piece(h, j, p):
                    if p < 3:
                        n, c = 3 * h + p + 1, slice(p * C3, (p + 1) * C3)
                        dve.wait_ge(S["q_made"], n)
                        dve.tensor_tensor(qT[64:96, j, c], B[7][64:96, 0:C3], k.rot[64:96, 0, c], ALU.mult)\
                           .then_inc(S["qr_cos"], 1)
                        dve.tensor_tensor(u[64:96, :], B[7][96:128, 0:C3], k.rot[96:128, 1, c], ALU.mult)\
                           .then_inc(S["qr_sin"], 1)
                        dve.wait_ge(S["qr_cos"], n)
                        dve.wait_ge(S["qr_sin"], n)
                        dve.tensor_tensor(qT[64:96, j, c], qT[64:96, j, c], u[64:96, :], ALU.add)\
                           .then_inc(S["qr_taken"], 1)
                        dve.wait_ge(S["qr_taken"], n)
                    elif p == 7:
                        dve.wait_ge(S["qabs_made"], h + 1)
                        for kk in range(KK):
                            last = dve.tensor_copy(
                                qabs[:, kk, :, bass.ds(h, 1), :],
                                B[7][:, kk * TS:(kk + 1) * TS].rearrange("p (b t) -> p b t", b=NB))
                        dve.tensor_copy(qrope[0:ROPE, :, bass.ds(h, 1), :],
                                        qT[64:96, j, TP:T].rearrange("p (b t) -> p b t", b=NB))
                        last.then_inc(S["qabs_taken"], 1)

                def head(it, j, follows=True):
                    h = 2 * it + j
                    for i in range(TILES):
                        dve.wait_ge(S["e_done"], TILES * h + i + 1)
                        dve.reciprocal(rinv[:, i:i + 1], rsum[:, i:i + 1]).then_inc(S["r_done"], 1)
                        if i + 2 < TILES:
                            maximum(h, i + 2)
                        elif follows:
                            maximum(h + 1, i + 2 - TILES)
                        if follows:
                            piece(h + 1, 1 - j, i)
                        dve.wait_ge(S["o_made"], TILES * h + i + 1)
                        dve.wait_ge(S["r_done"], TILES * h + i + 1)
                        dve.tensor_scalar(ot[:, i, j * HD:(j + 1) * HD], B[6][:, 0:HD], rinv[:, i:i + 1], None, ALU.mult)\
                           .then_inc(S["o_taken"], 1)
                        if j == 1 and i in (5, 7):
                            g = (i - 5) // 2
                            dve.wait_ge(S["ot_made"], 2 * it + g + 1)
                            dve.tensor_copy(k.mla[:, bass.ds(it, 1), g * 512:(g + 1) * 512], B[7].unsqueeze(1))\
                               .then_inc(S["ot_taken"], 1)
                for p in range(8):
                    piece(0, 0, p)
                maximum(0, 0)
                maximum(0, 1)
                with dve.Fori(0, NH // 2 - 1) as it:
                    head(it, 0)
                    head(it, 1)
                head(NH // 2 - 1, 0)
                head(NH // 2 - 1, 1, False)


def mla_sample_stage(k, free_y, free_cq, qabs, qrope):
    nc, io = k.nc, k.io
    R = NH * TSEQ
    GP, LW, GC = 4, KVL + ROPE, 4 * PAGE
    NGP = NPG // GP
    S = {n: k.sem(f"ms_{n}") for n in (
        "pg", "w", "kr0", "q_there", "t_made", "t_taken", "s_made", "s_copied", "s_taken", "n_made", "n_masked", "new_taken",
        "maxed", "m_ready", "e_done", "r_done", "pt_made", "pt_taken", "x_made", "x_taken", "o_made", "o_taken", "ot_made", "ot_taken", "uv_made")}
    LOADED = (0, 1, 3, 4, 6), (2, 5, 7)
    k_in = [[[k.sem(f"ms_k{e}{j}{g}") for g in range(NGP)] for j in range(2)] for e in "sp"]
    loads = [[2 * sum(n % 8 in mine for n in range(GP * g, GP * (g + 1))) for g in range(NGP)] for mine in LOADED]
    B = k.bank
    lat = k.cqkv[:, QK:QK + KK, :]
    sc = k.at(free_y, "ms_sc", [R, 2, PAST + TSEQ])
    kT = k.at(free_cq, "ms_kT", [P, 2, KK, GC])
    krT = k.at(free_cq, "ms_krT", [ROPE, 2, GC], words=2 * KK * GC)
    rw = k.rw
    X = {n: k.sem(f"sh_{n}") for n in ("in", "last", "diff", "first", "shifted", "out")}
    with ExitStack() as ctx:
        sh0 = k.sb(ctx, "sh_0", [P, RWK, NB])
        last = k.sb(ctx, "sh_last", [P, RWK, 1 + NB])
        tmp = k.sb(ctx, "sh_tmp", [P, 2, T])
        pages = k.sb(ctx, "ms_pages", [1, NB * NPG], I32)
        keys = k.sb(ctx, "ms_keys", [P, 2, NPG, LW])
        kr0 = k.sb(ctx, "ms_kr0", [ROPE, TS])
        qb = k.sb(ctx, "ms_qb", [P, 2, KK, R])
        qrb = k.sb(ctx, "ms_qrb", [ROPE, 2, R])
        krn = k.sb(ctx, "ms_krn", [ROPE, 2, TSEQ])
        newT = k.sb(ctx, "ms_newT", [P, 2, KK, TSEQ])
        new = k.sb(ctx, "ms_new", [TSEQ, KVL])
        pT = k.sb(ctx, "ms_pT", [P, NPG * R])
        pnT = k.sb(ctx, "ms_pnT", [TSEQ, R])
        ol = k.sb(ctx, "ms_ol", [R, KVL])
        olT = k.sb(ctx, "ms_olT", [P, KK, NH, NB, TSEQ])
        gmax = k.sb(ctx, "ms_gmax", [R, NGP + 1])
        stat = k.sb(ctx, "ms_stat", [R, 4])
        wuv = k.sb(ctx, "ms_wuv", [P, KK, NH, HD])
        new_sc, new_tr, x_tr = B[7][0:R, 0:TSEQ], B[7][0:TSEQ, 16:16 + KVL], B[7][0:TSEQ, 288:288 + R]
        o_ps, o_tr = B[7][0:R, 0:KVL], B[7][:, 384:384 + KK * R]

        def batches(eng, step, tail):
            step(0, 0, False)
            with eng.Fori(0, (NB - 2) // 2) as i:
                step(2 * i + 1, 1, True)
                step(2 * i + 2, 0, True)
            step(NB - 1, 1, True)
            tail(NB - 1, 1)

        def load_keys(eng, e):
            eng.wait_ge(S["pg"], 16)

            def load(b, j):
                for n in range(NPG):
                    if n % 8 in LOADED[e]:
                        page = eng.value_load(pages[0:1, bass.ds(b * NPG + n, 1)], min_val=0, max_val=io["lat"].shape[0] - 1)
                        eng.dma_start(keys[:, j, n, 0:KVL], io["lat"][bass.ds(page, 1)].rearrange("a p c -> p (a c)"))\
                           .then_inc(k_in[e][j][n // GP], 16)
                        eng.dma_start(keys[:, j, n, KVL:LW], io["kr"][bass.ds(page, 1)].rearrange("a p c -> p (a c)"))\
                           .then_inc(k_in[e][j][n // GP], 16)
            load(0, 0)
            load(1, 1)
            with eng.Fori(1, NB // 2) as i:
                for j in range(2):
                    eng.wait_ge(S["o_made"], 2 * i + j - 1)
                    load(2 * i + j, j)
        with nc.Block() as block:
            @block.sync
            def _(sp):
                sp.dma_start(pages[:, :], io["pages"]).then_inc(S["pg"], 16)
                sp.dma_start(sh0[:, :, :], io["shift0"]).then_inc(X["in"], 16)
                load_keys(sp, 0)
                sp.wait_ge(X["last"], 2)
                sp.dma_start(io["o_shift"], last[:, :, :]).then_inc(X["out"], 16)
                sp.wait_ge(X["out"], 16)
                for kk in range(KK):
                    sp.dma_start(wuv[:, kk, :, :], io["w_ukv"].rearrange("h p (k m) -> p k h m", k=KK)[:, kk, :, HD:])\
                      .then_inc(S["w"], 16)

            @block.gpsimd
            def _(pool):
                load_keys(pool, 1)

            @block.tensor
            def _(pe):
                def transposes(b, j, g):
                    for e in range(2):
                        pe.wait_ge(k_in[e][j][g], 8 * loads[e][g] * (b - j + 2))
                    pe.wait_ge(S["t_taken"], 3 * (NGP * b + g + 1))
                    for n in range(GP):
                        pg, c = GP * g + n, slice(n * PAGE, (n + 1) * PAGE)
                        for kk in range(KK):
                            pe.transpose(B[2 * (g % 2) + kk][:, c], keys[:, j, pg, kk * P:(kk + 1) * P], k.mask("ident"))
                        mm = pe.transpose(B[4][0:ROPE, c], keys[:, j, pg, KVL:LW], k.mask("ident"))
                    mm.then_inc(S["t_made"], 1)

                def scores(b, j, g):
                    pe.wait_ge(S["q_there"], 4 * (b + 1))
                    pe.wait_ge(S["t_taken"], 3 * (NGP * b + g + 2))
                    pe.wait_ge(S["s_taken"], NGP * b + g + 1)
                    for kk in range(KK):
                        pe.matmul(B[5][0:R, :], qb[:, j, kk, :], kT[:, g % 2, kk, :], start=(kk == 0), stop=False)
                    pe.matmul(B[5][0:R, :], qrb[:, j, :], krT[:, g % 2, :], start=False, stop=True).then_inc(S["s_made"], 1)

                def new_tokens(b, j):
                    pe.wait_ge(S["ot_taken"], b + 1)
                    for kk in range(KK):
                        pe.matmul(new_sc, qb[:, j, kk, :], newT[:, j, kk, :], start=(kk == 0), stop=False)
                    pe.matmul(new_sc, qrb[:, j, :], krn[:, j, :], start=False, stop=True)
                    for kk in range(KK):
                        mm = pe.transpose(new_tr[:, kk * P:(kk + 1) * P], newT[:, j, kk, :], k.mask("ident"))
                    mm.then_inc(S["n_made"], 1)

                def probabilities(b, j):
                    pe.wait_ge(S["e_done"], b + 1)
                    pe.wait_ge(S["new_taken"], b + 1)
                    pe.transpose(B[6][:, 0:P], k.mask("ident"), k.mask("ident"))
                    for n in range(NPG):
                        mm = pe.transpose(B[6][:, n * R:(n + 1) * R], sc[:, j, n * PAGE:(n + 1) * PAGE], k.mask("ident", R, R))
                    mm.then_inc(S["pt_made"], 1)
                    pe.transpose(x_tr, sc[:, j, PAST:], k.mask("ident", R, R)).then_inc(S["x_made"], 1)

                def outputs(b, j):
                    pe.wait_ge(S["pt_taken"], b + 1)
                    pe.wait_ge(S["x_taken"], b + 1)
                    for n in range(NPG):
                        pe.matmul(o_ps, pT[:, n * R:(n + 1) * R], keys[:, j, n, 0:KVL], start=(n == 0), stop=False)
                    pe.matmul(o_ps, pnT[:, :], new[:, :], start=False, stop=True).then_inc(S["o_made"], 1)

                def turn_outputs(b):
                    pe.wait_ge(S["o_taken"], b + 1)
                    for kk in range(KK):
                        mm = pe.matmul(o_tr[:, kk * R:(kk + 1) * R], ol[:, kk * P:(kk + 1) * P], k.mask("ident", R, R),
                                       start=True, stop=True)
                    mm.then_inc(S["ot_made"], 1)

                def step(b, j, before):
                    transposes(b, j, 0)
                    if before:
                        scores(b - 1, 1 - j, NGP - 1)
                        new_tokens(b - 1, 1 - j)
                    transposes(b, j, 1)
                    scores(b, j, 0)
                    if before:
                        probabilities(b - 1, 1 - j)
                    transposes(b, j, 2)
                    if before:
                        outputs(b - 1, 1 - j)
                    scores(b, j, 1)
                    if before:
                        turn_outputs(b - 1)
                    transposes(b, j, 3)
                    scores(b, j, 2)

                def tail(b, j):
                    scores(b, j, NGP - 1)
                    new_tokens(b, j)
                    probabilities(b, j)
                    outputs(b, j)
                    turn_outputs(b)
                pe.wait_ge(S["kr0"], 1)
                batches(pe, step, tail)
                pe.wait_ge(S["ot_taken"], NB + 1)
                pe.wait_ge(S["w"], 16 * KK)
                for h in range(NH):
                    for kk in range(KK):
                        mm = pe.matmul(B[h % 2][h % 2 * HD:(h % 2 + 1) * HD, h // 2 * TS:(h // 2 + 1) * TS],
                                       wuv[:, kk, h, :], olT[:, kk, h, :, :].rearrange("p b t -> p (b t)"),
                                       start=(kk == 0), stop=(kk == KK - 1))
                mm.then_inc(S["uv_made"], 1)

            @block.scalar
            def _(act):
                act.activation(kr0[:, :], k.krope[64:96, TP:T], ACT.Copy).then_inc(S["kr0"], 1)
                act.sem_inc(S["t_taken"], 3)
                act.sem_inc(S["ot_taken"], 1)
                act.wait_ge(S["kr0"], 1)

                def copy_keys(b, j, g):
                    act.wait_ge(S["t_made"], NGP * b + g + 1)
                    act.activation(krT[:, g % 2, :], B[4][0:ROPE, :], ACT.Copy).then_inc(S["t_taken"], 1)
                    for kk in range(KK):
                        act.activation(kT[:, g % 2, kk, :], B[2 * (g % 2) + kk], ACT.Copy).then_inc(S["t_taken"], 1)

                def exponential(b, j):
                    act.wait_ge(S["m_ready"], b + 1)
                    act.activation(sc[:, j, :], sc[:, j, :], ACT.Exp, bias=stat[:, 1:2], scale=SCALE, accum_out=stat[:, 2:3])\
                       .then_inc(S["e_done"], 1)

                def copy_probabilities(b):
                    act.wait_ge(S["pt_made"], b + 1)
                    act.activation(pT[:, :], B[6], ACT.Copy).then_inc(S["pt_taken"], 1)

                def copy_outputs(b):
                    act.wait_ge(S["ot_made"], b + 1)
                    for kk in range(KK):
                        last = act.activation(olT[:, kk, :, bass.ds(b, 1), :],
                                              o_tr[:, kk * R:(kk + 1) * R].rearrange("p (h t) -> p h t", h=NH), ACT.Copy)
                    last.then_inc(S["ot_taken"], 1)

                def step(b, j, before):
                    act.activation(qb[:, j, :, :], qabs[:, :, bass.ds(b, 1), :, :].rearrange("p k b h t -> p k (b h t)"),
                                   ACT.Copy).then_inc(S["q_there"], 1)
                    act.activation(qrb[:, j, :], qrope[:, bass.ds(b, 1), :, :].rearrange("p b h t -> p (b h t)"),
                                   ACT.Copy).then_inc(S["q_there"], 1)
                    act.activation(krn[:, j, :], kr0[:, bass.ds(b * TSEQ, TSEQ)], ACT.Copy).then_inc(S["q_there"], 1)
                    act.activation(newT[:, j, :, :], lat[:, :, bass.ds(TP + b * TSEQ, TSEQ)], ACT.Copy)\
                       .then_inc(S["q_there"], 1)
                    copy_keys(b, j, 0)
                    copy_keys(b, j, 1)
                    if before:
                        exponential(b - 1, 1 - j)
                        copy_probabilities(b - 1)
                    copy_keys(b, j, 2)
                    if before:
                        copy_outputs(b - 1)
                    copy_keys(b, j, 3)

                def tail(b, j):
                    exponential(b, j)
                    copy_probabilities(b)
                    copy_outputs(b)
                batches(act, step, tail)

            @block.vector
            def _(dve):
                dve.sem_inc(S["s_taken"], 1)
                dve.tensor_copy(last[:, :, 0:1], rw[:, :, TP - 1:TP]).then_inc(X["last"], 1)
                dve.tensor_copy(last[:, :, 1:], rw[:, :, TP + TSEQ - 1:T:TSEQ]).then_inc(X["last"], 1)
                dve.wait_ge(X["last"], 2)
                dve.wait_ge(X["in"], 16)

                def shift(m, j):
                    p, t, one = rw[:, bass.ds(m, 1), :], tmp[:, j, :].unsqueeze(1), bass.ds(m, 1)
                    dve.tensor_tensor(t[:, :, 1:T], p[:, :, 0:T - 1], p[:, :, 1:T], ALU.subtract).then_inc(X["diff"], 1)
                    dve.tensor_scalar(t[:, :, 0:1], p[:, :, 0:1], -1.0, None, ALU.mult)
                    dve.wait_ge(X["diff"], m + 1)
                    dve.tensor_tensor(t[:, :, TP:T:TSEQ], sh0[:, one, :], p[:, :, TP:T:TSEQ], ALU.subtract).then_inc(X["first"], 1)
                    dve.wait_ge(X["first"], m + 1)
                    dve.scalar_tensor_tensor(p[:, :, 0:T], t[:, :, 0:T], k.vecs[:, bass.ds(VEC["rw_mu"] + m, 1)], p[:, :, 0:T],
                                             ALU.mult, ALU.add).then_inc(X["shifted"], 1)

                def scores(b, j, g):
                    dve.wait_ge(S["s_made"], NGP * b + g + 1)
                    dve.tensor_copy(sc[:, j, g * GC:(g + 1) * GC], B[5][0:R, :]).then_inc(S["s_copied"], 1)
                    dve.reduce_max(gmax[:, g:g + 1], B[5][0:R, :], AX).then_inc(S["s_taken"], 1)

                def maximum(b, j):
                    dve.wait_ge(S["n_made"], b + 1)
                    dve.tensor_tensor(sc[:, j, PAST:], new_sc, k.mask("new_causal", TSEQ, R), ALU.add).then_inc(S["n_masked"], 1)
                    dve.wait_ge(S["n_masked"], 2 * b + 1)
                    dve.reduce_max(gmax[:, NGP:], sc[:, j, PAST:], AX).then_inc(S["n_masked"], 1)
                    dve.wait_ge(S["n_masked"], 2 * b + 2)
                    dve.wait_ge(S["s_taken"], NGP * (b + 1) + 1)
                    dve.reduce_max(stat[:, 0:1], gmax[:, :], AX).then_inc(S["maxed"], 1)
                    dve.wait_ge(S["maxed"], b + 1)
                    dve.tensor_scalar(stat[:, 1:2], stat[:, 0:1], -SCALE, None, ALU.mult).then_inc(S["m_ready"], 1)
                    dve.tensor_copy(new[:, :], new_tr).then_inc(S["new_taken"], 1)

                def divide(b, j):
                    dve.wait_ge(S["e_done"], b + 1)
                    dve.reciprocal(stat[:, 3:4], stat[:, 2:3]).then_inc(S["r_done"], 1)

                def new_probabilities(b):
                    dve.wait_ge(S["x_made"], b + 1)
                    dve.wait_ge(S["new_taken"], b + 1)
                    dve.tensor_copy(pnT[:, :], x_tr).then_inc(S["x_taken"], 1)

                def take_outputs(b):
                    dve.wait_ge(S["o_made"], b + 1)
                    dve.wait_ge(S["r_done"], b + 1)
                    dve.tensor_scalar(ol[:, :], o_ps, stat[:, 3:4], None, ALU.mult).then_inc(S["o_taken"], 1)

                def step(b, j, before):
                    if before:
                        scores(b - 1, 1 - j, NGP - 1)
                        maximum(b - 1, 1 - j)
                        divide(b - 1, 1 - j)
                    scores(b, j, 0)
                    if before:
                        new_probabilities(b - 1)
                        take_outputs(b - 1)
                    scores(b, j, 1)
                    more = not (isinstance(b, int) and b == NB - 1)
                    if more:
                        shift(2 * b, 0)
                    scores(b, j, 2)
                    if more:
                        shift(2 * b + 1, 1)

                def tail(b, j):
                    scores(b, j, NGP - 1)
                    maximum(b, j)
                    divide(b, j)
                    new_probabilities(b)
                    take_outputs(b)
                batches(dve, step, tail)
                dve.wait_ge(S["uv_made"], 1)
                for j in range(2):
                    dve.tensor_copy(k.mla[j * HD:(j + 1) * HD, :, TP:T],
                                    B[j][j * HD:(j + 1) * HD, 0:4 * TS].rearrange("p (h n) -> p h n", h=4))


def rwkv_prep_stage(k, c, a, kk, keep):
    nc, io, rw = k.nc, k.io, k.rw
    B = k.bank
    S = {n: k.sem(f"rp_{n}") for n in (
        "in", "w", "own", "zero", "half", "tanh", "z_made", "z_taken", "a_made", "a_taken", "kk", "sq", "ss_made",
        "root", "inv", "bc_made", "bc_taken",
        "m_squared", "m_added", "m_sums", "m_root", "m_inv")}
    G = 4
    with ExitStack() as ctx:
        msq = k.sb(ctx, "rp_msq", [P, 2, T])
        tmp = k.sb(ctx, "rp_tmp", [P, 2, T])
        w2 = k.sb(ctx, "rp_w2", [P, 512])
        hb = k.sb(ctx, "rp_hb", [P, 2 * G])
        with nc.Block() as block:
            @block.sync
            def _(sp):
                sp.dma_start(keep[:, :], io["keep"]).then_inc(S["in"], 16)
                sp.dma_start(w2[0:64, :], io["rw_w2"]).then_inc(S["w"], 16)
                sp.dma_start(w2[64:128, :], io["rw_a2"]).then_inc(S["w"], 16)

            @block.gpsimd
            def _(pool):
                pool.memset(c[:, :, 0:1], 0.0).then_inc(S["zero"], 1)
                pool.memset(c[:, :, 1 + T:], 0.0).then_inc(S["zero"], 1)
                pool.memset(a[:, :, T:], 0.0).then_inc(S["zero"], 1)
                pool.memset(kk[:, :, T:], 0.0).then_inc(S["zero"], 1)
                for i in range(1, 4):
                    pool.wait_ge(S["m_squared"], i + 1)
                    if i >= 2:
                        pool.wait_ge(S["m_added"], i - 1)
                    pool.tensor_tensor(k.acc, msq[:, 0, :] if i == 1 else k.acc, msq[:, i % 2, :], ALU.add).then_inc(S["m_added"], 1)
                pool.wait_ge(S["m_inv"], 3)
                for i in range(4):
                    pool.tensor_tensor(k.mla[:, i, :], k.mla[:, i, :], k.acc, ALU.mult)

            @block.tensor
            def _(pe):
                pe.wait_ge(S["w"], 32)
                pe.wait_ge(S["tanh"], 1)
                for q in range(G):
                    for n in range(3):
                        i = 3 * q + n
                        if i >= 2:
                            pe.wait_ge(S["z_taken"], i - 1)
                        pe.matmul(B[i % 2][:, 0:C3], w2[0:64, q * P:(q + 1) * P], third(rw[0:64, 12, 0:T], n),
                                  start=True, stop=True).then_inc(S["z_made"], 1)
                        if i >= 2:
                            pe.wait_ge(S["a_taken"], i - 1)
                        pe.matmul(B[2 + i % 2][:, 0:C3], w2[64:128, q * P:(q + 1) * P], third(rw[64:128, 12, 0:T], n),
                                  start=True, stop=True).then_inc(S["a_made"], 1)
                pe.wait_ge(S["m_added"], 3)
                for n in range(3):
                    if n:
                        pe.wait_ge(S["m_root"], n)
                    pe.matmul(B[7][:, 0:C3], k.mask("ones"), third(k.acc, n), start=True, stop=True).then_inc(S["m_sums"], 1)
                for q in range(G):
                    pe.wait_ge(S["sq"], q + 1)
                    for n in range(3):
                        mm = pe.matmul(B[4 + n][32 * q:32 * q + 32, 0:C3], k.mask("pick", 32), third(tmp[:, q % 2, :], n),
                                       start=True, stop=True)
                    mm.then_inc(S["ss_made"], 1)
                for q in range(G):
                    for n in range(3):
                        i = 3 * q + n
                        pe.wait_ge(S["inv"], 3)
                        if i >= 4:
                            pe.wait_ge(S["bc_taken"], i - 3)
                        pe.matmul(B[i % 4][:, 0:C3], k.masks[32 * q:32 * q + 32, MK["spread"]:MK["spread"] + P],
                                  third(tmp[32 * q:32 * q + 32, 0, :], n), start=True, stop=True).then_inc(S["bc_made"], 1)

            @block.scalar
            def _(act):
                act.activation(rw[0:64, 12, 0:T], rw[0:64, 12, 0:T], ACT.Tanh).then_inc(S["tanh"], 1)
                act.wait_ge(S["half"], 1)
                act.wait_ge(S["zero"], 4)
                for q in range(G):
                    for n in range(3):
                        i = 3 * q + n
                        act.wait_ge(S["z_made"], i + 1)
                        act.activation(c[:, q, 1 + n * C3:1 + (n + 1) * C3], B[i % 2][:, 0:C3], ACT.Tanh,
                                       bias=hb[:, q:q + 1], scale=0.5).then_inc(S["z_taken"], 1)
                        act.wait_ge(S["a_made"], i + 1)
                        act.activation(a[:, q, n * C3:(n + 1) * C3], B[2 + i % 2][:, 0:C3], ACT.Tanh,
                                       bias=hb[:, G + q:G + q + 1], scale=0.5).then_inc(S["a_taken"], 1)
                for i in range(4):
                    if i >= 2:
                        act.wait_ge(S["m_added"], max(1, i - 2))
                    act.activation(msq[:, i % 2, :], k.mla[:, i, :], ACT.Square).then_inc(S["m_squared"], 1)
                for n in range(3):
                    act.wait_ge(S["m_sums"], n + 1)
                    act.activation(third(k.acc, n), B[7][:, 0:C3], ACT.Sqrt, bias=k.mask("eps", 1), scale=1.0 / 512)\
                       .then_inc(S["m_root"], 1)
                for q in range(G):
                    act.wait_ge(S["kk"], q + 1)
                    if q >= 2:
                        act.wait_ge(S["ss_made"], q - 1)
                    act.activation(tmp[:, q % 2, :], kk[:, q, 0:T], ACT.Square).then_inc(S["sq"], 1)
                act.wait_ge(S["ss_made"], G)
                for n in range(3):
                    act.activation(tmp[:, 0, n * C3:(n + 1) * C3], B[4 + n][:, 0:C3], ACT.Sqrt).then_inc(S["root"], 1)

            @block.vector
            def _(dve):
                own = Chain(dve, S["own"])
                dve.wait_ge(S["in"], 16)
                own(dve.tensor_scalar(hb[:, 0:G], k.vecs[:, VEC["rw_w0"]:VEC["rw_w0"] + G], 0.5, None, ALU.mult))
                dve.tensor_scalar(hb[:, G:], k.vecs[:, VEC["rw_a0"]:VEC["rw_a0"] + G], 0.5, None, ALU.mult)\
                   .then_inc(S["half"], 1)
                for q in range(G):
                    dve.tensor_scalar(kk[:, q, 0:T], rw[:, 4 + q, 0:T], k.vec("rw_k_k", q), None, ALU.mult)\
                       .then_inc(S["kk"], 1)
                w = -0.5 * float(np.exp(-0.5))
                for q in range(G):
                    dve.wait_ge(S["z_taken"], 3 * (q + 1))
                    dve.wait_ge(S["a_taken"], 3 * (q + 1))
                    own(dve.tensor_scalar(c[:, q, 1:1 + T], c[:, q, 1:1 + T], w, w, ALU.mult, ALU.add))
                    own(dve.tensor_tensor_scan(c[:, q, 1:1 + TR], keep[:, :], c[:, q, 1:1 + TR], 0.0, ALU.mult, ALU.add))
                    own(dve.tensor_scalar(a[:, q, 0:T], a[:, q, 0:T], 0.5, 0.5, ALU.mult, ALU.add))
                for n in range(3):
                    t = tmp[:, 0, n * C3:(n + 1) * C3]
                    dve.wait_ge(S["root"], n + 1)
                    own(dve.tensor_scalar(t, t, 1e-12, None, ALU.max))
                    dve.reciprocal(t, t).then_inc(S["inv"], 1)
                dve.wait_ge(S["inv"], 3)
                for n in range(3):
                    dve.wait_ge(S["m_root"], n + 1)
                    dve.reciprocal(third(k.acc, n), third(k.acc, n)).then_inc(S["m_inv"], 1)
                for q in range(G):
                    for n in range(3):
                        x = third(kk[:, q, 0:T], n)
                        dve.wait_ge(S["bc_made"], 3 * q + n + 1)
                        dve.tensor_tensor(x, x, B[(3 * q + n) % 4][:, 0:C3], ALU.mult).then_inc(S["bc_taken"], 1)
                    t, kq, aq = tmp[:, 1, :], rw[:, 4 + q, 0:T], a[:, q, 0:T]
                    own(dve.tensor_scalar(t, aq, k.vec("rw_k_a", q), k.vec("rw_k_a", q), ALU.mult, ALU.subtract))
                    own(dve.scalar_tensor_tensor(kq, t, 1.0, kq, ALU.add, ALU.mult))
                    dve.wait_ge(S["bc_taken"], 3 * (q + 1))
                    own(dve.tensor_tensor(aq, aq, kk[:, q, 0:T], ALU.mult))


LEVELS = 6


def rwkv_chunk_stage(k, c, b, kk, keep, free_b, free_kk):
    nc, io, rw = k.nc, k.io, k.rw
    B = k.bank
    S = {n: k.sem(f"rc_{n}") for n in (
        "masks", "zero", "prev", "exp", "bd", "a_made", "vt_made", "a_taken", "l_taken", "vt_taken", 
        "kkt_taken", "lev_made", "n_taken", "t_taken", "mv_made", "mv_taken", "wt_made", "wt_taken", "sa_made", "sa_taken",
        "o_made", "o_taken", "st_made", "s1", "s_ready", "out",
        "ut_made", "ut_taken", "sb_zero", "sx_made", "sx_taken", "ex", "ns_made", "sum", "ns_done")}
    sb_in = [k.sem(f"rc_sb_in{j}") for j in range(2)]
    s_out = [k.sem(f"rc_s_out{j}") for j in range(2)]
    ps = k.psum[:, :].rearrange("p (b n) -> p b n", b=8)
    NT_, N_, TT_ = 0, 1, 2
    with ExitStack() as ctx:
        rm = k.sb(ctx, "rc_masks", [P, 2, 3, P])
        ex_ = k.sb(ctx, "rc_exp", [P, 2, 3, 4, CH])
        prev = k.sb(ctx, "rc_prev", [P, 4, CH])
        KR_ = k.sb(ctx, "rc_KR", [P, 2, 4, 2, P])
        BK_ = k.sb(ctx, "rc_BK", [P, 2, 4, 3, P])
        A4 = k.sb(ctx, "rc_A4", [P, 4, 4, P])
        W = k.sb(ctx, "rc_W", [P, 4, 3, P])
        tm = k.sb(ctx, "rc_tm", [P, 4, 4, P])
        MV = k.sb(ctx, "rc_MV", [P, 4, P])
        WT = k.sb(ctx, "rc_WT", [P, 4, P])
        SA = k.sb(ctx, "rc_SA", [P, 4, P])
        St = k.sb(ctx, "rc_S", [P, 4, P])
        S1 = k.sb(ctx, "rc_S1", [P, 4, P])

        def pe_common(pe, c_, sl):
            KR, BK = KR_[:, sl], BK_[:, sl]
            pe.wait_ge(S["bd"], 10 * (c_ + 1))
            for hf in range(2):
                for p in (2 * hf, 2 * hf + 1):
                    kr = KR[:, p].rearrange("p a n -> p (a n)")
                    pe.matmul(B[4 + p][:, 0:256], BK[:, p, 0, :], kr, start=True, stop=True)
                    pe.matmul(B[4 + p][:, 256:512], BK[:, p, 1, :], kr, start=True, stop=True)
                pe.wait_ge(S["s_ready"], 4 * (c_ + 1))
                pe.wait_ge(S["o_taken"], 4 * (c_ + 1))
                for p in (2 * hf, 2 * hf + 1):
                    mm = pe.matmul(B[p][:, 0:P], KR[:, p, 0, :], BK[:, p, 0, :], start=True, stop=True)
                mm.then_inc(S["a_made"], 1)
                for p in (2 * hf, 2 * hf + 1):
                    for j in range(3):
                        mm = pe.transpose(B[p][:, (1 + j) * P:(2 + j) * P], BK[:, p, j, :], k.mask("ident"))
                mm.then_inc(S["vt_made"], 1)
            for lev in range(LEVELS):
                for hf in range(2):
                    i = 2 * c_ + hf + 1
                    if lev == 0:
                        pe.wait_ge(S["a_taken"], i)
                        pe.wait_ge(S["l_taken"], i)
                    else:
                        if lev == 1:
                            pe.wait_ge(S["mv_taken"], i)
                            pe.wait_ge(S["kkt_taken"], i)
                        pe.wait_ge(S["n_taken"], 10 * c_ + 2 * (lev - 1) + hf + 1)
                        pe.wait_ge(S["t_taken"], 12 * c_ + 2 * (lev - 1) + hf + 1)
                    for p in (2 * hf, 2 * hf + 1):
                        o = B[4 + p]
                        if lev == 0:
                            pe.matmul(o[:, 0:P], W[:, p, N_, :], A4[:, p, 0, :], start=True, stop=True)
                            pe.matmul(o[:, P:256], A4[:, p, 0, :], W[:, p, N_, :], start=True, stop=True)
                            mm = pe.transpose(o[:, 384:512], KR[:, p, 0, :], k.mask("ident"))
                            continue
                        mm = pe.matmul(B[p][:, 0:P], W[:, p, N_, :], W[:, p, TT_, :], start=True, stop=True)
                        if lev < LEVELS - 2:
                            pe.matmul(o[:, 0:P], W[:, p, N_, :], W[:, p, NT_, :], start=True, stop=True)
                        if lev < LEVELS - 1:
                            mm = pe.matmul(o[:, P:256], W[:, p, NT_, :], W[:, p, N_, :], start=True, stop=True)
                    mm.then_inc(S["lev_made"], 1)
                    if lev == 0:
                        pe.wait_ge(S["vt_taken"], i)
                        for p in (2 * hf, 2 * hf + 1):
                            mm = pe.matmul(B[p][:, 0:P], A4[:, p, 2, :], tm[:, p, 2, :], start=True, stop=True)
                        mm.then_inc(S["mv_made"], 1)
            for hf in range(2):
                i = 2 * c_ + hf + 1
                pe.wait_ge(S["t_taken"], 12 * c_ + 10 + hf + 1)
                pe.wait_ge(S["kkt_taken"], i)
                for p in (2 * hf, 2 * hf + 1):
                    mm = pe.matmul(B[p][:, P:2 * P], tm[:, p, 3, :], W[:, p, TT_, :], start=True, stop=True)
                mm.then_inc(S["wt_made"], 1)

        def exponential(act, c_, sl, n):
            tok = bass.ds(1 + c_ * CH, CH)
            if n == 0:
                act.wait_ge(S["s_ready"], 4 * c_ if not isinstance(c_, int) or c_ else 4)
                act.activation(ex_[:, sl, 0], c[:, :, tok], ACT.Exp).then_inc(S["exp"], 1)
            elif n == 1:
                act.activation(ex_[:, sl, 1], c[:, :, tok], ACT.Exp, scale=-1.0).then_inc(S["exp"], 1)
            else:
                act.wait_ge(S["prev"], c_ + 1)
                act.activation(ex_[:, sl, 2], prev[:, :, :], ACT.Exp).then_inc(S["exp"], 1)

        def act_common(act, c_, sl, ahead=True):
            for hf in range(2):
                i, pp = 2 * c_ + hf + 1, slice(2 * hf, 2 * hf + 2)
                act.wait_ge(S["l_taken"], i)
                act.activation(tm[:, pp, 0:3, :].rearrange("p a b n -> p a (b n)"), ps[:, pp, P:512], ACT.Copy)\
                   .then_inc(S["vt_taken"], 1)
            for lev in range(LEVELS - 1):
                for hf in range(2):
                    i, pp = 2 * c_ + hf + 1, slice(2 * hf, 2 * hf + 2)
                    bk = slice(4 + 2 * hf, 6 + 2 * hf)
                    act.wait_ge(S["lev_made"], 12 * c_ + 2 * lev + hf + 1)
                    if lev < LEVELS - 2:
                        act.activation(W[:, pp, 0:2, :].rearrange("p b a n -> p b (a n)"), ps[:, bk, 0:256], ACT.Copy)\
                           .then_inc(S["n_taken"], 1)
                    else:
                        act.activation(W[:, pp, N_, :], ps[:, bk, P:256], ACT.Copy).then_inc(S["n_taken"], 1)
                    if lev == 0:
                        act.activation(tm[:, pp, 3, :], ps[:, bk, 384:512], ACT.Copy).then_inc(S["kkt_taken"], 1)
                        act.wait_ge(S["mv_made"], i)
                        act.activation(MV[:, pp, :], ps[:, pp, 0:P], ACT.Copy).then_inc(S["mv_taken"], 1)
                if ahead and lev < 3:
                    exponential(act, c_ + 1, 1 - sl, lev)
            for hf in range(2):
                pp = slice(2 * hf, 2 * hf + 2)
                act.wait_ge(S["wt_made"], 2 * c_ + hf + 1)
                act.activation(WT[:, pp, :], ps[:, pp, P:2 * P], ACT.Copy).then_inc(S["wt_taken"], 1)

        def decay_before(dve, c_):
            tok = bass.ds(c_ * CH, CH)
            dve.tensor_tensor(prev[:, :, :], c[:, :, tok], keep[:, tok].unsqueeze(1).broadcast_to([P, 4, CH]), ALU.mult)\
               .then_inc(S["prev"], 1)

        def scaled(dve, c_, sl, n):
            tok = bass.ds(c_ * CH, CH)
            KR, BK, ex = KR_[:, sl], BK_[:, sl], ex_[:, sl]
            for hh in range(2):
                h, o = slice(hh * CH, (hh + 1) * CH), slice(hh * CH, (hh + 1) * CH)
                if n == 0:
                    ins = dve.tensor_copy(BK[h, :, 2, o], rw[h, 8:12, tok])
                elif n == 1:
                    dve.wait_ge(S["exp"], 3 * c_ + 1)
                    ins = dve.tensor_tensor(KR[h, :, 1, o], rw[h, 0:4, tok], ex[h, 0], ALU.mult)
                elif n == 2:
                    dve.wait_ge(S["exp"], 3 * c_ + 2)
                    ins = dve.tensor_tensor(BK[h, :, 0, o], b[h, :, tok], ex[h, 1], ALU.mult)
                elif n == 3:
                    ins = dve.tensor_tensor(BK[h, :, 1, o], rw[h, 4:8, tok], ex[h, 1], ALU.mult)
                else:
                    dve.wait_ge(S["exp"], 3 * c_ + 3)
                    ins = dve.tensor_tensor(KR[h, :, 0, o], kk[h, :, tok], ex[h, 2], ALU.mult)
                ins.then_inc(S["bd"], 1)

        def dve_common(dve, c_, sl, g, ahead=True):
            if ahead:
                decay_before(dve, c_ + 1)
            for hf in range(2):
                i, pp, bk = 2 * c_ + hf + 1, slice(2 * hf, 2 * hf + 2), slice(4 + 2 * hf, 6 + 2 * hf)
                dve.wait_ge(S["a_made"], i)
                for j in range(2):
                    q = slice(2 * j, 2 * j + 2)
                    last = dve.tensor_tensor(
                        A4[:, pp, q, :].rearrange("p b a n -> p b (a n)"), ps[:, bk, 256 * j:256 * (j + 1)],
                        rm[:, g, 1:3, :].rearrange("p a n -> p (a n)").unsqueeze(1).broadcast_to([P, 2, 256]), ALU.mult)
                last.then_inc(S["a_taken"], 1)
                dve.wait_ge(S["vt_made"], i)
                dve.tensor_tensor(W[:, pp, N_, :], ps[:, pp, 0:P], rm[:, g, 0, :].unsqueeze(1).broadcast_to([P, 2, P]),
                                  ALU.mult).then_inc(S["l_taken"], 1)
                dve.wait_ge(S["a_taken"], i)
                dve.scalar_tensor_tensor(W[:, pp, TT_, :], A4[:, pp, 0, :], -1.0,
                                         k.mask("ident").unsqueeze(1).broadcast_to([P, 2, P]), ALU.mult, ALU.add)\
                   .then_inc(S["t_taken"], 1)
            for lev in range(1, LEVELS):
                for hf in range(2):
                    pp, bk = slice(2 * hf, 2 * hf + 2), slice(4 + 2 * hf, 6 + 2 * hf)
                    dve.wait_ge(S["lev_made"], 12 * c_ + 2 * lev + hf + 1)
                    dve.wait_ge(S["t_taken"], 12 * c_ + 2 * (lev - 1) + hf + 1)
                    dve.tensor_tensor(W[:, pp, TT_, :], W[:, pp, TT_, :], ps[:, pp, 0:P], ALU.add)\
                       .then_inc(S["t_taken"], 1)
                if ahead:
                    scaled(dve, c_ + 1, 1 - sl, lev - 1)

        with nc.Block() as block:
            @block.sync
            def _(sp):
                sp.dma_start(rm[:, :, :, :].rearrange("p a b n -> p (a b n)"), io["rwmasks"]).then_inc(S["masks"], 16)
                sp.wait_ge(S["s_ready"], 4 * (NCH + 1))
                for j in range(2):
                    h = slice(j * HD, (j + 1) * HD)
                    sp.dma_start(io["o_rwkv_p"].rearrange("(q j) k v -> j k q v", j=2)[j], St[h, :, h]).then_inc(S["out"], 16)
                sp.wait_ge(S["out"], 32)

            @block.gpsimd
            def _(pool):
                pool.memset(KR_[:, :, :, :, :], 0.0).then_inc(S["zero"], 1)
                pool.memset(BK_[:, :, :, :, :], 0.0).then_inc(S["zero"], 1)
                pool.memset(St[:, :, :], 0.0).then_inc(S["zero"], 1)

            @block.tensor
            def _(pe):
                pe.wait_ge(S["zero"], 3)

                def chunk(c_, sl):
                    KR = KR_[:, sl]
                    pe_common(pe, c_, sl)
                    for hf in range(2):
                        i = 2 * c_ + hf + 1
                        pe.wait_ge(S["mv_taken"], i)
                        pe.wait_ge(S["wt_taken"], i)
                        for p in (2 * hf, 2 * hf + 1):
                            pe.matmul(B[p][:, 256:384], W[:, p, TT_, :], MV[:, p, :], start=True, stop=False)
                            mm = pe.matmul(B[p][:, 256:384], WT[:, p, :], St[:, p, :], start=False, stop=True)
                        mm.then_inc(S["sa_made"], 1)
                    for hf in range(2):
                        i = 2 * c_ + hf + 1
                        pe.wait_ge(S["sa_taken"], i)
                        for p in (2 * hf, 2 * hf + 1):
                            pe.matmul(B[p][:, 0:P], tm[:, p, 0, :], SA[:, p, :], start=True, stop=False)
                            mm = pe.matmul(B[p][:, 0:P], tm[:, p, 1, :], tm[:, p, 2, :], start=False, stop=True)
                            pe.matmul(B[p][:, 384:512], St[:, p, :], KR[:, p, 1, :], start=True, stop=False)
                            pe.matmul(B[p][:, 384:512], SA[:, p, :], A4[:, p, 1, :], start=False, stop=False)
                            mm = pe.matmul(B[p][:, 384:512], tm[:, p, 2, :], A4[:, p, 3, :], start=False, stop=True)
                        mm.then_inc(S["o_made"], 1)
                with pe.Fori(0, NCH // 2) as i:
                    chunk(2 * i, 0)
                    chunk(2 * i + 1, 1)

            @block.scalar
            def _(act):
                def chunk(c_, sl):
                    act_common(act, c_, sl)
                    act.wait_ge(S["exp"], 3 * (c_ + 1))
                    act.wait_ge(S["s_ready"], 4 * (c_ + 1))
                    for p in range(4):
                        act.activation(S1[:, p, :], St[:, p, :], ACT.Copy, scale=ex_[:, sl, 0, p, CH - 1:CH]).then_inc(S["s1"], 1)
                for n in range(3):
                    exponential(act, 0, 0, n)
                with act.Fori(0, NCH // 2) as i:
                    chunk(2 * i, 0)
                    chunk(2 * i + 1, 1)

            @block.vector
            def _(dve):
                dve.wait_ge(S["masks"], 16)
                dve.wait_ge(S["zero"], 3)
                dve.sem_inc(S["s_ready"], 4)
                dve.sem_inc(S["o_taken"], 4)

                def chunk(c_, sl):
                    ex = ex_[:, sl]
                    dve_common(dve, c_, sl, 0)
                    for hf in range(2):
                        pp = slice(2 * hf, 2 * hf + 2)
                        dve.wait_ge(S["sa_made"], 2 * c_ + hf + 1)
                        dve.tensor_scalar(SA[:, pp, :], ps[:, pp, 256:384], -1.0, None, ALU.mult).then_inc(S["sa_taken"], 1)
                    dve.wait_ge(S["s1"], 4 * (c_ + 1))
                    for hf in range(2):
                        dve.wait_ge(S["o_made"], 2 * c_ + hf + 1)
                        for p in (2 * hf, 2 * hf + 1):
                            dve.scalar_tensor_tensor(St[:, p, :], B[p][:, 0:P], ex[:, 0, p, CH - 1:CH], S1[:, p, :],
                                                     ALU.mult, ALU.add).then_inc(S["s_ready"], 1)
                        for hh in range(2):
                            h, pp = slice(hh * HD, (hh + 1) * HD), slice(2 * hf, 2 * hf + 2)
                            dve.tensor_copy(c[h, pp, bass.ds(1 + c_ * CH, CH)], ps[h, pp, 384 + hh * CH:384 + (hh + 1) * CH])\
                               .then_inc(S["o_taken"], 1)
                decay_before(dve, 0)
                for n in range(5):
                    scaled(dve, 0, 0, n)
                with dve.Fori(0, NCH // 2) as i:
                    chunk(2 * i, 0)
                    chunk(2 * i + 1, 1)

        SB = k.at(free_b, "rc_SB", [P, 2, NB, P])
        EX = k.at(free_kk, "rc_EX", [P, 2, NB, P])
        bm = k.sb(ctx, "rc_bm", [P, NB])
        G = NCH
        KR, ex = KR_[:, 0], ex_[:, 0]
        with nc.Block() as block:
            @block.sync
            def _(sp):
                sp.dma_start(bm[:, :], io["batchmask"]).then_inc(S["masks"], 16)
                sp.wait_ge(S["sb_zero"], 1)
                for p in range(4):
                    if p >= 2:
                        sp.wait_ge(s_out[p % 2], 32)
                    for j in range(2):
                        h = slice(j * HD, (j + 1) * HD)
                        sp.dma_start(SB[h, p % 2, :, h], io["s0"][:, 2 * p + j].rearrange("b k v -> k b v"))\
                          .then_inc(sb_in[p % 2], 16)

            @block.gpsimd
            def _(pool):
                pool.memset(SB[:, :, :, :], 0.0).then_inc(S["sb_zero"], 1)
                for p in range(4):
                    pool.wait_ge(S["ns_done"], p + 1)
                    for j in range(2):
                        h = slice(j * HD, (j + 1) * HD)
                        pool.dma_start(io["o_rwkv_s"][:, 2 * p + j].rearrange("b k v -> k b v"), SB[h, p % 2, :, h])\
                            .then_inc(s_out[p % 2], 16)
                for j in range(2):
                    pool.wait_ge(s_out[j], 64)

            @block.tensor
            def _(pe):
                pe_common(pe, G, 0)
                for p in range(4):
                    own = (2 * G + p // 2 + 1)
                    pe.wait_ge(S["mv_taken"], own)
                    pe.wait_ge(S["wt_taken"], own)
                    pe.wait_ge(sb_in[p % 2], 32 * (p // 2 + 1))
                    sa = B[p][:, 256:384]
                    sav = sa.rearrange("p (h t) -> p h t", h=2)
                    wt = WT[:, p, :].rearrange("p (h t) -> p h t", h=2)
                    r = KR[:, p, 1, :].rearrange("p (h t) -> p h t", h=2)
                    pe.matmul(sa, MV[:, p, :], W[:, p, TT_, :], start=True, stop=True)
                    for n in range(NB):
                        t = slice(n * TSEQ, (n + 1) * TSEQ)
                        mm = pe.matmul(sav[:, :, t], SB[:, p % 2, n, :], wt[:, :, t], start=False, stop=True,
                                       skip_group_check=True)
                    mm.then_inc(S["ut_made"], 1)
                    pe.wait_ge(S["ut_taken"], p + 1)
                    pe.transpose(B[p][:, P:2 * P], S1[:, p, :], k.mask("ident")).then_inc(S["sx_made"], 1)
                    pe.wait_ge(S["sx_taken"], p + 1)
                    o = B[p][:, 384:512]
                    ov = o.rearrange("p (h t) -> p h t", h=2)
                    pe.matmul(o, SA[:, p, :], A4[:, p, 1, :], start=True, stop=False)
                    pe.matmul(o, tm[:, p, 2, :], A4[:, p, 3, :], start=False, stop=True)
                    for n in range(NB):
                        t = slice(n * TSEQ, (n + 1) * TSEQ)
                        mm = pe.matmul(ov[:, :, t], SB[:, p % 2, n, :], r[:, :, t], start=False, stop=True,
                                       skip_group_check=True)
                    mm.then_inc(S["o_made"], 1)
                    pe.wait_ge(S["ex"], 2 * (p + 1))
                    if p >= 2:
                        pe.wait_ge(S["sum"], p - 1)
                    for n in range(2):
                        o = B[4 + 2 * (p % 2) + n]
                        bt = slice(4 * n, 4 * n + 4)
                        pe.matmul(o, tm[:, p, 0, :], EX[:, 0, bt, :].rearrange("p b v -> p (b v)"), start=True, stop=False)
                        mm = pe.matmul(o, tm[:, p, 1, :], EX[:, 1, bt, :].rearrange("p b v -> p (b v)"), start=False, stop=True)
                    mm.then_inc(S["ns_made"], 1)

            @block.scalar
            def _(act):
                act_common(act, G, 0, False)
                for p in range(4):
                    act.wait_ge(S["sx_made"], p + 1)
                    act.activation(SA[:, p, :], B[p][:, P:2 * P], ACT.Copy).then_inc(S["sx_taken"], 1)

            @block.vector
            def _(dve):
                dve.wait_ge(S["masks"], 32)
                dve_common(dve, G, 0, 1, False)
                for p in range(4):
                    dve.wait_ge(S["ut_made"], p + 1)
                    dve.tensor_scalar(S1[:, p, :], B[p][:, 256:384], -1.0, None, ALU.mult).then_inc(S["ut_taken"], 1)
                    dve.wait_ge(S["sx_taken"], p + 1)
                    if p >= 1:
                        dve.wait_ge(S["ns_made"], p)
                    for j, x in enumerate((SA[:, p, :], tm[:, p, 2, :])):
                        dve.tensor_tensor(EX[:, j], x.unsqueeze(1).broadcast_to([P, NB, P]),
                                          bm[:, :].unsqueeze(2).broadcast_to([P, NB, P]), ALU.mult).then_inc(S["ex"], 1)
                    dve.wait_ge(S["o_made"], 2 * NCH + p + 1)
                    for hh in range(2):
                        h = slice(hh * HD, (hh + 1) * HD)
                        dve.tensor_copy(c[h, p, 1 + TP:1 + T], B[p][h, 384 + hh * CH:384 + hh * CH + TS])
                    dve.wait_ge(S["ns_made"], p + 1)
                    sb = SB[:, p % 2]
                    new = ps[:, 4 + 2 * (p % 2):6 + 2 * (p % 2), :].rearrange("p a n -> p (a n)").rearrange("p (b v) -> p b v", b=NB)
                    dve.tensor_tensor(sb, sb, new, ALU.add).then_inc(S["sum"], 1)
                    dve.wait_ge(S["sum"], p + 1)
                    end = ex[:, 0, p, TSEQ - 1:TS:TSEQ]
                    dve.tensor_tensor(sb, sb, end.unsqueeze(2).broadcast_to([P, NB, P]), ALU.mult).then_inc(S["ns_done"], 1)


def rwkv_out_stage(k, y):
    nc, io, rw = k.nc, k.io, k.rw
    B = k.bank
    S = {n: k.sem(f"ro_{n}") for n in ("w", "sig", "gated", "mean", "c_done", "sq", "var", "root", "inv", "rk", "made",
                                       "own", "aff")}
    Y = lambda q, n=None: y[:, q, 1:1 + T] if n is None else y[:, q, 1 + n * C3:1 + (n + 1) * C3]
    G = 4
    with ExitStack() as ctx:
        g2 = k.sb(ctx, "ro_g2", [P, 512])
        sq = k.sb(ctx, "ro_sq", [P, 2, T])
        inv = k.sb(ctx, "ro_inv", [P, T])
        rk = k.sb(ctx, "ro_rk", [P, 2, T])
        t = k.sb(ctx, "ro_t", [P, 2, C3])
        with nc.Block() as block:
            @block.sync
            def _(sp):
                sp.dma_start(g2[:, :], io["rw_g2"]).then_inc(S["w"], 16)

            @block.tensor
            def _(pe):
                for q in range(G):
                    for n in range(3):
                        i = 3 * q + n
                        if i >= 4:
                            pe.wait_ge(S["c_done"], i - 3)
                        pe.matmul(B[i % 4][:, 0:C3], k.mask("headones"), Y(q, n), start=True, stop=True).then_inc(S["mean"], 1)
                for q in range(G):
                    pe.wait_ge(S["sq"], q + 1)
                    for n in range(3):
                        mm = pe.matmul(B[4 + n][32 * q:32 * q + 32, 0:C3], k.mask("pick", 32), third(sq[:, q % 2, :], n),
                                       start=True, stop=True)
                    mm.then_inc(S["var"], 1)
                pe.wait_ge(S["inv"], 3)
                pe.wait_ge(S["w"], 16)
                pe.wait_ge(S["gated"], 1)
                pe.wait_ge(S["c_done"], 3 * G)
                for q in range(G):
                    pe.wait_ge(S["rk"], q + 1)
                    for n in range(3):
                        i = 3 * q + n
                        j = 3 * (i % 2)
                        if i >= 2:
                            pe.wait_ge(S["own"], i - 1)
                        pe.matmul(B[j][:, 0:C3], k.masks[32 * q:32 * q + 32, MK["spread"]:MK["spread"] + P],
                                  third(inv[32 * q:32 * q + 32, :], n), start=True, stop=True)
                        pe.matmul(B[j + 1][:, 0:C3], k.mask("headones"), third(rk[:, q % 2, :], n), start=True, stop=True)
                        pe.matmul(B[j + 2][:, 0:C3], g2[:, q * P:(q + 1) * P], third(rw[:, 13, 0:T], n),
                                  start=True, stop=True).then_inc(S["made"], 1)

            @block.scalar
            def _(act):
                act.activation(rw[:, 13, 0:T], rw[:, 13, 0:T], ACT.Tanh, scale=0.5).then_inc(S["sig"], 1)
                for q in range(G):
                    act.wait_ge(S["c_done"], 3 * (q + 1))
                    if q >= 2:
                        act.wait_ge(S["var"], q - 1)
                    act.activation(sq[:, q % 2, :], Y(q), ACT.Square).then_inc(S["sq"], 1)
                act.wait_ge(S["var"], G)
                for n in range(3):
                    act.activation(third(inv, n), B[4 + n][:, 0:C3], ACT.Sqrt, bias=k.mask("lnx_eps", 1), scale=1.0 / HD)\
                       .then_inc(S["root"], 1)

            @block.vector
            def _(dve):
                dve.wait_ge(S["sig"], 1)
                dve.tensor_scalar(rw[:, 13, 0:T], rw[:, 13, 0:T], 0.5, 0.5, ALU.mult, ALU.add).then_inc(S["gated"], 1)

                def bonus(q):
                    if q >= 2:
                        dve.wait_ge(S["made"], 3 * (q - 1))
                    dve.scalar_tensor_tensor(rk[:, q % 2, :], rw[:, q, 0:T], k.vec("rw_r_k", q), rw[:, 4 + q, 0:T],
                                             ALU.mult, ALU.mult).then_inc(S["rk"], 1)
                for q in range(G):
                    for n in range(3):
                        i = 3 * q + n
                        dve.wait_ge(S["mean"], i + 1)
                        dve.scalar_tensor_tensor(Y(q, n), B[i % 4][:, 0:C3], -1.0 / HD, Y(q, n), ALU.mult, ALU.add)\
                           .then_inc(S["c_done"], 1)
                bonus(0)
                bonus(1)
                for n in range(3):
                    dve.wait_ge(S["root"], n + 1)
                    dve.reciprocal(third(inv, n), third(inv, n)).then_inc(S["inv"], 1)
                step = Chain(dve, S["aff"])
                for q in range(G):
                    if q >= 2:
                        bonus(q)
                    for n in range(3):
                        i = 3 * q + n
                        j = 3 * (i % 2)
                        dve.wait_ge(S["made"], i + 1)
                        u, v = t[:, 0, :], third(rw[:, 8 + q, 0:T], n)
                        step(dve.tensor_tensor(Y(q, n), Y(q, n), B[j][:, 0:C3], ALU.mult))
                        dve.tensor_tensor(u, v, B[j + 1][:, 0:C3], ALU.mult)
                        step(dve.tensor_scalar(Y(q, n), Y(q, n), k.vec("rw_lnx_g", q), k.vec("rw_lnx_b", q), ALU.mult, ALU.add))
                        step(dve.tensor_tensor(Y(q, n), Y(q, n), u, ALU.add))
                        dve.tensor_tensor(Y(q, n), Y(q, n), B[j + 2][:, 0:C3], ALU.mult).then_inc(S["own"], 1)


def residual(k):
    def ep(eng, m, n, ps):
        xs = k.x[:, bass.ds(m, 1), n * C3:(n + 1) * C3].rearrange("p a t -> p (a t)")
        return eng.tensor_tensor(xs, xs, ps, ALU.add)
    return ep


def memory_kv_stage(k, wide, kmT, vm):
    nc, io = k.nc, k.io
    S = {n: k.sem(f"mk_{n}") for n in ("in", "squared", "high", "low", "added", "sums", "root", "inv", "w_high", "w_low", "made",
                                       "taken", "v_taken", "out")}
    w_in = [k.sem(f"mk_w{j}") for j in range(2)]
    B = k.bank
    size = DK * NM
    mem, low = k.at(wide, "mk_mem", [P, DK, NM]), k.at(wide, "mk_low", [P, DK, NM], FR)
    high, sq = k.at(wide, "mk_high", [P, DK, NM], FR, words=size), k.at(wide, "mk_sq", [P, DK, NM], words=2 * size)
    with ExitStack() as ctx:
        slot = k.sb(ctx, "mk_slot", [P, 2, D])
        part = k.sb(ctx, "mk_part", [P, 2, 2, D], FR)
        acc, row = k.sb(ctx, "mk_acc", [P, NM])[:, :], k.sb(ctx, "mk_row", [P, NM])[:, :]
        col = k.sb(ctx, "mk_col", [P, 2])
        with nc.Block() as block:
            @block.sync
            def _(sp):
                sp.dma_start(mem[:, :, :], io["memT"].rearrange("(k p) m -> p k m", p=P)).then_inc(S["in"], 16)
                for j in range(2):
                    sp.dma_start(slot[:, j], io["w_mkv"][j]).then_inc(w_in[j], 16)
                with sp.Fori(1, DK) as i:
                    for j in range(2):
                        sp.wait_ge(S["w_low"], 2 * i + j - 1)
                        sp.dma_start(slot[:, j], io["w_mkv"][bass.ds(2 * i + j, 1)].rearrange("a p n -> p (a n)"))\
                          .then_inc(w_in[j], 16)
                sp.wait_ge(S["taken"], DK + 2)
                sp.dma_start(io["o_memk"].rearrange("(k p) m -> p k m", p=P), kmT[:, :, :]).then_inc(S["out"], 16)
                sp.wait_ge(S["v_taken"], 4)
                sp.dma_start(io["o_memv"].rearrange("(a p) d -> p a d", p=P), vm[:, :, :]).then_inc(S["out"], 16)
                sp.wait_ge(S["out"], 32)

            @block.tensor
            def _(pe):
                def keys(m, j):
                    pe.wait_ge(S["w_low"], m + 1)
                    pe.wait_ge(S["taken"], m + 1)
                    products(pe, B[j][:, 0:NM], lambda a, kk: part[:, j, a, kk * P:(kk + 1) * P],
                             lambda b, kk: (high, low)[b][:, kk, :], DK, S["made"])
                pe.wait_ge(S["low"], DK)
                keys(0, 0)
                pe.wait_ge(S["added"], 1)
                pe.matmul(B[2][:, 0:NM], k.mask("ones"), acc, start=True, stop=True)
                for mt in range(2):
                    mm = pe.matmul(B[3][:, mt * P:(mt + 1) * P], acc[:, mt * P:(mt + 1) * P], k.mask("ones"), start=True, stop=True)
                mm.then_inc(S["sums"], 1)
                keys(1, 1)
                with pe.Fori(1, DK // 2) as i:
                    keys(2 * i, 0)
                    keys(2 * i + 1, 1)
                for kk in range(DK):
                    pe.wait_ge(S["w_low"], DK + kk + 1)
                    for mt in range(2):
                        for n in range(2):
                            for x, (a, b) in enumerate(((0, 0), (0, 1), (1, 0))):
                                mm = pe.matmul(B[4 + 2 * mt + n], (high, low)[b][:, kk, mt * P:(mt + 1) * P],
                                               part[:, kk % 2, a, n * 512:(n + 1) * 512],
                                               start=(kk == 0 and x == 0), stop=(kk == DK - 1 and x == 2))
                    mm.then_inc(S["made"], 1)

            @block.scalar
            def _(act):
                act.wait_ge(S["in"], 16)
                act.activation(sq[:, :, :], mem[:, :, :], ACT.Square).then_inc(S["squared"], 1)
                for i in range(DK):
                    act.activation(high[:, i, :], mem[:, i, :], ACT.Copy, scale=k.vec("g_mem_kv", i)).then_inc(S["high"], 1)

                def rounded(i, s, j, free=True):
                    act.wait_ge(w_in[j], 16 * (i + 1))
                    if free:
                        act.wait_ge(S["made"], s - 1)
                    act.activation(part[:, j, 0], slot[:, j], ACT.Copy).then_inc(S["w_high"], 1)
                rounded(0, 0, 0, False)
                rounded(0, 1, 1, False)
                act.wait_ge(S["sums"], 1)
                act.activation(row, B[2][:, 0:NM], ACT.Sqrt, bias=k.mask("eps", 1), scale=1.0 / D).then_inc(S["root"], 1)
                act.activation(col[:, :], B[3][:, 0:NM:P], ACT.Sqrt, bias=k.mask("eps", 1), scale=1.0 / D).then_inc(S["root"], 1)
                with act.Fori(1, DK) as i:
                    rounded(i, 2 * i, 0)
                    rounded(i, 2 * i + 1, 1)
                act.wait_ge(S["made"], 2 * DK)
                act.wait_ge(S["inv"], 2)
                for mt in range(2):
                    for n in range(2):
                        act.activation(vm[:, mt, n * 512:(n + 1) * 512], B[4 + 2 * mt + n], ACT.Copy, scale=col[:, mt:mt + 1])\
                           .then_inc(S["v_taken"], 1)

            @block.vector
            def _(dve):
                dve.sem_inc(S["taken"], 2)
                dve.wait_ge(S["squared"], 1)
                for i in range(DK):
                    dve.wait_ge(S["high"], i + 1)
                    dve.scalar_tensor_tensor(low[:, i, :], mem[:, i, :], k.vec("g_mem_kv", i), high[:, i, :].bitcast(F32),
                                             ALU.mult, ALU.subtract).then_inc(S["low"], 1)
                dve.tensor_reduce(acc, sq[:, :, :].rearrange("p k m -> p m k"), AX, ALU.add).then_inc(S["added"], 1)

                def rest(s, j):
                    dve.wait_ge(S["w_high"], s + 1)
                    dve.tensor_tensor(part[:, j, 1], slot[:, j], part[:, j, 0].bitcast(F32), ALU.subtract).then_inc(S["w_low"], 1)
                rest(0, 0)
                rest(1, 1)
                dve.wait_ge(S["root"], 2)
                dve.reciprocal(row, row).then_inc(S["inv"], 1)
                dve.reciprocal(col[:, :], col[:, :]).then_inc(S["inv"], 1)
                dve.wait_ge(S["inv"], 2)
                with dve.Fori(0, DK // 2) as i:
                    for j in range(2):
                        m = 2 * i + j
                        rest(m + 2, j)
                        dve.wait_ge(S["made"], m + 1)
                        dve.tensor_tensor(kmT[:, bass.ds(m, 1), :], B[j][:, 0:NM].unsqueeze(1), row.unsqueeze(1), ALU.mult)\
                           .then_inc(S["taken"], 1)
                with dve.Fori(DK // 2 + 1, DK) as i:
                    rest(2 * i, 0)
                    rest(2 * i + 1, 1)


def memory_attention_stage(k, q, kmT, vm, H, L, qt, pr):
    nc, io = k.nc, k.io
    B = k.bank
    N = TILES
    assert N == NB
    names = ("s_made", "maxed", "m_ready", "e_done", "r_done", "p_scaled", "t_made", "t_taken", "o_made", "o_high", "o_taken")
    S = {n: k.sem(f"ma_{n}") for n in names + ("q_there",)}
    Z = {n: k.sem(f"mz_{n}") for n in names}
    kv_in = [k.sem(f"mz_kv{j}") for j in range(2)]
    HALF = MH // 2
    with ExitStack() as ctx:
        pT = k.acc[:, 0:MH * NM].rearrange("p (h a n) -> p h a n", h=MH, a=2)
        st = k.sb(ctx, "ma_st", [P, 2, 4, MH])
        ks = k.sb(ctx, "mz_k", [P, 2, DK, NM])
        vs = k.sb(ctx, "mz_v", [P, 2, 2, D])
        zpr = k.sb(ctx, "mz_p", [P, NM])
        zpT = k.sb(ctx, "mz_pT", [P, 2, P])
        zst = k.sb(ctx, "mz_st", [P, 4])
        z_s, z_t, z_o = B[5][:, 0:NM], B[5][:, NM:2 * NM], B[5][:, 0:DK * TSEQ]

        def steps(eng, step):
            with eng.Fori(0, N // 2 - 2) as it:
                for j in range(2):
                    step(2 * it + j, j, True, True, True)
            for i in range(N - 4, N):
                step(i, i % 2, i + 1 < N, i + 2 < N, i + 3 < N)
        with nc.Block() as block:
            @block.sync
            def _(sp):
                def load(b, j):
                    bb = bass.ds(b, 1)
                    sp.dma_start(ks[:, j], io["memk"][bb].rearrange("a (k p) m -> p (a k) m", p=P)).then_inc(kv_in[j], 16)
                    sp.dma_start(vs[:, j], io["memv"][bb].rearrange("a (k p) d -> p (a k) d", p=P)).then_inc(kv_in[j], 16)
                load(0, 0)
                load(1, 1)
                with sp.Fori(1, NB // 2) as it:
                    for j in range(2):
                        sp.wait_ge(Z["o_made"], 2 * it + j - 1)
                        load(2 * it + j, j)

            @block.tensor
            def _(pe):
                def scores(i, j):
                    pe.wait_ge(S["q_there"], i + 1)
                    for h in range(MH):
                        for dk in range(2):
                            mm = pe.matmul(B[2 * j + h // 2][:, h % 2 * NM:(h % 2 + 1) * NM], qt[:, j, 2 * h + dk, :],
                                           kmT[:, 2 * h + dk, :], start=(dk == 0), stop=(dk == 1))
                    mm.then_inc(S["s_made"], 1)

                def transposes(i, j, a):
                    pe.wait_ge(S["p_scaled"], i + 1)
                    pe.wait_ge(S["t_taken"], 2 * i + a + 1)
                    for h in range(HALF * a, HALF * (a + 1)):
                        for mt in range(2):
                            mm = pe.transpose(B[4][:, (h % 2 * 2 + mt) * P:(h % 2 * 2 + mt + 1) * P],
                                              pr[:, j, h, mt * P:(mt + 1) * P], k.mask("ident"))
                    mm.then_inc(S["t_made"], 1)

                def values(i, a):
                    pe.wait_ge(S["t_taken"], 2 * i + a + 2)
                    pe.wait_ge(S["o_taken"], 2 * i + a + 1)
                    for c in range(4 * a, 4 * a + 4):
                        for mt in range(2):
                            mm = pe.matmul(B[6 + a][:, c % 4 * P:(c % 4 + 1) * P], vm[:, mt, c * P:(c + 1) * P],
                                           pT[:, c // 2, mt, :], start=(mt == 0), stop=(mt == 1))
                    mm.then_inc(S["o_made"], 1)

                def step(i, j, next1, next2, next3):
                    pe.wait_ge(kv_in[j], 16 * (i - j + 2))
                    pe.wait_ge(Z["o_taken"], i + 1)
                    for h in range(MH):
                        for dk in range(2):
                            mm = pe.matmul(z_s[32 * h:32 * h + 32, :], q[:, 2 * h + dk, TP:T], ks[:, j, 2 * h + dk, :],
                                           start=(dk == 0), stop=(dk == 1))
                    mm.then_inc(Z["s_made"], 1)
                    transposes(i, j, 0)
                    if next2:
                        scores(i + 2, j)
                    pe.wait_ge(Z["p_scaled"], i + 1)
                    for mt in range(2):
                        mm = pe.transpose(z_t[:, mt * P:(mt + 1) * P], zpr[:, mt * P:(mt + 1) * P], k.mask("ident"))
                    mm.then_inc(Z["t_made"], 1)
                    transposes(i, j, 1)
                    values(i, 0)
                    pe.wait_ge(Z["t_taken"], i + 1)
                    for c in range(DK):
                        for mt in range(2):
                            mm = pe.matmul(z_o[:, c * TSEQ:(c + 1) * TSEQ], vs[:, j, mt, c * P:(c + 1) * P],
                                           zpT[:, mt, bass.ds(c // 2 * TS + i * TSEQ, TSEQ)], start=(mt == 0), stop=(mt == 1))
                    mm.then_inc(Z["o_made"], 1)
                    values(i, 1)
                scores(0, 0)
                scores(1, 1)
                steps(pe, step)

            @block.scalar
            def _(act):
                act.sem_inc(S["t_taken"], 1)

                def queries(i, j):
                    act.wait_ge(S["s_made"], i - 1)
                    act.activation(qt[:, j, :, :], q[:, :, bass.ds(i * P, P)], ACT.Copy).then_inc(S["q_there"], 1)

                def exponentials(i, j):
                    act.wait_ge(S["m_ready"], i + 1)
                    for h in range(MH):
                        act.activation(pr[:, j, h, :], B[2 * j + h // 2][:, h % 2 * NM:(h % 2 + 1) * NM], ACT.Exp,
                                       bias=st[:, j, 1, h:h + 1], scale=MSCALE, accum_out=st[:, j, 2, h:h + 1])\
                           .then_inc(S["e_done"], 1)

                def turned(i, a):
                    act.wait_ge(S["t_made"], 2 * i + a + 1)
                    act.activation(pT[:, HALF * a:HALF * (a + 1), :, :].rearrange("p h a n -> p (h a n)"), B[4], ACT.Copy)\
                       .then_inc(S["t_taken"], 1)

                def step(i, j, next1, next2, next3):
                    turned(i, 0)
                    act.wait_ge(Z["m_ready"], i + 1)
                    act.activation(zpr[:, :], z_s, ACT.Exp, bias=zst[:, 1:2], scale=MSCALE, accum_out=zst[:, 2:3])\
                       .then_inc(Z["e_done"], 1)
                    if next1:
                        exponentials(i + 1, 1 - j)
                    act.wait_ge(Z["t_made"], i + 1)
                    act.activation(zpT[:, :, :].rearrange("p a n -> p (a n)"), z_t, ACT.Copy).then_inc(Z["t_taken"], 1)
                    turned(i, 1)
                    if next3:
                        queries(i + 3, 1 - j)
                for i in range(2):
                    act.activation(qt[:, i, :, :], q[:, :, i * P:(i + 1) * P], ACT.Copy).then_inc(S["q_there"], 1)
                exponentials(0, 0)
                queries(2, 0)
                steps(act, step)

            @block.vector
            def _(dve):
                dve.sem_inc(S["o_taken"], 2)
                dve.sem_inc(Z["o_taken"], 1)

                def maxima(i, j):
                    dve.wait_ge(S["s_made"], i + 1)
                    dve.reduce_max(st[:, j, 0, :], k.psum[:, 1024 * j:1024 * (j + 1)].rearrange("p (h n) -> p h n", h=MH), AX)\
                       .then_inc(S["maxed"], 1)
                    dve.wait_ge(S["maxed"], i + 1)
                    dve.tensor_scalar(st[:, j, 1, :], st[:, j, 0, :], -MSCALE, None, ALU.mult).then_inc(S["m_ready"], 1)

                def divide(i, j):
                    dve.wait_ge(S["e_done"], MH * (i + 1))
                    dve.reciprocal(st[:, j, 3, :], st[:, j, 2, :]).then_inc(S["r_done"], 1)
                    dve.wait_ge(S["r_done"], i + 1)
                    dve.tensor_tensor(pr[:, j, :, :], pr[:, j, :, :], st[:, j, 3, :].unsqueeze(2).broadcast_to([P, MH, NM]), ALU.mult)\
                       .then_inc(S["p_scaled"], 1)

                def put(tiles, cols, ps, S, n):
                    dve.wait_ge(S["o_made"], n + 1)
                    dve.tensor_copy(H[:, tiles, cols], ps).then_inc(S["o_high"], 1)
                    dve.wait_ge(S["o_high"], n + 1)
                    dve.tensor_tensor(L[:, tiles, cols], ps, H[:, tiles, cols].bitcast(F32), ALU.subtract).then_inc(S["o_taken"], 1)

                def step(i, j, next1, next2, next3):
                    dve.wait_ge(Z["s_made"], i + 1)
                    dve.reduce_max(zst[:, 0:1], z_s, AX).then_inc(Z["maxed"], 1)
                    dve.wait_ge(Z["maxed"], i + 1)
                    dve.tensor_scalar(zst[:, 1:2], zst[:, 0:1], -MSCALE, None, ALU.mult).then_inc(Z["m_ready"], 1)
                    if next1:
                        maxima(i + 1, 1 - j)
                    dve.wait_ge(Z["e_done"], i + 1)
                    dve.reciprocal(zst[:, 3:4], zst[:, 2:3]).then_inc(Z["r_done"], 1)
                    dve.wait_ge(Z["r_done"], i + 1)
                    dve.tensor_scalar(zpr[:, :], zpr[:, :], zst[:, 3:4], None, ALU.mult).then_inc(Z["p_scaled"], 1)
                    if next1:
                        divide(i + 1, 1 - j)
                    cols = bass.ds(i * P, P)
                    put(slice(0, 4), cols, B[6].rearrange("p (c n) -> p c n", c=4), S, 2 * i)
                    put(slice(0, DK), bass.ds(TP + i * TSEQ, TSEQ), z_o.rearrange("p (c n) -> p c n", c=DK), Z, i)
                    put(slice(4, DK), cols, B[7].rearrange("p (c n) -> p c n", c=4), S, 2 * i + 1)
                maxima(0, 0)
                divide(0, 0)
                steps(dve, step)


def ffn_stage(k, H, L, hid, hid_full):
    nc, io = k.nc, k.io
    B = k.bank
    UP, US = 2 + TP, 2 + TSEQ
    U = UP + NB * US
    CV = U - 2
    ROUNDS = FK // 2
    S = {n: k.sem(f"ff_{n}") for n in (
        "past_in", "zero", "w_high", "w_low", "up_made", "up_taken", "past", "u_free", "c_first", "c_mid", "c_done", "cap", "tanh",
        "g_done", "hid_full", "hid_high", "hid_low", "down_made", "down_taken",
        "squared", "added", "out")}
    rows = RowScale(k, "nffn")
    w_in = [k.sem(f"ff_w{j}") for j in range(2)]
    DG = 3 * DK
    with ExitStack() as ctx:
        slot = k.sb(ctx, "ff_slot", [P, 2, D])
        up = k.sb(ctx, "ff_up", [P, 2, 2, D], FR)
        down = k.sb(ctx, "ff_down", [P, 2, 2, D], FR)
        u = k.sb(ctx, "ff_u", [P, 2, U])
        cv_ = k.sb(ctx, "ff_c", [P, 2, U])
        th_ = k.sb(ctx, "ff_t", [P, U])
        cv, th = cv_[:, :, 0:CV], th_[:, 0:CV]
        past = k.sb(ctx, "ff_past", [P, F2K, NB, 2])
        cap = k.sb(ctx, "ff_cap", [P, F2K, 1 + NB, 2])
        seg = lambda ap, lo: ap[:, UP:U].rearrange("p (b n) -> p b n", b=NB)[:, :, lo:lo + TSEQ]
        with nc.Block() as block:
            @block.sync
            def _(sp):
                row = lambda w, m: w[bass.ds(m, 1)].rearrange("a p n -> p (a n)")
                for e in range(4):
                    if e >= 2:
                        sp.wait_ge(S["w_low"], e - 1)
                    sp.dma_start(slot[:, e % 2], io["w_up"][e]).then_inc(w_in[e % 2], 16)
                    if e == 1:
                        sp.dma_start(past[:, :, :, :], io["conv0"]).then_inc(S["past_in"], 16)

                def next_tile(r, e, src):
                    sp.wait_ge(S["w_low"], 6 * r + e - 3)
                    sp.dma_start(slot[:, e % 2], src).then_inc(w_in[e % 2], 16)
                with sp.Fori(1, ROUNDS) as r:
                    for e, src in ((0, row(io["w_up"], 4 * r)), (1, row(io["w_up"], 4 * r + 1)),
                                   (2, row(io["w_down"], 2 * r - 2)), (3, row(io["w_down"], 2 * r - 1)),
                                   (4, row(io["w_up"], 4 * r + 2)), (5, row(io["w_up"], 4 * r + 3))):
                        next_tile(r, e, src)
                for e in range(2):
                    next_tile(ROUNDS, e, io["w_down"][FK - 2 + e])
                sp.wait_ge(S["cap"], F2K + 1)
                sp.dma_start(io["o_conv"], cap[:, :, :, :].rearrange("p m s j -> p m (s j)")).then_inc(S["out"], 16)
                sp.wait_ge(S["out"], 16)

            @block.gpsimd
            def _(pool):
                def divide(dst, j, count, n_tile):
                    pool.wait_ge(w_in[j], 16 * count)
                    pool.tensor_tensor(dst[:, 0], slot[:, j], k.mask("ones", 1).broadcast_to([P, D]), ALU.mult).then_inc(S["w_high"], 1)
                    pool.wait_ge(S["w_high"], n_tile + 1)
                    pool.tensor_tensor(dst[:, 1], slot[:, j], dst[:, 0].bitcast(F32), ALU.subtract).then_inc(S["w_low"], 1)
                for e in range(4):
                    if e >= 2:
                        pool.wait_ge(S["up_made"], 3 * (e - 1))
                    divide(up[:, e % 2], e % 2, e // 2 + 1, e)

                def up_tile(r, e, t):
                    pool.wait_ge(S["up_made"], 3 * (4 * r + t - 1))
                    divide(up[:, e % 2], e % 2, 3 * r + e // 2, 6 * r - 2 + e)

                def down_tile(r, e, j):
                    pool.wait_ge(S["down_taken"], DG * (r - 1) + 4)
                    divide(down[:, j], e % 2, 3 * r + e // 2, 6 * r - 2 + e)
                with pool.Fori(1, ROUNDS) as r:
                    up_tile(r, 0, 0)
                    up_tile(r, 1, 1)
                    down_tile(r, 2, 0)
                    down_tile(r, 3, 1)
                    up_tile(r, 4, 2)
                    up_tile(r, 5, 3)
                down_tile(ROUNDS, 0, 0)
                down_tile(ROUNDS, 1, 1)

            @block.tensor
            def _(pe):
                rows.pe(pe)

                def round_up(r, q, w_count):
                    for j in range(2):
                        pe.wait_ge(S["w_low"], w_count + j)
                        t = 4 * r + 2 * q + j
                        for n in range(3):
                            pe.wait_ge(S["up_taken"], 3 * t + n + 1)
                            products(pe, B[(3 * (2 * q + j) + n) % 4][:, 0:C3], lambda a, kk: up[:, j, a, kk * P:(kk + 1) * P],
                                     lambda b, kk: third((H, L)[b][:, kk, :], n), DK, S["up_made"])

                def round_down(r, buf, w_count):
                    pe.wait_ge(S["w_low"], w_count)
                    pe.wait_ge(S["hid_low"], 2 * (r + 1))
                    for m in range(DK):
                        for n in range(3):
                            g = 3 * m + n
                            pe.wait_ge(S["down_taken"], DG * r + g + 1)
                            products(pe, B[4 + g % 4][:, 0:C3], lambda a, kk: down[:, kk, a, m * P:(m + 1) * P],
                                     lambda b, kk: third(hid[:, buf, b, kk, :], n), 2, S["down_made"])
                round_up(0, 0, 1)
                pe.wait_ge(rows.S["root"], 3)
                round_up(0, 1, 3)
                with pe.Fori(0, (ROUNDS - 1) // 2) as i:
                    for a in range(2):
                        r = 2 * i + a + 1
                        round_up(r, 0, 6 * r - 1)
                        round_down(r - 1, a, 6 * r + 2)
                        round_up(r, 1, 6 * r + 3)
                round_down(ROUNDS - 1, (ROUNDS - 1) % 2, 6 * ROUNDS)

            @block.scalar
            def _(act):
                rows.act(act)
                act.wait_ge(S["past_in"], 16)
                act.wait_ge(S["zero"], 1)

                def hidden(i):
                    for j in range(2):
                        t = 2 * i + j
                        act.wait_ge(S["u_free"], t + 1)
                        act.activation(u[:, j, UP:U].rearrange("p (b n) -> p b n", b=NB)[:, :, 0:2],
                                       past[:, bass.ds(i + FK * j, 1), :, :].rearrange("p a b n -> p (a b) n"), ACT.Copy)\
                           .then_inc(S["past"], 1)
                        act.wait_ge(S["past"], t + 1)
                        act.wait_ge(S["up_taken"], 3 * t + 7)
                        act.wait_ge(S["hid_full"], 2 * (i + 1))
                        b0 = VEC["conv_b"] + i + FK * j
                        w2 = VEC["conv_w"] + 2 * F2K + i + FK * j
                        act.activation(cv[:, j, :], u[:, j, 2:U], ACT.Identity, bias=k.vecs[:, bass.ds(b0, 1)],
                                       scale=k.vecs[:, bass.ds(w2, 1)]).then_inc(S["c_first"], 1)
                    act.wait_ge(S["c_done"], 2 * i + 1)
                    act.activation(th[:, :], cv[:, 0, :], ACT.Tanh, scale=0.5).then_inc(S["tanh"], 1)
                with act.Fori(0, ROUNDS) as r:
                    hidden(2 * r)
                    hidden(2 * r + 1)
                for m in range(DK):
                    act.wait_ge(S["down_taken"], DG * (ROUNDS - 1) + 3 * (m + 1) + 4)
                    if m >= 2:
                        act.wait_ge(S["added"], m - 1)
                    act.activation(cv_[:, m % 2, 0:T], k.x[:, m, :], ACT.Square).then_inc(S["squared"], 1)

            @block.vector
            def _(dve):
                dve.sem_inc(S["up_taken"], 4)
                dve.sem_inc(S["u_free"], 2)
                dve.sem_inc(S["cap"], 1)
                dve.sem_inc(S["hid_full"], 2)
                dve.sem_inc(S["down_taken"], 4)
                dve.memset(u[:, :, 0:2], 0.0).then_inc(S["zero"], 1)
                rows.dve(dve)

                def rows_of(i, q, j):
                    t, w = 2 * i + j, TP - 2 * C3
                    for n in range(3):
                        ps, f = B[(3 * (2 * q + j) + n) % 4], third(k.acc, n)
                        dve.wait_ge(S["up_made"], 3 * t + n + 1)
                        if n < 2:
                            last = dve.tensor_tensor(u[:, j, 2 + n * C3:2 + (n + 1) * C3], ps[:, 0:C3], f, ALU.mult)
                        else:
                            dve.tensor_tensor(u[:, j, 2 + 2 * C3:UP], ps[:, 0:w], f[:, 0:w], ALU.mult)
                            by_batch = lambda ap: ap[:, w:C3].rearrange("p (b n) -> p b n", b=NB)
                            last = dve.tensor_tensor(seg(u[:, j, :], 2), by_batch(ps), by_batch(f), ALU.mult)
                        last.then_inc(S["up_taken"], 1)

                def convolve(i, j):
                    t = 2 * i + j
                    dve.wait_ge(S["c_first"], t + 1)
                    dst = cap[:, bass.ds(i + FK * j, 1), :, :].rearrange("p a s j -> p (a s) j")
                    dve.tensor_copy(dst[:, 0:1, :], u[:, j, UP - 2:UP].unsqueeze(1))
                    dve.tensor_copy(dst[:, 1:, :], u[:, j, UP:U].rearrange("p (b n) -> p b n", b=NB)[:, :, US - 2:US])\
                       .then_inc(S["cap"], 1)
                    tap = lambda n: k.vecs[:, bass.ds(VEC["conv_w"] + n * F2K + i + FK * j, 1)]
                    dve.scalar_tensor_tensor(cv[:, j, :], u[:, j, 1:U - 1], tap(1), cv[:, j, :], ALU.mult, ALU.add)\
                       .then_inc(S["c_mid"], 1)
                    dve.wait_ge(S["c_mid"], t + 1)
                    dve.scalar_tensor_tensor(cv[:, j, :], u[:, j, 0:U - 2], tap(0), cv[:, j, :], ALU.mult, ALU.add)\
                       .then_inc(S["c_done"], 1)
                    dve.wait_ge(S["c_done"], t + 1)
                    dve.wait_ge(S["cap"], t + 2)
                    dve.sem_inc(S["u_free"], 1)

                def multiply(i, q, buf):
                    dve.wait_ge(S["tanh"], i + 1)
                    dve.scalar_tensor_tensor(th[:, :], th[:, :], 1.0, cv[:, 0, :], ALU.add, ALU.mult).then_inc(S["g_done"], 1)
                    dve.wait_ge(S["g_done"], i + 1)
                    high, low, full = hid[:, buf, 0, q, :], hid[:, buf, 1, q, :], hid_full[:, buf, 1, q, :]
                    dve.scalar_tensor_tensor(full[:, 0:TP], th[:, 0:TP], 0.5, cv[:, 1, 0:TP], ALU.mult, ALU.mult)\
                       .then_inc(S["hid_full"], 1)
                    dve.scalar_tensor_tensor(full[:, TP:T].rearrange("p (b n) -> p b n", b=NB), seg(th_[:, :], 0), 0.5,
                                             seg(cv_[:, 1, :], 0), ALU.mult, ALU.mult).then_inc(S["hid_full"], 1)
                    dve.wait_ge(S["hid_full"], 2 * (i + 2))
                    dve.tensor_copy(high, full).then_inc(S["hid_high"], 1)
                    dve.wait_ge(S["hid_high"], i + 1)
                    dve.tensor_tensor(low, full, high.bitcast(F32), ALU.subtract).then_inc(S["hid_low"], 1)

                def add_down(r, last=False):
                    for m in range(DK):
                        for n in range(3):
                            g = 3 * m + n
                            dve.wait_ge(S["down_made"], DG * r + g + 1)
                            xs = third(k.x[:, m, :], n)
                            dve.tensor_tensor(xs, xs, B[4 + g % 4][:, 0:C3], ALU.add).then_inc(S["down_taken"], 1)
                        if last and m >= 1:
                            add_squares(m - 1)

                def add_squares(m):
                    dve.wait_ge(S["squared"], m + 1)
                    if m:
                        dve.wait_ge(S["added"], m)
                        dve.tensor_tensor(k.acc, k.acc, cv_[:, m % 2, 0:T], ALU.add).then_inc(S["added"], 1)
                    else:
                        dve.tensor_copy(k.acc, cv_[:, 0, 0:T]).then_inc(S["added"], 1)

                def hidden_pair(r, buf, add):
                    rows_of(2 * r, 0, 0)
                    convolve(2 * r, 0)
                    rows_of(2 * r, 0, 1)
                    if add:
                        add_down(r - 1)
                    convolve(2 * r, 1)
                    multiply(2 * r, 0, buf)
                    rows_of(2 * r + 1, 1, 0)
                    convolve(2 * r + 1, 0)
                    rows_of(2 * r + 1, 1, 1)
                    convolve(2 * r + 1, 1)
                    multiply(2 * r + 1, 1, buf)
                hidden_pair(0, 0, False)
                with dve.Fori(0, (ROUNDS - 1) // 2) as i:
                    for a in range(2):
                        hidden_pair(2 * i + a + 1, (a + 1) % 2, True)
                add_down(ROUNDS - 1, True)
                add_squares(DK - 1)


def final_stage(k, y):
    s, s_full = k.sem("y_out"), k.sem("y_full")
    rows = RowScale(k, "nfin")
    with k.nc.Block() as block:
        @block.sync
        def _(sp):
            for n in range(3):
                sp.wait_ge(s_full, DK * (n + 1))
                sp.dma_start(third(k.io["o_y"], n).rearrange("(k p) t -> p k t", p=P), y[:, :, n * C3:(n + 1) * C3]).then_inc(s, 16)
            sp.wait_ge(s, 48)
        block.scalar(rows.act)
        block.tensor(rows.pe)

        @block.vector
        def _(dve):
            rows.dve(dve)
            for n in range(3):
                for i in range(DK):
                    dve.scalar_tensor_tensor(third(y[:, i, :], n), third(k.x[:, i, :], n), k.vec("g_final", i), third(k.acc, n),
                                             ALU.mult, ALU.mult).then_inc(s_full, 1)


def program(nc, io):
    with ExitStack() as ctx:
        k = K(nc, ctx, io)
        k.masks = k.sb(ctx, "masks", [P, NMK])
        k.vecs = k.sb(ctx, "vecs", [P, NVEC])
        k.acc = k.sb(ctx, "acc", [P, T])[:, :]
        start = lambda: (nc.sbuf_base + 31) // 32 * 32
        wide = start()
        k.sb(ctx, "wide_area", [P, 2 * DK * T])
        mix = start()
        k.sb(ctx, "mix_area", [P, Y_WORDS + 4 * T])
        k.rw = k.at(wide, "rw", [P, RWK, TR])
        H, L = k.at(wide, "high", [P, DK, T], FR), k.at(wide, "low", [P, DK, T], FR, words=DK * T)
        k.y, k.mla = k.at(mix, "y", [P, 4, 1 + TR]), k.at(mix, "mla", [P, 4, T], words=Y_WORDS)
        load_stage(k)
        with ExitStack() as mctx:
            cqkv = start()
            k.cqkv = k.sb(mctx, "cqkv", [P, QK + KK, T])
            k.krope = k.sb(mctx, "krope", [P, T])
            qabs = k.sb(mctx, "qabs", [P, KK, NB, NH, TSEQ])
            qrope = k.sb(mctx, "qrope", [ROPE, NB, NH, TSEQ])
            with ExitStack() as tctx:
                k.rot = k.sb(tctx, "rot", [P, 2, T])
                with ExitStack() as hctx:
                    h_high = k.sb(hctx, "h_high", [P, DK, T], FR)
                    proj_stage(k, h_high, k.at(mix, "h_low", [P, DK, T], FR), k.at(mix, "h_full", [P, DK, T]))
                mla_prompt_stage(k, k.at(cqkv, "cq_low", [P, QK, T], FR), qabs, qrope)
            mla_sample_stage(k, mix, cqkv, qabs, qrope)
        k.recycle()
        with ExitStack() as rctx:
            at_a = start()
            a = k.sb(rctx, "rw_a", [P, 4, TR])
            at_kk = start()
            kk = k.sb(rctx, "rw_kk", [P, 4, TR])
            keep = k.sb(rctx, "rw_keep", [P, TR])
            rwkv_prep_stage(k, k.y, a, kk, keep)
            rwkv_chunk_stage(k, k.y, a, kk, keep, at_a, at_kk)
        k.recycle()
        rwkv_out_stage(k, k.y)
        k.x = k.sb(ctx, "x", [P, DK, T])
        s_x = k.sem("x1")
        with ExitStack() as actx:
            spare = start()
            k.sb(actx, "spare_area", [P, DK * T])
            m_high, m_low = k.at(mix, "m_high", [P, DK, T], FR), k.at(spare, "m_low", [P, DK, T], FR)
            with ExitStack() as octx:
                sq = k.sb(octx, "wo_tile", [P, T])
                parts = TwoParts(k, "wo_in", [(k.y[:, i, 1:1 + T], None) for i in range(4)]
                                 + [(k.mla[:, i, :], k.vec("g_mla_out", i)) for i in range(4)], H, L)
                linear_stage(k, "wo", io["w_o"], DK, [(DK, residual(k))], H, L, prepare=parts, drain_wait=(s_x, 16),
                             nxt=NextInput(k, "to_mq", "g_mem_q", m_high, m_low, sq[:, :]),
                             then=[(k.x[:, :, :], io["x"].rearrange("(k p) t -> p k t", p=P), s_x)])
            k.recycle()
            place = lambda name, shape, words: k.at(wide, name, shape, words=DK * T + words)
            kmT, vm = place("kmT", [P, DK, NM], 0), place("vm", [P, 2, D], DK * NM)
            memory_kv_stage(k, wide, kmT, vm)
            q = k.at(wide, "q", [P, DK, T])
            linear_stage(k, "mq", io["w_mq"], DK, [(DK, scaled(k, q))], m_high, m_low, rows=RowScale(k, "nmq"))
            memory_attention_stage(k, q, kmT, vm, m_high, m_low, place("ma_q", [P, 2, DK, P], 2 * DK * NM),
                                   place("ma_p", [P, 2, MH, NM], 2 * DK * NM + 2 * D))
            with ExitStack() as octx:
                sq = k.sb(octx, "nffn_tile", [P, T])
                linear_stage(k, "mo", io["w_mo"], DK, [(DK, residual(k))], m_high, m_low,
                             nxt=NextInput(k, "to_ffn", "g_ffn", H, L, sq[:, :]))
        k.recycle()
        hid = [P, 2, 2, 2, T]
        ffn_stage(k, H, L, k.at(mix, "hid", hid, FR), k.at(mix, "hid_full", hid))
        final_stage(k, k.at(wide, "result", [P, DK, T]))


OUTS = {
    "o_y": (D, T), "o_lat": (KVL, T), "o_krope": (ROPE, T),
    "o_memk": (D, NM), "o_memv": (NM, D),
    "o_rwkv_p": (NH, HD, HD), "o_rwkv_s": (NB, NH, HD, HD),
    "o_shift": (P, RWK, 1 + NB), "o_conv": (P, F2K, 2 * (1 + NB)),
}


def build(nc, arrays):
    io = {}
    for name, a in arrays.items():
        io[name] = nc.dram_tensor(f"in_{name}", a.shape, mybir.dt.from_np(a.dtype), kind="ExternalInput").ap()
    for name, shape in OUTS.items():
        io[name] = nc.dram_tensor(name, shape, F32, kind="ExternalOutput").ap()
    program(nc, io)


def kernel(**inputs):
    import numpy as _np
    import concourse.bacc as _bacc
    from concourse.bass_utils import run_bass_kernel_spmd as _run

    x = {n: _np.asarray(a) for n, a in inputs.items()}
    tile = lambda a: _np.ascontiguousarray(a)
    m, rw, rot, keep, batch = tables()
    arrays = {"masks": m, "rwmasks": rw, "rot": rot, "keep": keep, "batchmask": batch}
    arrays["vecs"] = tile(_np.concatenate([x[n].reshape(-1, P) for n in VEC]).T)
    arrays["x"] = tile(_np.concatenate([x["x_prompt"][0], x["x_sample"].reshape(TS, D)]).T)
    arrays["memT"] = tile(x["mem_prompt"][0].T)
    arrays["lat"] = x["cache_mla_latent"][0]
    arrays["kr"] = x["cache_mla_krope"][0]
    arrays["pages"] = x["page_table"].reshape(1, -1)
    arrays["memk"] = tile(x["cache_mem_k"][0].reshape(NB, NM, D).transpose(0, 2, 1))
    arrays["memv"] = x["cache_mem_v"][0].reshape(NB, NM, D)
    arrays["s0"] = tile(x["state_rwkv"][0].transpose(0, 1, 3, 2))
    arrays["shift0"] = tile(x["state_rwkv_shift"][0].reshape(NB, RWK, P).transpose(2, 1, 0))
    arrays["conv0"] = tile(x["state_ffn_conv"][0].reshape(NB, 2, F2K, P).transpose(3, 2, 0, 1))
    for n in ("rw_w2", "rw_a2", "rw_g2"):
        arrays[n] = x[n][0]
    by_tile = lambda w: tile(w.reshape(DK, P, -1, P).transpose(2, 1, 0, 3)).reshape(-1, P, D)
    for n in ("w_o", "w_mq", "w_mo"):
        arrays[n] = by_tile(x[n][0])
    arrays["w_mkv"] = _np.concatenate([by_tile(x["w_mk"][0]), x["w_mv"][0].reshape(DK, P, D)])
    w = x["w_in"][0]
    key, half = w[:, QL + KVL:MLA_PROJ], ROPE // 2
    swapped = _np.concatenate([key[:, half:], key[:, :half]], 1)
    arrays["w_in"] = by_tile(_np.concatenate([w[:, :QL + KVL], w[:, MLA_PROJ:], key, swapped, key, swapped], 1))
    by_head = lambda w, n: tile(w.reshape(n, P, NH, -1).transpose(2, 1, 0, 3)).reshape(NH, P, -1)
    w = x["w_uq"][0].reshape(QL, NH, NOPE + ROPE)
    arrays["w_uq"] = by_head(_np.concatenate([w, w[:, :, NOPE + half:], w[:, :, NOPE:NOPE + half]], 2).reshape(QL, -1), QK)
    arrays["w_ukv"] = by_head(x["w_ukv"][0], KK)
    arrays["w_up"] = tile(by_tile(x["w_up"][0]).reshape(2, FK, P, D).transpose(1, 0, 2, 3)).reshape(F2K, P, D)
    arrays["w_down"] = x["w_down"][0].reshape(FK, P, D)
    nc = _bacc.Bacc("TRN2", target_bir_lowering=False, num_devices=1)
    build(nc, arrays)
    r = _run(nc, [{f"in_{n}": a for n, a in arrays.items()}], core_ids=[0]).results[0]
    T_ = lambda a: tile(a.T)
    y, lat, kr = T_(r["o_y"]), T_(r["o_lat"]), T_(r["o_krope"])
    sh = r["o_shift"].transpose(2, 1, 0).reshape(1 + NB, RWP)
    cv = r["o_conv"].transpose(2, 1, 0).reshape(1 + NB, 2, 2 * FF)
    st = lambda a, n: tile(a.reshape(n, NH, HD, HD).transpose(0, 1, 3, 2))[None]
    return (y[None, :TP], y[TP:].reshape(NB, TSEQ, D),
            lat[None, None, :TP], kr[None, None, :TP],
            T_(r["o_memk"]).reshape(1, 1, NM, MH, MD), r["o_memv"].reshape(1, 1, NM, MH, MD),
            st(r["o_rwkv_p"], 1), sh[None, :1], cv[None, :1],
            lat[TP:].reshape(1, NB, TSEQ, KVL), kr[TP:].reshape(1, NB, TSEQ, ROPE),
            st(r["o_rwkv_s"], NB), sh[None, 1:], cv[None, 1:])
```
